# Optimizing a Trainium2 kernel written in Bass

```python
import jax, jax.numpy as jnp
from jax import lax
import numpy as np

D_MODEL = 1024
BATCH = 1
SEQ = 256
DEPTH = 1

CHUNK = 64
N_MEM = 256
NORM_EPS = 1e-6
SSD_WIDTH = D_MODEL
SSD_HEAD_DIM = 64
SSD_HEADS = SSD_WIDTH // SSD_HEAD_DIM
SSD_GROUPS = 4
SSD_STATE = 128
SSD_CONV = 4
SSD_CONV_DIM = SSD_WIDTH + 2 * SSD_GROUPS * SSD_STATE
LRU_WIDTH = D_MODEL
LRU_BLOCKS = 16
LRU_BLOCK_W = LRU_WIDTH // LRU_BLOCKS
LRU_CONV = 4
RG_C = 8.0
MIX_WIDTH = SSD_WIDTH + LRU_WIDTH
IN_PROJ = SSD_WIDTH + SSD_CONV_DIM + SSD_HEADS + 2 * LRU_WIDTH
X_HEADS = 4
X_HEAD_DIM = D_MODEL // X_HEADS
N_EXPERTS = 32
TOP_K = 4
D_FF = D_MODEL
SWIGLU_LIMIT = 7.0
SWIGLU_ALPHA = 1.702
MOE_BLOCK = 128

kernel_name = 'hybrid_ssd_rglru_memxattn_moe'

def rmsnorm(x, g):
    xf = x.astype(jnp.float32)
    y = xf * lax.rsqrt(jnp.mean(xf * xf, axis=-1, keepdims=True) + NORM_EPS)
    return (y * g.astype(jnp.float32)).astype(x.dtype)

def gated_rmsnorm(y, z, g):
    b, s, w = y.shape
    u = (y * jax.nn.silu(z)).astype(jnp.float32).reshape(b, s, SSD_GROUPS, w // SSD_GROUPS)
    u = u * lax.rsqrt(jnp.mean(u * u, axis=-1, keepdims=True) + NORM_EPS)
    return (u.reshape(b, s, w) * g.astype(jnp.float32)).astype(y.dtype)

def causal_dwconv(x, w, bias):
    k, c = w.shape
    y = lax.conv_general_dilated(x, w[:, None, :], window_strides=(1,), padding=[(k - 1, 0)],
                                 dimension_numbers=('NWC', 'WIO', 'NWC'), feature_group_count=c)
    return y + bias

def ssd_chunked(xh, dt, a, bm, cm):
    b, s, h, p = xh.shape
    g, n = bm.shape[2], bm.shape[3]
    k = h // g
    c = s // CHUNK
    xdt = (xh * dt[..., None]).reshape(b, c, CHUNK, g, k, p)
    a_cs = jnp.cumsum((dt * a).reshape(b, c, CHUNK, g, k), axis=2)
    bc = bm.reshape(b, c, CHUNK, g, n)
    cc = cm.reshape(b, c, CHUNK, g, n)
    causal = jnp.tril(jnp.ones((CHUNK, CHUNK), dtype=bool))[None, None, :, :, None, None]
    seg = a_cs[:, :, :, None] - a_cs[:, :, None, :]
    decay = jnp.exp(jnp.where(causal, seg, -jnp.inf))
    cb = jnp.einsum('bclgn,bcsgn->bclsg', cc, bc)
    y_diag = jnp.einsum('bclsgk,bcsgkp->bclgkp', cb[..., None] * decay, xdt)
    decay_end = jnp.exp(a_cs[:, :, -1:] - a_cs)
    states = jnp.einsum('bclgn,bclgkp->bcgkpn', bc, decay_end[..., None] * xdt)
    chunk_decay = jnp.exp(a_cs[:, :, -1])

    def step(hs, inp):
        dec, st = inp
        return dec[..., None, None] * hs + st, hs

    _, prev = lax.scan(step, jnp.zeros_like(states[:, 0]),
                       (jnp.moveaxis(chunk_decay, 1, 0), jnp.moveaxis(states, 1, 0)))
    prev = jnp.moveaxis(prev, 0, 1)
    y_off = jnp.einsum('bclgn,bcgkpn->bclgkp', cc, prev) * jnp.exp(a_cs)[..., None]
    return (y_diag + y_off).reshape(b, s, h, p)

def rg_lru(xr, wa, ba, wx, bx, lam):
    b, s, w = xr.shape
    nb, bw, _ = wa.shape
    xb = xr.reshape(b, s, nb, bw)
    r = jax.nn.sigmoid(jnp.einsum('bsni,nij->bsnj', xb, wa).reshape(b, s, w) + ba)
    i = jax.nn.sigmoid(jnp.einsum('bsni,nij->bsnj', xb, wx).reshape(b, s, w) + bx)
    log_a = -RG_C * r * jax.nn.softplus(-lam)
    a = jnp.exp(log_a)
    u = xr * i * jnp.sqrt(-jnp.expm1(2.0 * log_a))

    def combine(left, right):
        a1, b1 = left
        a2, b2 = right
        return a1 * a2, a2 * b1 + b2

    _, hs = lax.associative_scan(combine, (a, u), axis=1)
    return hs

def hybrid_mixer(hn, w_in, ssd_conv_w, ssd_conv_b, ssd_dt_bias, ssd_a_log, ssd_d, ssd_norm,
                 lru_conv_w, lru_conv_b, lru_wa, lru_ba, lru_wx, lru_bx, lru_lambda, w_out):
    b, s, _ = hn.shape
    proj = hn @ w_in
    o1 = SSD_WIDTH
    o2 = o1 + SSD_CONV_DIM
    o3 = o2 + SSD_HEADS
    o4 = o3 + LRU_WIDTH
    z, xbc, dt_raw, xr, gr = proj[..., :o1], proj[..., o1:o2], proj[..., o2:o3], proj[..., o3:o4], proj[..., o4:]
    xbc = jax.nn.silu(causal_dwconv(xbc, ssd_conv_w, ssd_conv_b)).astype(jnp.float32)
    nbc = SSD_GROUPS * SSD_STATE
    xs = xbc[..., :SSD_WIDTH].reshape(b, s, SSD_HEADS, SSD_HEAD_DIM)
    bm = xbc[..., SSD_WIDTH:SSD_WIDTH + nbc].reshape(b, s, SSD_GROUPS, SSD_STATE)
    cm = xbc[..., SSD_WIDTH + nbc:].reshape(b, s, SSD_GROUPS, SSD_STATE)
    dt = jax.nn.softplus(dt_raw.astype(jnp.float32) + ssd_dt_bias.astype(jnp.float32))
    a = -jnp.exp(ssd_a_log.astype(jnp.float32))
    y = ssd_chunked(xs, dt, a, bm, cm) + xs * ssd_d.astype(jnp.float32)[:, None]
    y_ssd = gated_rmsnorm(y.reshape(b, s, SSD_WIDTH).astype(hn.dtype), z, ssd_norm)
    xr = causal_dwconv(xr, lru_conv_w, lru_conv_b).astype(jnp.float32)
    hl = rg_lru(xr, lru_wa.astype(jnp.float32), lru_ba.astype(jnp.float32), lru_wx.astype(jnp.float32),
                lru_bx.astype(jnp.float32), lru_lambda.astype(jnp.float32)).astype(hn.dtype)
    y_lru = hl * jax.nn.gelu(gr)
    return jnp.concatenate([y_ssd, y_lru], axis=-1) @ w_out

def memory_cross_attention(hn, mn, w_q, w_kv, w_o):
    b, s, d = hn.shape
    m = mn.shape[1]
    q = (hn @ w_q).reshape(b, s, X_HEADS, X_HEAD_DIM)
    kv = mn @ w_kv
    k = kv[..., :d].reshape(b, m, X_HEADS, X_HEAD_DIM)
    v = kv[..., d:].reshape(b, m, X_HEADS, X_HEAD_DIM)
    scores = jnp.einsum('bshd,bmhd->bhsm', q, k).astype(jnp.float32) * (X_HEAD_DIM ** -0.5)
    probs = jax.nn.softmax(scores, axis=-1).astype(v.dtype)
    o = jnp.einsum('bhsm,bmhd->bshd', probs, v).reshape(b, s, d)
    return o @ w_o

def moe_ffn(hn, w_router, b_router, w_gate_up, b_gate_up, w_down, b_down):
    b, s, d = hn.shape
    t = b * s
    xt = hn.reshape(t, d)
    logits = (xt @ w_router + b_router).astype(jnp.float32)
    top_val, top_idx = lax.top_k(logits, TOP_K)
    gate = jax.nn.softmax(top_val, axis=-1)
    n_pairs = t * TOP_K
    flat_e = top_idx.reshape(-1).astype(jnp.int32)
    flat_tok = jnp.arange(n_pairs, dtype=jnp.int32) // TOP_K
    flat_gate = gate.reshape(-1)
    order = jnp.argsort(flat_e)
    se, stok, sg = flat_e[order], flat_tok[order], flat_gate[order]
    counts = jnp.bincount(flat_e, length=N_EXPERTS).astype(jnp.int32)
    pcounts = (counts + MOE_BLOCK - 1) // MOE_BLOCK * MOE_BLOCK
    start = jnp.cumsum(counts) - counts
    pend = jnp.cumsum(pcounts)
    pstart = pend - pcounts
    dest = pstart[se] + (jnp.arange(n_pairs, dtype=jnp.int32) - start[se])
    n_blocks = (n_pairs + N_EXPERTS * (MOE_BLOCK - 1) + MOE_BLOCK - 1) // MOE_BLOCK
    rows = n_blocks * MOE_BLOCK
    row_tok = jnp.full((rows,), t, dtype=jnp.int32).at[dest].set(stok)
    row_gate = jnp.zeros((rows,), jnp.float32).at[dest].set(sg)
    block_e = jnp.searchsorted(pend, jnp.arange(n_blocks, dtype=jnp.int32) * MOE_BLOCK, side='right')
    block_e = jnp.minimum(block_e, N_EXPERTS - 1).astype(jnp.int32)
    xpad = jnp.concatenate([xt, jnp.zeros((1, d), xt.dtype)], axis=0)
    xrows = xpad[row_tok].reshape(n_blocks, MOE_BLOCK, d)

    def expert_block(args):
        xb, e = args
        gu = xb @ w_gate_up[e] + b_gate_up[e]
        g_ = jnp.minimum(gu[..., ::2], SWIGLU_LIMIT)
        u_ = jnp.clip(gu[..., 1::2], -SWIGLU_LIMIT, SWIGLU_LIMIT)
        act = (u_ + 1.0) * (g_ * jax.nn.sigmoid(SWIGLU_ALPHA * g_))
        return act @ w_down[e] + b_down[e]

    yrows = lax.map(expert_block, (xrows, block_e)).reshape(rows, d)
    yrows = yrows * row_gate[:, None].astype(yrows.dtype)
    out = jax.ops.segment_sum(yrows, row_tok, num_segments=t + 1)[:t]
    return out.reshape(b, s, d)

def setup_inputs(seed: int = 0) -> dict:
    key = jax.random.key(seed)
    ks = iter(jax.random.split(key, 40))
    L = DEPTH

    def nrm(shape, scale):
        return jax.random.normal(next(ks), shape, jnp.float32) * scale

    def gain(shape):
        return 1.0 + nrm(shape, 0.02)

    def unif(shape, lo, hi):
        return jax.random.uniform(next(ks), shape, jnp.float32, lo, hi)

    x = nrm((BATCH, SEQ, D_MODEL), 1.0)
    mem = nrm((BATCH, N_MEM, D_MODEL), 1.0)
    norm_mix = gain((L, D_MODEL))
    w_in = nrm((L, D_MODEL, IN_PROJ), D_MODEL ** -0.5)
    ssd_conv_w = nrm((L, SSD_CONV, SSD_CONV_DIM), SSD_CONV ** -0.5)
    ssd_conv_b = nrm((L, SSD_CONV_DIM), 0.01)
    dt0 = jnp.exp(unif((L, SSD_HEADS), float(np.log(1e-3)), float(np.log(1e-1))))
    ssd_dt_bias = dt0 + jnp.log(-jnp.expm1(-dt0))
    ssd_a_log = jnp.log(unif((L, SSD_HEADS), 1.0, 16.0))
    ssd_d = gain((L, SSD_HEADS))
    ssd_norm = gain((L, SSD_WIDTH))
    lru_conv_w = nrm((L, LRU_CONV, LRU_WIDTH), LRU_CONV ** -0.5)
    lru_conv_b = nrm((L, LRU_WIDTH), 0.01)
    lru_wa = nrm((L, LRU_BLOCKS, LRU_BLOCK_W, LRU_BLOCK_W), LRU_BLOCK_W ** -0.5)
    lru_ba = nrm((L, LRU_WIDTH), 0.01)
    lru_wx = nrm((L, LRU_BLOCKS, LRU_BLOCK_W, LRU_BLOCK_W), LRU_BLOCK_W ** -0.5)
    lru_bx = nrm((L, LRU_WIDTH), 0.01)
    a0 = unif((L, LRU_WIDTH), 0.9, 0.999) ** (1.0 / RG_C)
    lru_lambda = jnp.log(a0) - jnp.log1p(-a0)
    w_out = nrm((L, MIX_WIDTH, D_MODEL), MIX_WIDTH ** -0.5)
    norm_xattn = gain((L, D_MODEL))
    norm_mem = gain((L, D_MODEL))
    w_q = nrm((L, D_MODEL, D_MODEL), D_MODEL ** -0.5)
    w_kv = nrm((L, D_MODEL, 2 * D_MODEL), D_MODEL ** -0.5)
    w_o = nrm((L, D_MODEL, D_MODEL), D_MODEL ** -0.5)
    norm_moe = gain((L, D_MODEL))
    w_router = nrm((L, D_MODEL, N_EXPERTS), D_MODEL ** -0.5)
    b_router = nrm((L, N_EXPERTS), 0.01)
    w_gate_up = nrm((L, N_EXPERTS, D_MODEL, 2 * D_FF), D_MODEL ** -0.5)
    b_gate_up = nrm((L, N_EXPERTS, 2 * D_FF), 0.01)
    w_down = nrm((L, N_EXPERTS, D_FF, D_MODEL), D_FF ** -0.5)
    b_down = nrm((L, N_EXPERTS, D_MODEL), 0.01)
    norm_final = gain((D_MODEL,))
    return {'x': x, 'mem': mem, 'norm_mix': norm_mix, 'w_in': w_in,
            'ssd_conv_w': ssd_conv_w, 'ssd_conv_b': ssd_conv_b, 'ssd_dt_bias': ssd_dt_bias,
            'ssd_a_log': ssd_a_log, 'ssd_d': ssd_d, 'ssd_norm': ssd_norm,
            'lru_conv_w': lru_conv_w, 'lru_conv_b': lru_conv_b, 'lru_wa': lru_wa, 'lru_ba': lru_ba,
            'lru_wx': lru_wx, 'lru_bx': lru_bx, 'lru_lambda': lru_lambda, 'w_out': w_out,
            'norm_xattn': norm_xattn, 'norm_mem': norm_mem, 'w_q': w_q, 'w_kv': w_kv, 'w_o': w_o,
            'norm_moe': norm_moe, 'w_router': w_router, 'b_router': b_router,
            'w_gate_up': w_gate_up, 'b_gate_up': b_gate_up, 'w_down': w_down, 'b_down': b_down,
            'norm_final': norm_final}

def reference(x, mem, norm_mix, w_in, ssd_conv_w, ssd_conv_b, ssd_dt_bias, ssd_a_log, ssd_d, ssd_norm,
              lru_conv_w, lru_conv_b, lru_wa, lru_ba, lru_wx, lru_bx, lru_lambda, w_out,
              norm_xattn, norm_mem, w_q, w_kv, w_o, norm_moe, w_router, b_router,
              w_gate_up, b_gate_up, w_down, b_down, norm_final):
    h = x
    for l in range(DEPTH):
        h = h + hybrid_mixer(rmsnorm(h, norm_mix[l]), w_in[l], ssd_conv_w[l], ssd_conv_b[l], ssd_dt_bias[l],
                             ssd_a_log[l], ssd_d[l], ssd_norm[l], lru_conv_w[l], lru_conv_b[l], lru_wa[l],
                             lru_ba[l], lru_wx[l], lru_bx[l], lru_lambda[l], w_out[l])
        h = h + memory_cross_attention(rmsnorm(h, norm_xattn[l]), rmsnorm(mem, norm_mem[l]),
                                       w_q[l], w_kv[l], w_o[l])
        h = h + moe_ffn(rmsnorm(h, norm_moe[l]), w_router[l], b_router[l], w_gate_up[l], b_gate_up[l],
                        w_down[l], b_down[l])
    return rmsnorm(h, norm_final)


_drawn_inputs = setup_inputs


def setup_inputs(seed=0):
    import zlib

    import numpy as np

    out = dict(_drawn_inputs(seed))
    spreads = {}
    factors = {'ssd_d': 2.864,
     'lru_ba': 8.0,
     'lru_bx': 4.996,
     'norm_xattn': 7.906,
     'norm_mem': 3.736,
     'b_gate_up': 34.564,
     'b_down': 39.605,
     'norm_final': 7.669,
     'norm_moe': 4.295,
     'b_router': 8.0}
    for name, (base, spread) in spreads.items():
        noise = np.random.default_rng([zlib.crc32(name.encode()), seed]).standard_normal(out[name].shape)
        drawn = base * np.exp(spread * noise) if base else spread * noise
        out[name] = __import__('jax').numpy.asarray(drawn.astype(out[name].dtype))
    for name, factor in factors.items():
        out[name] = (out[name] * factor).astype(out[name].dtype)
    return out
```

```python
from contextlib import ExitStack

import concourse.bass as bass
from concourse import mybir

F32 = mybir.dt.float32
I32 = mybir.dt.int32
ALU = mybir.AluOpType
ACT = mybir.ActivationFunctionType
AX_X = mybir.AxisListType.X

P = 128
BANK = 512
D = 1024
S = 256
T = S // P
KT = D // P
EPS = 1e-6
HEADS = 16
HEAD_P = 64
GROUPS = 4
X_HEADS = 4
X_SCALE = float(D // X_HEADS) ** -0.5
RG_C = 8.0
EXPERTS = 32
TOP_K = 4
SLOTS = 64
SPILLS = 16
LIMIT = 7.0
ALPHA = 1.702

SLOT = 2048
RING = 12
CHUNK_COLS = SLOT // KT
DENSE_RING = 4
IN_CHUNKS, KV_CHUNKS, OUT_CHUNKS, Q_CHUNKS, O_CHUNKS = 20, 8, 8, 4, 4
KV0 = IN_CHUNKS
OUT0 = KV0 + KV_CHUNKS
Q0 = OUT0 + OUT_CHUNKS
O0 = Q0 + Q_CHUNKS
DENSE = O0 + O_CHUNKS
UP_CHUNKS, DOWN_CHUNKS = 8, 4

LCW, SCW, SCB, LCB, BA = 0, 32, 96, 112, 120
BX, LAM, SNORM, NMIX, NX, NMEM, NMOE = 128, 136, 144, 152, 160, 168, 176
PAR = 184

MISC_USES = ([("params", "dve")]
             + [(f"norm0_{n}", "dve" if n % 2 == 0 else "act") for n in range(4)]
             + [("dt", "dve"), ("cumsum", "dve")]
             + [(f"norm1_{n}", "dve" if n % 2 == 0 else "act") for n in range(4)]
             + [(f"lru{j}", "act") for j in range(8)]
             + [(f"xdt{n}", "dve") for n in range(4)]
             + [(f"cb{g}", "dve") for g in range(4)]
             + [("rows0", "dve")]
             + [x for q in range(8) for x in ([(f"rows{q + 1}", "dve")] if q < 7 else []) + [(f"y{q}", "dve")]]
             + [(f"power{n}", "dve") for n in range(2)]
             + [(f"norm2_{n}", "dve" if n % 2 == 0 else "act") for n in range(4)]
             + [(n, "act") for n in "score0 score1 probT0 score2 probT1 o0 score3 probT2 o1 probT3 o2 o3".split()]
             + [(f"norm3_{n}", "dve" if n % 2 == 0 else "act") for n in range(4)]
             + [(n, "dve") for n in "logits rank spill tables first".split()])
MISC_AT = {name: n for n, (name, _) in enumerate(MISC_USES)}


def hybrid_trunk_kernel(nc, x, mem, norm_mix, w_in, ssd_conv_w, ssd_conv_b, ssd_dt_bias, ssd_a_log, ssd_d,
                        ssd_norm, lru_conv_w, lru_conv_b, lru_wa, lru_ba, lru_wx, lru_bx, lru_lambda, w_out,
                        norm_xattn, norm_mem, w_q, w_kv, w_o, norm_moe, w_router, b_router,
                        w_gate_up, b_gate_up, w_down, b_down, norm_final, out):
    with ExitStack() as ctx:
        def sb(name, shape, dt=F32):
            return ctx.enter_context(nc.sbuf_tensor(name, shape, dt))

        def sem(name):
            return ctx.enter_context(nc.semaphore(name))

        ring = sb("ring", [P, RING, SLOT])
        h = sb("h", [P, T, D])
        xn = sb("xn", [P, T, D])
        xT = sb("xT", [P, KT, S])
        xbc = sb("xbc", [P, 16, S])
        zs = sb("zs", [P, KT, S])
        kT = sb("kT", [P, KT, S])
        v = sb("v", [P, T, D])
        gain_row = sb("gain_row", [P, D])
        scratch = sb("scratch", [P, 6400])
        ident = sb("ident", [P, P])
        mask3 = sb("mask3", [P, 3 * P])
        before = sb("before", [P, P])
        slot_id = sb("slot_id", [P, P])
        spill_id = sb("spill_id", [P, SPILLS])
        spill_base = sb("spill_base", [P, SPILLS])
        part_id = sb("part_id", [P, 1])
        rowsA = sb("rowsA", [P, P])
        rowsB = sb("rowsB", [PAR - P, P])
        par = sb("par", [P, PAR])
        w_dt = sb("w_dt", [P, KT, HEADS])
        heads_bc = sb("heads_bc", [P, 3, HEADS])
        d_col = sb("d_col", [P, KT])
        sp = sb("sp", [P, 8, 40])
        dt = sb("dt", [P, T, HEADS])
        dtA = sb("dtA", [P, T, HEADS])
        expA = sb("expA", [P, HEADS])
        lru_rate = sb("lru_rate", [P, KT])
        seg_bias = sb("seg_bias", [P, 3, HEADS])
        stats = sb("stats", [P, 5, 4, T])
        soft = sb("soft", [P, X_HEADS, 4, T])
        lg = sb("lg", [P, T, EXPERTS])
        top8 = sb("top8", [P, T, 8])
        top_neg = sb("top_neg", [P, T])
        rest = sb("rest", [P, T, EXPERTS])
        sel = sb("sel", [P, T, EXPERTS])
        gsum = sb("gsum", [P, 2, T])
        rank_tab = sb("rank_tab", [P, T, EXPERTS + SPILLS + 1])
        gate_tab = sb("gate_tab", [P, T, EXPERTS + SPILLS + 1])
        spill_cols = sb("spill_cols", [EXPERTS, 8])
        one_hot = sb("one_hot", [EXPERTS, 2, SPILLS])
        rgT = sb("rgT", [EXPERTS, 2, S])
        spill_int = sb("spill_int", [1, SPILLS + 1], I32)

        tri = mask3[:, 0:P]
        ones = mask3[:, P:2 * P]

        def slot_view(n):
            return ring[:, n, :].rearrange("p (k s) -> p k s", k=KT)

        mnT, rb, ib, ab, gg, xr = (slot_view(n) for n in range(4, 10))
        xdt = ring[:, 10, :].rearrange("p (t c) -> p t c", t=T)
        mem_sb = ring[:, 11, :].rearrange("p (t c) -> p t c", t=T)
        junk = zs[:, :, :].rearrange("p k s -> p (k s)")
        xsT, bcT = xbc[:, 0:8, :], xbc[:, 8:16, :]
        group_scale = xbc[:, 8:12, :]
        qT, oT = xbc[:, 0:8, :], xbc[:, 8:16, :]
        bdown = junk[0:EXPERTS, 0:D]
        wr = junk[:, D:D + KT * EXPERTS].rearrange("p (k e) -> p k e", k=KT)
        br = junk[:, D + KT * EXPERTS:D + (KT + 1) * EXPERTS]
        bd = scratch[:, 0:2048].rearrange("p (w j c) -> p w j c", w=2, j=KT)
        xpad = scratch[:, 2048:2048 + 4 * (S + 3)].rearrange("p (b j s) -> p b j s", b=2, j=2)
        cbm = scratch[:, 3088:3088 + 1536].rearrange("p (g l) -> p g l", g=GROUPS)
        mt = scratch[:, 4624:4624 + 1536].rearrange("p (b h l) -> p b h l", b=2, h=2)
        prob = scratch[:, 0:2048].rearrange("p (b t m) -> p b t m", b=4, t=T)
        probT = scratch[:, 2048:4096].rearrange("p (b t m) -> p b t m", b=4, t=T)
        bias_row = scratch[0:1, 0:2 * D]
        pick = scratch[:, 2048:2176].rearrange("p (t c) -> p t c", t=T)
        pick_gate = scratch[:, 2176:2432].rearrange("p (t c) -> p t c", t=T)
        put = scratch[:, 2432:2688]
        xsel = scratch[:, 2688:3200].rearrange("p (k c) -> p k c", k=KT)
        g_sb, sig, u_sb, act_sb, y_sb = (scratch[:, 3200 + 512 * n:3712 + 512 * n] for n in range(5))
        actT = scratch[:, 5760:6272].rearrange("p (j c) -> p j c", j=4)

        wide = ctx.enter_context(nc.psum_tensor("wide", [P, 4, BANK], F32))
        misc = ctx.enter_context(nc.psum_tensor("misc", [P, 4, BANK], F32))
        gu_ps = misc[:, 0:2, :].rearrange("p b n -> p (b n)")
        turn_ps, y_ps = misc[:, 2, :], misc[:, 3, :]

        def misc_bank(name):
            return misc[:, MISC_AT[name] % 4, :]

        consts_made = sem("consts_made")
        x_landed, mem_landed = sem("x_landed"), sem("mem_landed")
        params_landed, heads_landed, gates_landed = sem("params_landed"), sem("heads_landed"), sem("gates_landed")
        router_landed = sem("router_landed")
        ring_landed = [sem(f"ring_landed{n}") for n in range(RING)]
        bias_landed, bias_used = sem("bias_landed"), sem("bias_used")
        chunk_used = sem("chunk_used")
        misc_filled = sem("misc_filled")
        misc_freed = {"dve": sem("misc_freed_dve"), "act": sem("misc_freed_act")}
        squared = {"dve": sem("squared_dve"), "act": sem("squared_act")}
        mean_made, root_made, rstd_made = sem("mean_made"), sem("root_made"), sem("rstd_made")
        normed = {"dve": sem("normed_dve"), "act": sem("normed_act")}
        dve_step = sem("dve_step")
        sp_step, sp_act = sem("sp_step"), sem("sp_act")
        dtA_made, seg_made, rate_made = sem("dtA_made"), sem("seg_made"), sem("rate_made")
        padded, pad_filled, tap_done, convolved = sem("padded"), sem("pad_filled"), sem("tap_done"), sem("convolved")
        wide_freed = sem("wide_freed")
        silu_made = sem("silu_made")
        decay_made, lru_poly, lru_root, lru_out = (sem(n) for n in ("decay_made", "lru_poly", "lru_root", "lru_out"))
        seg_exp, mt_made, power_made, ssd_root, ssd_out = (
            sem(n) for n in ("seg_exp", "mt_made", "power_made", "ssd_root", "ssd_out"))
        ssd_squares = sem("ssd_squares")
        h_added = sem("h_added")
        score_max, prob_exp, prob_made = sem("score_max"), sem("prob_exp"), sem("prob_made")
        logits_made, gate_exp, sel_made, gates_made, spill_made, hot_made, rgT_made, tables_made = (
            sem(n) for n in ("logits_made", "gate_exp", "sel_made", "gates_made", "spill_made", "hot_made",
                             "rgT_made", "tables_made"))
        pick_made, pick_gate_made, picked, xsel_made = (
            sem(n) for n in ("pick_made", "pick_gate_made", "picked", "xsel_made"))
        g_made, sig_made, gu_freed, act_made = (sem(n) for n in ("g_made", "sig_made", "gu_freed", "act_made"))
        put_turned, put_made, act_turned, actT_made, y_made = (
            sem(n) for n in ("put_turned", "put_made", "act_turned", "actT_made", "y_made"))
        gated = sem("gated")
        combined = sem("combined")
        out_made, stored = sem("out_made"), sem("stored")

        def wait_misc_filled(eng, name):
            eng.wait_ge(misc_filled, MISC_AT[name] + 1)

        def wait_misc_free(pe, name):
            n = MISC_AT[name] - 4
            if n >= 0:
                who = MISC_USES[n][1]
                pe.wait_ge(misc_freed[who], sum(e == who for _, e in MISC_USES[:n + 1]))

        def dense_landed(pe, c):
            pe.wait_ge(ring_landed[c % DENSE_RING], 16 * (c // DENSE_RING + 1))

        def item_landed(pe, i, c):
            dense = DENSE // DENSE_RING if c < DENSE_RING else 0
            pe.wait_ge(ring_landed[c], (i + (dense + 1)) * 16)

        def used(eng, i, c):
            eng.wait_ge(chunk_used, i * RING + (DENSE + c + 1))

        w_in_v, w_kv_v, w_q_v, w_o_v = (w[0].rearrange("(k p) n -> p k n", p=P) for w in (w_in, w_kv, w_q, w_o))
        w_out_v = w_out[0].rearrange("(h k p) n -> h p k n", h=2, p=P)
        up_v = w_gate_up[0].rearrange("e (k p) n -> e k p n", p=P)
        down_v = w_down[0].rearrange("e (c k p) n -> e c p k n", k=2, p=P)

        block = ctx.enter_context(nc.Block())

        @block.sync
        def _(sp_):
            def fill(slot, src):
                sp_.dma_start(slot_view(slot), src).then_inc(ring_landed[slot], 16)

            XR = 3 * D + HEADS
            for c in range(DENSE_RING):
                fill(c, w_in_v[:, :, XR + c * CHUNK_COLS:XR + (c + 1) * CHUNK_COLS])
            for c in range(DENSE_RING):
                sp_.wait_ge(chunk_used, c + 1)
                fill(c, w_in_v[:, :, XR + D + c * CHUNK_COLS:XR + D + (c + 1) * CHUNK_COLS])
            with sp_.Fori(0, 3) as g:
                for c in range(DENSE_RING):
                    sp_.wait_ge(chunk_used, g * DENSE_RING + (DENSE_RING + c + 1))
                    fill(c, w_in_v[:, :, bass.ds(g * D + c * CHUNK_COLS, CHUNK_COLS)])
            rest_of_dense = ([w_kv_v[:, :, n * CHUNK_COLS:(n + 1) * CHUNK_COLS] for n in range(KV_CHUNKS)]
                             + [w_out_v[half, :, :, n * CHUNK_COLS:(n + 1) * CHUNK_COLS]
                                for half in (1, 0) for n in range(4)]
                             + [w_q_v[:, :, n * CHUNK_COLS:(n + 1) * CHUNK_COLS] for n in range(Q_CHUNKS)]
                             + [w_o_v[:, :, n * CHUNK_COLS:(n + 1) * CHUNK_COLS] for n in range(O_CHUNKS)])
            for c, src in enumerate(rest_of_dense, KV0):
                sp_.wait_ge(chunk_used, c - (DENSE_RING - 1))
                fill(c % DENSE_RING, src)

            def item_chunk(e, c):
                if c < UP_CHUNKS:
                    dst, src = ring[:, c, :], up_v[e, c]
                else:
                    dst, src = ring[:, c, :].rearrange("p (k n) -> p k n", k=2), down_v[e, c - UP_CHUNKS]
                sp_.dma_start(dst, src).then_inc(ring_landed[c], 16)

            def bias_chunk(e):
                sp_.dma_start(bias_row, b_gate_up[0, e:e + 1, :] if isinstance(e, int)
                              else b_gate_up[0, bass.ds(e, 1), :]).then_inc(bias_landed, 16)

            sp_.wait_ge(chunk_used, OUT0 + 4)
            for c in range(DENSE_RING, RING):
                item_chunk(0, c)
            for c in range(DENSE_RING):
                sp_.wait_ge(chunk_used, DENSE - DENSE_RING + 1 + c)
                item_chunk(0, c)
            sp_.wait_ge(misc_filled, MISC_AT["o3"] + 1)
            bias_chunk(0)

            def refill(i, e):
                for c in range(RING):
                    used(sp_, i - 1, c)
                    if c < UP_CHUNKS:
                        src = up_v[bass.ds(e, 1), c].rearrange("e p n -> p (e n)")
                        dst = ring[:, c, :]
                    else:
                        src = down_v[bass.ds(e, 1), c - UP_CHUNKS].rearrange("e p k n -> p (e k) n")
                        dst = ring[:, c, :].rearrange("p (k n) -> p k n", k=2)
                    sp_.dma_start(dst, src).then_inc(ring_landed[c], 16)
                    if c == 0:
                        sp_.wait_ge(bias_used, i)
                        bias_chunk(e)

            with sp_.Fori(1, EXPERTS) as i:
                refill(i, i)
            sp_.wait_ge(tables_made, 1)
            spills = sp_.value_load(spill_int[0:1, SPILLS:SPILLS + 1], min_val=0, max_val=SPILLS)
            with sp_.If(spills > 0):
                with sp_.Fori(0, spills) as j:
                    e = sp_.value_load(spill_int[0:1, bass.ds(j, 1)], min_val=0, max_val=EXPERTS - 1)
                    refill(j + EXPERTS, e)
            out_v = out[0].rearrange("(t p) d -> p t d", p=P)
            for t in range(T):
                sp_.wait_ge(out_made, t + 1)
                sp_.dma_start(out_v[:, t, :], xn[:, t, :]).then_inc(stored, 16)
            sp_.wait_ge(stored, 16 * T)

        @block.gpsimd
        def _(pool):
            def rows(dst, at, src):
                n = src.shape[0]
                pool.dma_start(dst[at:at + n, :], src).then_inc(params_landed, 16)

            rows(rowsA, LCW, lru_conv_w[0].rearrange("k (j p) -> (k j) p", p=P))
            rows(rowsA, SCW, ssd_conv_w[0].rearrange("k (j p) -> (k j) p", p=P))
            for at, w in ((SCB, ssd_conv_b), (LCB, lru_conv_b), (BA, lru_ba)):
                rows(rowsA, at, w[0].rearrange("(j p) -> j p", p=P))
            for at, w in ((BX, lru_bx), (LAM, lru_lambda), (SNORM, ssd_norm), (NMIX, norm_mix), (NX, norm_xattn),
                          (NMEM, norm_mem), (NMOE, norm_moe)):
                rows(rowsB, at - P, w[0].rearrange("(j p) -> j p", p=P))
            pool.memset(ident[:, :], 0.0).then_inc(consts_made, 1)
            pool.memset(mask3[:, :], 1.0).then_inc(consts_made, 1)
            pool.memset(before[:, :], 1.0).then_inc(consts_made, 1)
            pool.memset(bd, 0.0).then_inc(consts_made, 1)
            pool.wait_ge(consts_made, 4)
            pool.affine_select(out=ident[:, :], in_=ident[:, :], compare_op=ALU.not_equal, fill=1.0, base=0,
                               pattern=[[-1, P]], channel_multiplier=1).then_inc(consts_made, 1)
            for n in (0, 2):
                m = mask3[:, n * P:(n + 1) * P]
                pool.affine_select(out=m, in_=m, compare_op=ALU.is_ge, fill=0.0, base=0, pattern=[[1, P]],
                                   channel_multiplier=-1).then_inc(consts_made, 1)
            pool.affine_select(out=before[:, :], in_=before[:, :], compare_op=ALU.is_ge, fill=0.0, base=-1,
                               pattern=[[1, P]], channel_multiplier=-1).then_inc(consts_made, 1)
            pool.iota(slot_id[:, :], pattern=[[0, 2], [1, SLOTS]], base=0, channel_multiplier=0,
                      allow_small_or_imprecise_dtypes=True).then_inc(consts_made, 1)
            pool.iota(spill_id[:, :], pattern=[[1, SPILLS]], base=0, channel_multiplier=0,
                      allow_small_or_imprecise_dtypes=True).then_inc(consts_made, 1)
            pool.iota(spill_base[:, :], pattern=[[SLOTS, SPILLS]], base=SLOTS, channel_multiplier=0,
                      allow_small_or_imprecise_dtypes=True).then_inc(consts_made, 1)
            pool.iota(part_id[:, :], pattern=[[0, 1]], base=0, channel_multiplier=1,
                      allow_small_or_imprecise_dtypes=True).then_inc(consts_made, 1)
            pool.memset(xpad[:, :, :, 0:3], 0.0).then_inc(padded, 1)
            for w, src in enumerate((lru_wa, lru_wx)):
                blocks = src[0].rearrange("(j b) i o -> b i j o", b=2)
                for b in range(2):
                    pool.dma_start(bd[64 * b:64 * b + 64, w, :, 64 * b:64 * b + 64], blocks[b]).then_inc(gates_landed, 16)
            pool.dma_start(gain_row[:, :], norm_final.rearrange("(a d) -> a d", a=1).broadcast_to([P, D]))\
                .then_inc(router_landed, 16)
            pool.wait_ge(chunk_used, OUT0 + OUT_CHUNKS)
            pool.dma_start(bdown, b_down[0]).then_inc(router_landed, 16)
            pool.dma_start(wr, w_router[0].rearrange("(k p) e -> p k e", p=P)).then_inc(router_landed, 16)
            pool.dma_start(br, b_router[0:1, :].broadcast_to([P, EXPERTS])).then_inc(router_landed, 16)

        CONSTS = 12

        def norm_stage(n):
            if n == 1:
                return mem_sb, junk.rearrange("p (t d) -> p t d", t=T), mem_sb
            return h, xn, xn

        NORM_GAIN = {0: NMIX, 1: NMEM, 2: NX, 3: NMOE}

        def norm_T(n):
            return mnT if n == 1 else xT

        @block.scalar
        def _(act):
            h_v = x[0].rearrange("(t p) d -> p t d", p=P)
            act.dma_start(h[:, :, :], h_v).then_inc(x_landed, 16)
            act.dma_start(w_dt[:, :, :], w_in_v[:, :, 3 * D:3 * D + HEADS]).then_inc(heads_landed, 16)
            for n, w in enumerate((ssd_dt_bias, ssd_a_log, ssd_d)):
                act.dma_start(heads_bc[:, n, :], w[0:1, :].broadcast_to([P, HEADS])).then_inc(heads_landed, 16)
            act.dma_start(mem_sb, mem[0].rearrange("(t p) d -> p t d", p=P)).then_inc(mem_landed, 16)

            def norm(n):
                src, sq, dst = norm_stage(n)
                if n >= 2:
                    act.wait_ge(h_added, T * (n - 1) - 1)
                act.activation(sq[:, 0, :], src[:, 0, :], ACT.Square, accum_out=stats[:, n, 0, 0:1])\
                    .then_inc(squared["act"], 1)
                act.wait_ge(mean_made, n + 1)
                act.activation(stats[:, n, 2, :], stats[:, n, 1, :], ACT.Sqrt).then_inc(root_made, 1)
                act.wait_ge(rstd_made, n + 1)
                if n < 4:
                    act.activation(dst[:, 0, :], src[:, 0, :], ACT.Copy, scale=stats[:, n, 3, 0:1])\
                        .then_inc(normed["act"], 1)

            def norm_turned(n):
                for b in (1, 3):
                    wait_misc_filled(act, f"norm{n}_{b}")
                    bank = misc_bank(f"norm{n}_{b}")
                    for j in range(2):
                        k = 2 * b + j
                        last = act.activation(norm_T(n)[:, k, :], bank[:, j * S:(j + 1) * S], ACT.Copy,
                                              scale=par[:, NORM_GAIN[n] + k:NORM_GAIN[n] + k + 1])
                    last.then_inc(misc_freed["act"], 1)

            def bank_of(c):
                return wide[:, c % DENSE_RING, :].rearrange("p (j s) -> p j s", j=2)

            act.wait_ge(x_landed, 16)
            norm(0)
            act.wait_ge(dve_step, 1)
            norm_turned(0)
            act.wait_ge(sp_step, 1)
            act.activation(sp[:, 2, :], sp[:, 1, :], ACT.Exp).then_inc(sp_act, 1)
            act.wait_ge(heads_landed, 64)
            act.activation(expA[:, :], heads_bc[:, 1, :], ACT.Exp).then_inc(sp_act, 1)
            act.wait_ge(sp_step, 2)
            act.activation(sp[:, 4, :], sp[:, 3, :], ACT.Ln).then_inc(sp_act, 1)
            act.wait_ge(mem_landed, 16)
            norm(1)

            def pad_copy(c, n):
                act.wait_ge(chunk_used, c + 1)
                if n >= 2:
                    act.wait_ge(convolved, n - 1)
                act.activation(xpad[:, n % 2, :, 3:3 + S], bank_of(c), ACT.Copy).then_inc(pad_filled, 1)

            act.wait_ge(padded, 1)
            for c in range(4):
                pad_copy(c, c)
            for c in range(4, 8):
                act.wait_ge(chunk_used, c + 1)
                j = 2 * (c - 4)
                act.activation(gg[:, j:j + 2, :], bank_of(c), ACT.Gelu_apprx_tanh).then_inc(wide_freed, 1)
            for c in range(8, 12):
                act.wait_ge(chunk_used, c + 1)
                j = 2 * (c - 8)
                act.activation(zs[:, j:j + 2, :], bank_of(c), ACT.Silu).then_inc(wide_freed, 1)

            def silu(n):
                act.wait_ge(convolved, 4 + n + 1)
                act.activation(xbc[:, 2 * n:2 * n + 2, :], xbc[:, 2 * n:2 * n + 2, :], ACT.Silu).then_inc(silu_made, 1)

            for c in range(12, 20):
                pad_copy(c, c - 8)
                if c > 12:
                    silu(c - 13)
            silu(7)
            norm_turned(1)
            for j in range(KT):
                wait_misc_filled(act, f"lru{j}")
                bank = misc_bank(f"lru{j}")
                act.activation(rb[:, j, :], bank[:, 0:S], ACT.Sigmoid, bias=par[:, BA + j:BA + j + 1])
                act.activation(ib[:, j, :], bank[:, S:2 * S], ACT.Sigmoid, bias=par[:, BX + j:BX + j + 1])\
                    .then_inc(misc_freed["act"], 1)
            act.wait_ge(rate_made, 1)
            act.wait_ge(misc_freed["act"], 4 + KT)
            for j in range(KT):
                act.activation(ab[:, j, :], rb[:, j, :], ACT.Exp, scale=lru_rate[:, j:j + 1])
                last = act.activation(rb[:, j, :], rb[:, j, :], ACT.Tanh, scale=lru_rate[:, j:j + 1])
            last.then_inc(decay_made, 1)
            act.wait_ge(seg_made, 1 + 1)
            act.activation(mt[:, 0, :, :], mt[:, 0, :, :], ACT.Exp).then_inc(seg_exp, 1)
            act.wait_ge(lru_poly, 1)
            act.activation(rb, rb, ACT.Sqrt, scale=-1.0).then_inc(lru_root, 1)

            for q in range(KV_CHUNKS):
                act.wait_ge(chunk_used, KV0 + q + 1)
                dst = kT[:, 2 * q:2 * q + 2, :] if q < 4 else v[:, :, (q - 4) * CHUNK_COLS:(q - 3) * CHUNK_COLS]
                act.activation(dst, bank_of(KV0 + q), ACT.Copy).then_inc(wide_freed, 1)
                if q + 1 < 8:
                    act.wait_ge(seg_made, q + 3)
                    act.activation(mt[:, (q + 1) % 2, :, :], mt[:, (q + 1) % 2, :, :], ACT.Exp).then_inc(seg_exp, 1)
            act.wait_ge(power_made, 1)
            act.activation(group_scale, group_scale, ACT.Sqrt).then_inc(ssd_root, 1)

            norm(2)
            norm_turned(2)

            def q_copy(c):
                act.wait_ge(chunk_used, Q0 + c + 1)
                act.activation(qT[:, 2 * c:2 * c + 2, :], bank_of(Q0 + c), ACT.Copy).then_inc(wide_freed, 1)

            def prob_exps(hd):
                act.wait_ge(score_max, hd + 1)
                bank = misc_bank(f"score{hd}")
                for t in range(T):
                    last = act.activation(prob[:, hd, t, :], bank[:, t * S:(t + 1) * S], ACT.Exp,
                                          bias=soft[:, hd, 1, t:t + 1], scale=X_SCALE,
                                          accum_out=soft[:, hd, 2, t:t + 1])
                last.then_inc(misc_freed["act"], 1)

            def copy_out(name, dst):
                wait_misc_filled(act, name)
                act.activation(dst, misc_bank(name).rearrange("p (j s) -> p j s", j=2), ACT.Copy)\
                    .then_inc(misc_freed["act"], 1)

            q_copy(0)
            q_copy(1)
            prob_exps(0)
            q_copy(2)
            prob_exps(1)
            copy_out("probT0", probT[:, 0, :, :])
            q_copy(3)
            prob_exps(2)
            copy_out("probT1", probT[:, 1, :, :])
            copy_out("o0", oT[:, 0:2, :])
            prob_exps(3)
            copy_out("probT2", probT[:, 2, :, :])
            copy_out("o1", oT[:, 2:4, :])
            copy_out("probT3", probT[:, 3, :, :])
            copy_out("o2", oT[:, 4:6, :])
            copy_out("o3", oT[:, 6:8, :])

            norm(3)
            norm_turned(3)
            for t in range(T):
                act.wait_ge(logits_made, t + 1)
                act.activation(rest[:, t, :], lg[:, t, :], ACT.Exp, bias=top_neg[:, t:t + 1]).then_inc(gate_exp, 1)

            act.wait_ge(misc_filled, MISC_AT["o3"] + 1)
            act.activation(put, mask3[:, 0:S], ACT.Copy, scale=0.0).then_inc(put_made, 1)
            act.activation(y_sb[:, 0:S], mask3[:, 0:S], ACT.Copy, scale=0.0)
            act.activation(y_sb[:, S:2 * S], mask3[:, 0:S], ACT.Copy, scale=0.0).then_inc(y_made, 1)

            def expert(i):
                act.wait_ge(g_made, i + 1)
                act.activation(sig, g_sb, ACT.Sigmoid, scale=ALPHA).then_inc(sig_made, 1)
                act.wait_ge(put_turned, i + 1)
                act.activation(put, y_ps[:, 0:S], ACT.Copy).then_inc(put_made, 1)
                act.wait_ge(act_turned, i + 1)
                act.activation(actT.rearrange("p j c -> p (j c)"), turn_ps, ACT.Copy).then_inc(actT_made, 1)
                used(act, i, RING - 1)
                act.activation(y_sb, y_ps, ACT.Copy).then_inc(y_made, 1)

            with act.Fori(0, EXPERTS) as i:
                expert(i)
            act.wait_ge(tables_made, 1)
            spills = act.value_load(spill_int[0:1, SPILLS:SPILLS + 1], min_val=0, max_val=SPILLS)
            with act.If(spills > 0):
                with act.Fori(0, spills) as j:
                    expert(j + EXPERTS)
            norm(4)

        @block.tensor
        def _(pe):
            def norm_turn(n):
                dst = norm_stage(n)[2]
                pe.wait_ge(normed["act"], n + 1)
                pe.wait_ge(normed["dve"], n + 1)
                for b in range(4):
                    name = f"norm{n}_{b}"
                    wait_misc_free(pe, name)
                    for j in range(2):
                        k = 2 * b + j
                        for t in range(T):
                            last = pe.transpose(misc_bank(name)[:, j * S + t * P:j * S + (t + 1) * P],
                                                dst[:, t, k * P:(k + 1) * P], ident[:, :])
                    last.then_inc(misc_filled, 1)

            def project_T(slot, actT_):
                for j in range(2):
                    for k in range(KT):
                        last = pe.matmul(wide[:, slot, j * S:(j + 1) * S], slot_view(slot)[:, k, j * P:(j + 1) * P],
                                         actT_[:, k, :], start=(k == 0), stop=(k == KT - 1))
                last.then_inc(chunk_used, 1)

            def project_rows(c, src, n, first, last_pass):
                slot = c % DENSE_RING
                for t in range(T):
                    at = n % 2 * CHUNK_COLS
                    for k in range(KT):
                        last = pe.matmul(wide[:, 2 * t + n // 2, at:at + CHUNK_COLS], src[:, k, t * P:(t + 1) * P],
                                         slot_view(slot)[:, k, :], start=(first and n % 2 == 0 and k == 0),
                                         stop=(last_pass and k == KT - 1), skip_group_check=True)
                last.then_inc(chunk_used, 1)

            pe.wait_ge(consts_made, CONSTS)
            pe.wait_ge(params_landed, 16 * 12)
            bank = misc_bank("params")
            pe.transpose(bank[:, 0:P], rowsA[:, :], ident[:, :])
            pe.transpose(bank[:, P:PAR], rowsB[:, :], ident[0:PAR - P, 0:PAR - P]).then_inc(misc_filled, 1)
            norm_turn(0)
            wait_misc_free(pe, "dt")
            pe.wait_ge(heads_landed, 64)
            pe.wait_ge(misc_freed["dve"], 3)
            pe.wait_ge(misc_freed["act"], 2)
            for t in range(T):
                for k in range(KT):
                    last = pe.matmul(misc_bank("dt")[:, t * HEADS:(t + 1) * HEADS], xT[:, k, t * P:(t + 1) * P],
                                     w_dt[:, k, :], start=(k == 0), stop=(k == KT - 1))
            last.then_inc(misc_filled, 1)

            def in_chunk(g, s):
                pe.wait_ge(ring_landed[s], (g + 1) * 16)
                project_T(s, xT)

            for s in range(DENSE_RING):
                in_chunk(0, s)
            for s in range(DENSE_RING):
                pe.wait_ge(pad_filled, s + 1)
                in_chunk(1, s)
            for s in range(DENSE_RING):
                pe.wait_ge(wide_freed, s + 1)
                in_chunk(2, s)
            for s in range(DENSE_RING):
                pe.wait_ge(wide_freed, 4 + s + 1)
                in_chunk(3, s)
            for s in range(DENSE_RING):
                pe.wait_ge(pad_filled, 4 + s + 1)
                in_chunk(4, s)

            wait_misc_free(pe, "cumsum")
            pe.wait_ge(dtA_made, 1)
            bank = misc_bank("cumsum")
            for t in range(T):
                pe.matmul(bank[:, t * HEADS:(t + 1) * HEADS], tri, dtA[:, t, :], start=True, stop=True)
            pe.matmul(bank[:, 2 * HEADS:3 * HEADS], ones, dtA[:, 0, :], start=True, stop=True).then_inc(misc_filled, 1)
            norm_turn(1)
            pe.wait_ge(gates_landed, 64)
            pe.wait_ge(convolved, 4)
            for j in range(KT):
                wait_misc_free(pe, f"lru{j}")
                bank = misc_bank(f"lru{j}")
                for w in range(2):
                    last = pe.matmul(bank[:, w * S:(w + 1) * S], bd[:, w, j, :], xr[:, j, :], start=True, stop=True)
                last.then_inc(misc_filled, 1)
            pe.wait_ge(silu_made, 4)
            for t in range(T):
                for half in range(2):
                    name = f"xdt{2 * t + half}"
                    wait_misc_free(pe, name)
                    for j in range(4):
                        last = pe.transpose(misc_bank(name)[:, j * P:(j + 1) * P],
                                            xsT[:, 4 * half + j, t * P:(t + 1) * P], ident[:, :])
                    last.then_inc(misc_filled, 1)
            pe.wait_ge(silu_made, 8)
            for g in range(GROUPS):
                wait_misc_free(pe, f"cb{g}")
                bank = misc_bank(f"cb{g}")
                pe.matmul(bank[:, 0:S], bcT[:, g, 0:P], bcT[:, GROUPS + g, :], start=True, stop=True)
                pe.matmul(bank[:, S:S + P], bcT[:, g, P:S], bcT[:, GROUPS + g, P:S], start=True, stop=True)\
                    .then_inc(misc_filled, 1)

            def decay_rows(q):
                name = f"rows{q}"
                wait_misc_free(pe, name)
                for hh in range(2):
                    for t in range(T):
                        at = hh * S + t * P
                        last = pe.matmul(misc_bank(name)[:, at:at + P],
                                         dtA[:, t, 2 * q + hh:2 * q + hh + 1].broadcast_to([P, P]), tri,
                                         start=True, stop=True)
                last.then_inc(misc_filled, 1)

            def ssd_heads(q):
                name = f"y{q}"
                wait_misc_free(pe, name)
                pe.wait_ge(mt_made, q + 1)
                bank = misc_bank(name)
                for t in range(T):
                    for hh in range(2):
                        at = (2 * q + hh) * HEAD_P
                        m = mt[:, q % 2, hh, 0:S] if t == 0 else mt[:, q % 2, hh, S:S + P]
                        last = pe.matmul(bank[HEAD_P * hh:HEAD_P * (hh + 1), t * P:S], xdt[:, t, at:at + HEAD_P], m,
                                         start=(t == 0), stop=(t == 1), skip_group_check=True)
                last.then_inc(misc_filled, 1)

            decay_rows(0)
            for q in range(KV_CHUNKS):
                c = KV0 + q
                dense_landed(pe, c)
                if q < 4:
                    pe.wait_ge(pad_filled, 8 + q + 1)
                    project_T(c % DENSE_RING, mnT)
                else:
                    pe.wait_ge(wide_freed, 8 + q - 3)
                    for t in range(T):
                        for k in range(KT):
                            last = pe.matmul(wide[:, c % DENSE_RING, t * S:(t + 1) * S], mnT[:, k, t * P:(t + 1) * P],
                                             slot_view(c % DENSE_RING)[:, k, :], start=(k == 0), stop=(k == KT - 1))
                    last.then_inc(chunk_used, 1)
                if q < 7:
                    decay_rows(q + 1)
                ssd_heads(q)
            for n in range(2):
                name = f"power{n}"
                wait_misc_free(pe, name)
                pe.wait_ge(ssd_squares, 4 * (n + 1))
                for g in range(2):
                    for j in range(2):
                        last = pe.matmul(misc_bank(name)[:, g * S:(g + 1) * S], ones, xsT[:, 4 * n + 2 * g + j, :],
                                         start=(j == 0), stop=(j == 1))
                last.then_inc(misc_filled, 1)
            pe.wait_ge(wide_freed, 16)
            pe.wait_ge(lru_out, 1)
            for n in range(4):
                dense_landed(pe, OUT0 + n)
                project_rows(OUT0 + n, gg, n, True, False)
            pe.wait_ge(ssd_out, 1)
            for n in range(4):
                dense_landed(pe, OUT0 + 4 + n)
                project_rows(OUT0 + 4 + n, zs, n, False, True)
            norm_turn(2)

            def q_chunk(c):
                dense_landed(pe, Q0 + c)
                project_T(c, xT)

            def score(hd):
                name = f"score{hd}"
                wait_misc_free(pe, name)
                pe.wait_ge(wide_freed, 16 + hd + 1)
                for t in range(T):
                    for k in range(2):
                        last = pe.matmul(misc_bank(name)[:, t * S:(t + 1) * S], qT[:, 2 * hd + k, t * P:(t + 1) * P],
                                         kT[:, 2 * hd + k, :], start=(k == 0), stop=(k == 1))
                last.then_inc(misc_filled, 1)

            def prob_turn(hd):
                name = f"probT{hd}"
                wait_misc_free(pe, name)
                pe.wait_ge(prob_made, hd + 1)
                for m in range(T):
                    for t in range(T):
                        at = m * S + t * P
                        last = pe.transpose(misc_bank(name)[:, at:at + P], prob[:, hd, t, m * P:(m + 1) * P], ident[:, :])
                last.then_inc(misc_filled, 1)

            def attend(hd):
                name = f"o{hd}"
                wait_misc_free(pe, name)
                who = MISC_AT[f"probT{hd}"]
                pe.wait_ge(misc_freed["act"], sum(e == "act" for _, e in MISC_USES[:who + 1]))
                for d in range(2):
                    for m in range(T):
                        at = (2 * hd + d) * P
                        last = pe.matmul(misc_bank(name)[:, d * S:(d + 1) * S], v[:, m, at:at + P], probT[:, hd, m, :],
                                         start=(m == 0), stop=(m == 1))
                last.then_inc(misc_filled, 1)

            pe.wait_ge(h_added, T)
            pe.wait_ge(misc_freed["dve"], sum(e == "dve" for _, e in MISC_USES[:MISC_AT["norm2_3"] + 1]))
            pe.wait_ge(misc_freed["act"], sum(e == "act" for _, e in MISC_USES[:MISC_AT["norm2_3"] + 1]))
            q_chunk(0)
            q_chunk(1)
            score(0)
            q_chunk(2)
            score(1)
            prob_turn(0)
            q_chunk(3)
            score(2)
            prob_turn(1)
            attend(0)
            score(3)
            prob_turn(2)
            attend(1)
            prob_turn(3)
            attend(2)
            attend(3)
            pe.wait_ge(misc_freed["act"], sum(e == "act" for _, e in MISC_USES[:MISC_AT["o3"] + 1]))
            for n in range(4):
                dense_landed(pe, O0 + n)
                project_rows(O0 + n, oT, n, True, True)
            norm_turn(3)

            pe.wait_ge(misc_freed["dve"], sum(e == "dve" for _, e in MISC_USES[:MISC_AT["norm3_3"] + 1]))
            pe.wait_ge(misc_freed["act"], sum(e == "act" for _, e in MISC_USES[:MISC_AT["norm3_3"] + 1]))
            pe.wait_ge(router_landed, 64)
            wait_misc_free(pe, "logits")
            for t in range(T):
                for k in range(KT):
                    last = pe.matmul(misc_bank("logits")[:, t * EXPERTS:(t + 1) * EXPERTS], xT[:, k, t * P:(t + 1) * P],
                                     wr[:, k, :], start=(k == 0), stop=(k == KT - 1))
            last.then_inc(misc_filled, 1)
            wait_misc_free(pe, "rank")
            pe.wait_ge(sel_made, T)
            bank = misc_bank("rank")
            pe.matmul(bank[:, 0:EXPERTS], before[:, :], sel[:, 0, :], start=True, stop=True)
            pe.matmul(bank[:, EXPERTS:2 * EXPERTS], ones, sel[:, 0, :], start=True, stop=False)
            pe.matmul(bank[:, EXPERTS:2 * EXPERTS], before[:, :], sel[:, 1, :], start=False, stop=True)
            for t in range(T):
                last = pe.matmul(bank[0:EXPERTS, 2 * EXPERTS:2 * EXPERTS + 1], sel[:, t, :], ones[:, 0:1],
                                 start=(t == 0), stop=(t == 1))
            last.then_inc(misc_filled, 1)
            wait_misc_free(pe, "spill")
            pe.wait_ge(spill_made, 1)
            pe.wait_ge(gates_made, T)
            bank = misc_bank("spill")
            pe.matmul(bank[0:EXPERTS, BANK - 2:BANK - 1], before[0:EXPERTS, 0:EXPERTS], spill_cols[:, 4:5],
                      start=True, stop=True)
            pe.matmul(bank[0:1, BANK - 1:BANK], spill_cols[:, 4:5], ones[0:EXPERTS, 0:1], start=True, stop=True)\
                .then_inc(misc_filled, 1)
            wait_misc_free(pe, "tables")
            bank = misc_bank("tables")
            for t in range(T):
                pe.transpose(bank[0:EXPERTS, t * P:(t + 1) * P], rank_tab[:, t, 0:EXPERTS], ident[:, :])
                last = pe.transpose(bank[0:EXPERTS, S + t * P:S + (t + 1) * P], gate_tab[:, t, 0:EXPERTS], ident[:, :])
            last.then_inc(misc_filled, 1)
            wait_misc_free(pe, "first")
            pe.wait_ge(rgT_made, 1)
            pe.wait_ge(hot_made, 1)
            bank = misc_bank("first")
            for w in range(2):
                for t in range(T):
                    at = (2 * w + t) * SPILLS
                    pe.matmul(bank[:, at:at + SPILLS], rgT[:, w, t * P:(t + 1) * P], one_hot[:, 1, :],
                              start=True, stop=True)
            pe.matmul(bank[0:1, 4 * SPILLS:5 * SPILLS], part_id[0:EXPERTS, :], one_hot[:, 1, :], start=True, stop=True)\
                .then_inc(misc_filled, 1)

            pe.wait_ge(h_added, 2 * T)
            for t in range(T):
                for half in range(2):
                    pe.matmul(wide[:, 2 * t + half, :], rgT[:, 1, t * P:(t + 1) * P],
                              bdown[:, half * BANK:(half + 1) * BANK], start=True, stop=False, skip_group_check=True)

            def gather(i):
                pe.wait_ge(pick_made, i + 1)
                for k in range(KT):
                    for t in range(T):
                        last = pe.matmul(turn_ps[:, k * SLOTS:(k + 1) * SLOTS], xn[:, t, k * P:(k + 1) * P],
                                         pick[:, t, :], start=(t == 0), stop=(t == T - 1))
                last.then_inc(picked, 1)

            def combine():
                for t in range(T):
                    for half in range(2):
                        at = slice(SLOTS * half, SLOTS * (half + 1))
                        last = pe.matmul(wide[:, 2 * t + half, :], put[at, t * P:(t + 1) * P], y_sb[at, :],
                                         start=False, stop=False, skip_group_check=True)
                last.then_inc(combined, 1)

            def expert(i):
                pe.wait_ge(gu_freed, i + 1)
                pe.wait_ge(bias_landed, (i + 1) * 16)
                for n in range(2):
                    for half in range(2):
                        at = half * D + n * BANK
                        last = pe.matmul(gu_ps[SLOTS * half:SLOTS * (half + 1), n * BANK:(n + 1) * BANK],
                                         ones[0:1, 0:SLOTS], bias_row[:, at:at + BANK], start=True, stop=False,
                                         skip_group_check=True)
                last.then_inc(bias_used, 1)
                pe.wait_ge(xsel_made, i + 1)
                for k in range(UP_CHUNKS):
                    item_landed(pe, i, k)
                    for n in range(2):
                        for half in range(2):
                            at = half * D + n * BANK
                            last = pe.matmul(gu_ps[SLOTS * half:SLOTS * (half + 1), n * BANK:(n + 1) * BANK],
                                             xsel[:, k, :], ring[:, k, at:at + BANK], start=False,
                                             stop=(k == UP_CHUNKS - 1), skip_group_check=True)
                    last.then_inc(chunk_used, 1)
                    if k == 1:
                        pe.wait_ge(y_made, i + 1)
                        pe.wait_ge(put_made, i + 1)
                        combine()
                pe.wait_ge(pick_gate_made, i + 1)
                for t in range(T):
                    last = pe.transpose(y_ps[:, t * P:(t + 1) * P], pick_gate[:, t, :], ident[:, :])
                last.then_inc(put_turned, 1)
                gather(i + 1)
                pe.wait_ge(act_made, i + 1)
                pe.wait_ge(xsel_made, i + 2)
                for j in range(4):
                    last = pe.transpose(turn_ps[:, j * P:(j + 1) * P], act_sb[:, j * P:(j + 1) * P], ident[:, :])
                last.then_inc(act_turned, 1)
                pe.wait_ge(actT_made, i + 1)
                pe.wait_ge(put_made, i + 2)
                for c in range(DOWN_CHUNKS):
                    item_landed(pe, i, UP_CHUNKS + c)
                    for kk in range(2):
                        f = 2 * c + kk
                        for half in range(2):
                            at = kk * D + half * BANK
                            last = pe.matmul(y_ps[SLOTS * half:SLOTS * (half + 1), :],
                                             actT[:, f % 4, SLOTS * (f // 4):SLOTS * (f // 4 + 1)],
                                             ring[:, UP_CHUNKS + c, at:at + BANK], start=(f == 0), stop=(f == 7),
                                             skip_group_check=True)
                    last.then_inc(chunk_used, 1)

            gather(0)
            with pe.Fori(0, EXPERTS) as i:
                expert(i)
            pe.wait_ge(tables_made, 1)
            spills = pe.value_load(spill_int[0:1, SPILLS:SPILLS + 1], min_val=0, max_val=SPILLS)
            with pe.If(spills > 0):
                with pe.Fori(0, spills) as j:
                    expert(j + EXPERTS)
            pe.wait_ge(y_made, spills + (EXPERTS + 1))
            pe.wait_ge(put_made, spills + (EXPERTS + 1))
            combine()

        @block.vector
        def _(dve):
            steps = [1]

            def step(ins):
                steps[0] += 1
                ins.then_inc(dve_step, 1)
                dve.wait_ge(dve_step, steps[0])

            def norm(n):
                src, sq, dst = norm_stage(n)
                if n >= 2:
                    dve.wait_ge(h_added, T * (n - 1))
                dve.tensor_tensor_reduce(sq[:, 1, :], src[:, 1, :], src[:, 1, :], 1.0, 0.0, ALU.mult, ALU.add,
                                         stats[:, n, 0, 1:2]).then_inc(squared["dve"], 1)
                dve.wait_ge(squared["dve"], n + 1)
                dve.wait_ge(squared["act"], n + 1)
                dve.tensor_scalar(stats[:, n, 1, :], stats[:, n, 0, :], 1.0 / D, EPS, ALU.mult, ALU.add)\
                    .then_inc(mean_made, 1)
                dve.wait_ge(root_made, n + 1)
                dve.reciprocal(stats[:, n, 3, :], stats[:, n, 2, :]).then_inc(rstd_made, 1)
                dve.wait_ge(rstd_made, n + 1)
                if n < 4:
                    dve.tensor_scalar(dst[:, 1, :], src[:, 1, :], stats[:, n, 3, 1:2], None, ALU.mult)\
                        .then_inc(normed["dve"], 1)

            def norm_turned(n):
                for b in (0, 2):
                    wait_misc_filled(dve, f"norm{n}_{b}")
                    bank = misc_bank(f"norm{n}_{b}")
                    for j in range(2):
                        k = 2 * b + j
                        last = dve.tensor_scalar(norm_T(n)[:, k, :], bank[:, j * S:(j + 1) * S],
                                                 par[:, NORM_GAIN[n] + k:NORM_GAIN[n] + k + 1], None, ALU.mult)
                    last.then_inc(misc_freed["dve"], 1)

            def freed(ins):
                ins.then_inc(misc_freed["dve"], 1)

            dve.wait_ge(x_landed, 16)
            norm(0)
            wait_misc_filled(dve, "params")
            dve.tensor_copy(par[:, :], misc_bank("params")[:, 0:PAR]).then_inc(dve_step, 1)
            dve.wait_ge(dve_step, 1)
            dve.tensor_copy(sp[:, 7, 0:1], par[:, 0:1]).then_inc(misc_freed["dve"], 1)
            norm_turned(0)

            dve.wait_ge(heads_landed, 64)
            wait_misc_filled(dve, "dt")
            step(dve.tensor_scalar(sp[:, 0, 32:40], par[:, LAM:LAM + KT], -1.0, None, ALU.mult))
            for t in range(T):
                last = dve.tensor_tensor(sp[:, 0, t * HEADS:(t + 1) * HEADS], misc_bank("dt")[:, t * HEADS:(t + 1) * HEADS],
                                         heads_bc[:, 0, :], ALU.add)
            freed(last)
            dve.wait_ge(misc_freed["dve"], 4)
            dve.scalar_tensor_tensor(out=sp[:, 1, :], in0=sp[:, 0, :], scalar=-1.0, in1=sp[:, 0, :], op0=ALU.mult,
                                     op1=ALU.min).then_inc(sp_step, 1)
            dve.wait_ge(sp_act, 1)
            dve.tensor_scalar(sp[:, 3, :], sp[:, 2, :], 1.0, None, ALU.add).then_inc(sp_step, 1)
            dve.wait_ge(sp_step, 2)
            step(dve.tensor_scalar(sp[:, 5, :], sp[:, 3, :], -1.0, None, ALU.add))
            step(dve.tensor_scalar(sp[:, 6, :], sp[:, 5, :], 0.0, None, ALU.is_equal))
            step(dve.tensor_tensor(sp[:, 5, :], sp[:, 5, :], sp[:, 6, :], ALU.add))
            step(dve.reciprocal(sp[:, 7, :], sp[:, 5, :]))
            dve.wait_ge(sp_act, 3)
            step(dve.tensor_tensor(sp[:, 7, :], sp[:, 7, :], sp[:, 4, :], ALU.mult))
            step(dve.tensor_tensor(sp[:, 7, :], sp[:, 7, :], sp[:, 6, :], ALU.add))
            step(dve.tensor_tensor(sp[:, 7, :], sp[:, 7, :], sp[:, 2, :], ALU.mult))
            step(dve.scalar_tensor_tensor(out=sp[:, 5, :], in0=sp[:, 0, :], scalar=0.0, in1=sp[:, 7, :], op0=ALU.max,
                                          op1=ALU.add))
            dve.tensor_scalar(lru_rate[:, :], sp[:, 5, 32:40], -RG_C, None, ALU.mult).then_inc(rate_made, 1)
            for t in range(T):
                part = sp[:, 5, t * HEADS:(t + 1) * HEADS]
                dve.tensor_copy(dt[:, t, :], part)
                last = dve.scalar_tensor_tensor(out=dtA[:, t, :], in0=part, scalar=-1.0, in1=expA[:, :], op0=ALU.mult,
                                                op1=ALU.mult)
            last.then_inc(dtA_made, 1)
            pairs = heads_bc[:, 2, :].rearrange("p (j b) -> p b j", b=2)
            for b in range(2):
                step(dve.tensor_copy(d_col[64 * b:64 * b + 64, :], pairs[64 * b:64 * b + 64, b, :]))

            dve.wait_ge(mem_landed, 16)
            norm(1)

            def convolve(n, buf, dst, j, taps, tap_step, bias):
                dve.wait_ge(pad_filled, n + 1)
                for tap in range(4):
                    if tap:
                        dve.wait_ge(tap_done, n * 3 + tap)
                    for b in range(2):
                        o = dst[:, j + b, :]
                        src = xpad[:, buf, b, tap:tap + S]
                        col = taps + tap * tap_step + j + b
                        if tap == 0:
                            last = dve.tensor_scalar(o, src, par[:, col:col + 1], par[:, bias + j + b:bias + j + b + 1],
                                                     ALU.mult, ALU.add)
                        else:
                            last = dve.scalar_tensor_tensor(out=o, in0=src, scalar=par[:, col:col + 1], in1=o,
                                                            op0=ALU.mult, op1=ALU.add)
                    last.then_inc(convolved if tap == 3 else tap_done, 1)

            for n in range(4):
                convolve(n, n % 2, xr, 2 * n, LCW, 8, LCB)
            for n in range(8):
                convolve(4 + n, n % 2, xbc, 2 * n, SCW, 16, SCB)

            wait_misc_filled(dve, "cumsum")
            bank = misc_bank("cumsum")
            dve.tensor_copy(seg_bias[:, 1, :], bank[:, 2 * HEADS:3 * HEADS]).then_inc(dve_step, 1)
            steps[0] += 1
            dve.tensor_scalar(seg_bias[:, 0, :], bank[:, 0:HEADS], -1.0, None, ALU.mult)
            dve.tensor_scalar(seg_bias[:, 2, :], bank[:, HEADS:2 * HEADS], -1.0, None, ALU.mult).then_inc(misc_freed["dve"], 1)
            dve.wait_ge(misc_freed["dve"], 5)
            dve.tensor_tensor(seg_bias[:, 1, :], seg_bias[:, 1, :], seg_bias[:, 0, :], ALU.add).then_inc(seg_made, 1)
            dve.wait_ge(seg_made, 1)
            norm_turned(1)

            for t in range(T):
                for half in range(2):
                    name = f"xdt{2 * t + half}"
                    wait_misc_filled(dve, name)
                    freed(dve.tensor_tensor(
                        xdt[:, t, half * BANK:(half + 1) * BANK].rearrange("p (h c) -> p h c", c=HEAD_P),
                        misc_bank(name).rearrange("p (h c) -> p h c", c=HEAD_P),
                        dt[:, t, 8 * half:8 * half + 8].unsqueeze(2).broadcast_to([P, 8, HEAD_P]), ALU.mult))
            for g in range(GROUPS):
                wait_misc_filled(dve, f"cb{g}")
                freed(dve.tensor_tensor(cbm[:, g, :], misc_bank(f"cb{g}")[:, 0:3 * P], mask3[:, :], ALU.mult))

            def exponents(q):
                name = f"rows{q}"
                wait_misc_filled(dve, name)
                if q >= 2:
                    wait_misc_filled(dve, f"y{q - 2}")
                bank = misc_bank(name)
                for hh in range(2):
                    for part in range(3):
                        at = hh * S + (P if part else 0)
                        hd = 2 * q + hh
                        last = dve.tensor_scalar(mt[:, q % 2, hh, part * P:(part + 1) * P], bank[:, at:at + P],
                                                 seg_bias[:, part, hd:hd + 1], 0.0, ALU.add, ALU.min)
                        if part == 2 and hh == 0:
                            last.then_inc(dve_step, 1)
                            steps[0] += 1
                last.then_inc(misc_freed["dve"], 1)

            def exponents_done(q):
                dve.wait_ge(misc_freed["dve"], sum(e == "dve" for _, e in MISC_USES[:MISC_AT[f"rows{q}"] + 1]))
                dve.tensor_copy(sp[:, 0, q:q + 1], seg_bias[:, 0, 0:1]).then_inc(seg_made, 1)

            exponents(0)
            exponents_done(0)
            dve.wait_ge(decay_made, 1)
            dve.wait_ge(chunk_used, IN_CHUNKS)
            step(dve.tensor_tensor(xT[:, :, :], ab, ab, ALU.mult))
            dve.scalar_tensor_tensor(out=rb, in0=xT[:, :, :], scalar=1.0, in1=rb, op0=ALU.add, op1=ALU.mult)\
                .then_inc(lru_poly, 1)
            step(dve.tensor_tensor(ib, ib, xr, ALU.mult))
            dve.wait_ge(lru_root, 1)
            step(dve.tensor_tensor(ib, ib, rb, ALU.mult))
            for j in range(KT):
                last = dve.tensor_tensor_scan(rb[:, j, :], ab[:, j, :], ib[:, j, :], 0.0, ALU.mult, ALU.add)
            step(last)
            dve.tensor_tensor(gg, gg, rb, ALU.mult).then_inc(lru_out, 1)

            for q in range(8):
                dve.wait_ge(seg_exp, q + 1)
                m = mt[:, q % 2, :, :]
                dve.tensor_tensor(m, m, cbm[:, q // 2, :].unsqueeze(1).broadcast_to([P, 2, 3 * P]), ALU.mult)\
                    .then_inc(mt_made, 1)
                if q + 1 < 8:
                    exponents(q + 1)
                    exponents_done(q + 1)
                name = f"y{q}"
                wait_misc_filled(dve, name)
                xs = xsT[:, q, :]
                freed(dve.scalar_tensor_tensor(out=xs, in0=xs, scalar=d_col[:, q:q + 1], in1=misc_bank(name)[:, 0:S],
                                               op0=ALU.mult, op1=ALU.add))
                dve.wait_ge(misc_freed["dve"], sum(e == "dve" for _, e in MISC_USES[:MISC_AT[name] + 1]))
                step(dve.tensor_tensor(zs[:, q, :], zs[:, q, :], xs, ALU.mult))
                dve.tensor_tensor(xs, zs[:, q, :], zs[:, q, :], ALU.mult).then_inc(ssd_squares, 1)
            for n in range(2):
                name = f"power{n}"
                wait_misc_filled(dve, name)
                last = dve.tensor_scalar(group_scale[:, 2 * n:2 * n + 2, :],
                                         misc_bank(name).rearrange("p (g s) -> p g s", g=2), 1.0 / 256, EPS,
                                         ALU.mult, ALU.add)
                freed(last)
            dve.wait_ge(misc_freed["dve"], sum(e == "dve" for _, e in MISC_USES[:MISC_AT["power1"] + 1]))
            dve.tensor_copy(sp[:, 0, 0:1], seg_bias[:, 0, 0:1]).then_inc(power_made, 1)
            dve.wait_ge(ssd_root, 1)
            step(dve.reciprocal(group_scale, group_scale))
            for j in range(KT):
                last = dve.scalar_tensor_tensor(out=zs[:, j, :], in0=zs[:, j, :], scalar=par[:, SNORM + j:SNORM + j + 1],
                                                in1=group_scale[:, j // 2, :], op0=ALU.mult, op1=ALU.mult)
            last.then_inc(ssd_out, 1)

            def add_to_h():
                for t in range(T):
                    dve.tensor_tensor(h[:, t, :], h[:, t, :], wide[:, 2 * t:2 * t + 2, :].rearrange("p b n -> p (b n)"),
                                      ALU.add).then_inc(h_added, 1)

            dve.wait_ge(chunk_used, Q0)
            add_to_h()
            norm(2)
            norm_turned(2)

            for hd in range(X_HEADS):
                name = f"score{hd}"
                wait_misc_filled(dve, name)
                step(dve.tensor_reduce(soft[:, hd, 0, :], misc_bank(name).rearrange("p (t m) -> p t m", t=T), AX_X, ALU.max))
                dve.tensor_scalar(soft[:, hd, 1, :], soft[:, hd, 0, :], -X_SCALE, None, ALU.mult).then_inc(score_max, 1)
                dve.wait_ge(misc_freed["act"], sum(e == "act" for _, e in MISC_USES[:MISC_AT[name] + 1]))
                step(dve.reciprocal(soft[:, hd, 3, :], soft[:, hd, 2, :]))
                for t in range(T):
                    last = dve.tensor_scalar(prob[:, hd, t, :], prob[:, hd, t, :], soft[:, hd, 3, t:t + 1], None, ALU.mult)
                last.then_inc(prob_made, 1)

            dve.wait_ge(chunk_used, DENSE)
            add_to_h()
            norm(3)
            norm_turned(3)

            dve.wait_ge(router_landed, 64)
            wait_misc_filled(dve, "logits")
            for t in range(T):
                last = dve.tensor_tensor(lg[:, t, :], misc_bank("logits")[:, t * EXPERTS:(t + 1) * EXPERTS], br, ALU.add)
            freed(last)
            dve.wait_ge(misc_freed["dve"], sum(e == "dve" for _, e in MISC_USES[:MISC_AT["logits"] + 1]))
            for t in range(T):
                step(dve.max(top8[:, t, :], lg[:, t, :]))
            for t in range(T):
                dve.tensor_scalar(top_neg[:, t:t + 1], top8[:, t, 0:1], -1.0, None, ALU.mult).then_inc(logits_made, 1)
            step(dve.memset(top8[:, :, TOP_K:8], 3.0e38))
            for t in range(T):
                last = dve.match_replace(sel[:, t, :], top8[:, t, :], lg[:, t, :], -3.0e38)
            step(last)
            for t in range(T):
                dve.tensor_tensor(sel[:, t, :], sel[:, t, :], lg[:, t, :], ALU.not_equal).then_inc(sel_made, 1)
            dve.wait_ge(sel_made, T)
            for t in range(T):
                dve.wait_ge(gate_exp, t + 1)
                step(dve.tensor_tensor_reduce(rest[:, t, :], rest[:, t, :], sel[:, t, :], 1.0, 0.0, ALU.mult, ALU.add,
                                              gsum[:, 0, t:t + 1]))
            step(dve.reciprocal(gsum[:, 1, :], gsum[:, 0, :]))
            wait_misc_filled(dve, "rank")
            bank = misc_bank("rank")
            for t in range(T):
                step(dve.scalar_tensor_tensor(out=rank_tab[:, t, 0:EXPERTS], in0=sel[:, t, :], scalar=-4096.0,
                                              in1=bank[:, t * EXPERTS:(t + 1) * EXPERTS], op0=ALU.mult, op1=ALU.add))
            step(dve.tensor_scalar(rank_tab[:, :, 0:EXPERTS], rank_tab[:, :, 0:EXPERTS], 4096.0, None, ALU.add))
            freed(dve.tensor_copy(spill_cols[:, 0:1], bank[0:EXPERTS, 2 * EXPERTS:2 * EXPERTS + 1]))
            dve.wait_ge(misc_freed["dve"], sum(e == "dve" for _, e in MISC_USES[:MISC_AT["rank"] + 1]))
            for t in range(T):
                dve.tensor_scalar(gate_tab[:, t, 0:EXPERTS], rest[:, t, :], gsum[:, 1, t:t + 1], None, ALU.mult)\
                    .then_inc(gates_made, 1)
            for n in range(3):
                step(dve.tensor_scalar(spill_cols[:, 1 + n:2 + n], spill_cols[:, 0:1], float(SLOTS * (n + 1)), None,
                                       ALU.is_gt))
            dve.tensor_reduce(spill_cols[:, 4:5], spill_cols[:, 1:4], AX_X, ALU.add).then_inc(spill_made, 1)
            dve.wait_ge(spill_made, 1)
            wait_misc_filled(dve, "spill")
            bank = misc_bank("spill")
            step(dve.tensor_copy(spill_cols[:, 5:6], bank[0:EXPERTS, BANK - 2:BANK - 1]))
            step(dve.tensor_copy(spill_int[:, SPILLS:SPILLS + 1], bank[0:1, BANK - 1:BANK]))
            step(dve.tensor_tensor(spill_cols[:, 6:7], spill_cols[:, 5:6], spill_cols[:, 4:5], ALU.add))
            freed(dve.tensor_scalar(spill_cols[:, 7:8], spill_cols[:, 5:6], float(SLOTS), None, ALU.mult))
            dve.wait_ge(misc_freed["dve"], sum(e == "dve" for _, e in MISC_USES[:MISC_AT["spill"] + 1]))
            step(dve.tensor_scalar(one_hot[:, 0, :], spill_id[0:EXPERTS, :], spill_cols[:, 5:6], None, ALU.is_ge))
            dve.scalar_tensor_tensor(out=one_hot[:, 1, :], in0=spill_id[0:EXPERTS, :], scalar=spill_cols[:, 6:7],
                                     in1=one_hot[:, 0, :], op0=ALU.is_lt, op1=ALU.mult).then_inc(hot_made, 1)
            wait_misc_filled(dve, "tables")
            bank = misc_bank("tables")
            dve.tensor_scalar(rgT[:, 0, :], bank[0:EXPERTS, 0:S], spill_cols[:, 7:8], None, ALU.add).then_inc(dve_step, 1)
            steps[0] += 1
            freed(dve.tensor_copy(rgT[:, 1, :], bank[0:EXPERTS, S:2 * S]))
            dve.wait_ge(misc_freed["dve"], sum(e == "dve" for _, e in MISC_USES[:MISC_AT["tables"] + 1]))
            dve.tensor_copy(sp[:, 0, 0:1], seg_bias[:, 0, 0:1]).then_inc(rgT_made, 1)
            wait_misc_filled(dve, "first")
            bank = misc_bank("first")
            n0, n1 = EXPERTS, EXPERTS + SPILLS
            dve.memset(rank_tab[:, :, n1:n1 + 1], -1.0)
            dve.memset(gate_tab[:, :, n1:n1 + 1], 0.0)
            for t in range(T):
                dve.tensor_tensor(rank_tab[:, t, n0:n1], bank[:, t * SPILLS:(t + 1) * SPILLS], spill_base[:, :],
                                  ALU.subtract)
                dve.tensor_copy(gate_tab[:, t, n0:n1], bank[:, (2 + t) * SPILLS:(3 + t) * SPILLS])
            dve.tensor_copy(spill_int[:, 0:SPILLS], bank[0:1, 4 * SPILLS:5 * SPILLS]).then_inc(tables_made, 1)
            dve.wait_ge(tables_made, 1)

            def make_pick(i):
                for t in range(T):
                    last = dve.tensor_scalar(pick[:, t, :], slot_id[:, 0:SLOTS], rank_tab[:, t, bass.ds(i, 1)], None,
                                             ALU.is_equal)
                last.then_inc(pick_made, 1)

            def make_pick_gate(i):
                for t in range(T):
                    last = dve.tensor_scalar(pick_gate[:, t, :], slot_id[:, :], rank_tab[:, t, bass.ds(i, 1)],
                                             gate_tab[:, t, bass.ds(i, 1)], ALU.is_equal, ALU.mult)
                last.then_inc(pick_gate_made, 1)

            def take_xsel(i):
                dve.wait_ge(picked, i + 1)
                dve.tensor_tensor(xsel, turn_ps.rearrange("p (k c) -> p k c", k=KT),
                                  par[:, NMOE:NMOE + KT].unsqueeze(2).broadcast_to([P, KT, SLOTS]), ALU.mult)\
                    .then_inc(xsel_made, 1)

            make_pick(0)
            make_pick_gate(0)
            dve.memset(top_neg[:, :], 0.0).then_inc(gu_freed, 1)
            take_xsel(0)

            def expert(i):
                make_pick(i + 1)
                used(dve, i, UP_CHUNKS - 1)
                pairs_ = gu_ps.rearrange("p (f b) -> p b f", b=2)
                dve.tensor_scalar(g_sb, pairs_[:, 0, :], LIMIT, None, ALU.min).then_inc(g_made, 1)
                dve.tensor_scalar(u_sb, pairs_[:, 1, :], LIMIT, -LIMIT, ALU.min, ALU.max).then_inc(gu_freed, 1)
                dve.wait_ge(sig_made, i + 1)
                dve.tensor_tensor(g_sb, g_sb, sig, ALU.mult).then_inc(gated, 1)
                dve.wait_ge(gated, i + 1)
                dve.scalar_tensor_tensor(out=act_sb, in0=u_sb, scalar=1.0, in1=g_sb, op0=ALU.add, op1=ALU.mult)\
                    .then_inc(act_made, 1)
                take_xsel(i + 1)
                dve.wait_ge(put_turned, i + 1)
                make_pick_gate(i + 1)

            with dve.Fori(0, EXPERTS) as i:
                expert(i)
            spills = dve.value_load(spill_int[0:1, SPILLS:SPILLS + 1], min_val=0, max_val=SPILLS)
            with dve.If(spills > 0):
                with dve.Fori(0, spills) as j:
                    expert(j + EXPERTS)
            dve.wait_ge(combined, spills + (EXPERTS + 1))
            add_to_h()
            norm(4)
            dve.wait_ge(router_landed, 64)
            for t in range(T):
                dve.scalar_tensor_tensor(out=xn[:, t, :], in0=h[:, t, :], scalar=stats[:, 4, 3, t:t + 1],
                                         in1=gain_row[:, :], op0=ALU.mult, op1=ALU.mult).then_inc(out_made, 1)


_INS = ['x', 'mem', 'norm_mix', 'w_in', 'ssd_conv_w', 'ssd_conv_b', 'ssd_dt_bias', 'ssd_a_log', 'ssd_d', 'ssd_norm',
        'lru_conv_w', 'lru_conv_b', 'lru_wa', 'lru_ba', 'lru_wx', 'lru_bx', 'lru_lambda', 'w_out',
        'norm_xattn', 'norm_mem', 'w_q', 'w_kv', 'w_o', 'norm_moe', 'w_router', 'b_router',
        'w_gate_up', 'b_gate_up', 'w_down', 'b_down', 'norm_final']
_OUTS = [((1, 256, 1024), 'float32')]


def kernel(**inputs):
    import numpy as _np
    import concourse.bacc as _bacc
    from concourse import mybir as _mybir
    from concourse.bass_utils import run_bass_kernel_spmd as _run

    nc = _bacc.Bacc("TRN2", target_bir_lowering=False, num_devices=1)
    arrays, args = {}, []
    for name in _INS:
        a = _np.ascontiguousarray(inputs[name])
        arrays[f"in_{name}_dram"] = a
        args.append(nc.dram_tensor(f"in_{name}_dram", a.shape, _mybir.dt.from_np(a.dtype), kind="ExternalInput").ap())
    for i, (shape, dtype) in enumerate(_OUTS):
        dt = _mybir.dt.from_np(_np.dtype(dtype))
        args.append(nc.dram_tensor(f"out_{i}_dram", shape, dt, kind="ExternalOutput").ap())
    hybrid_trunk_kernel(nc, *args)
    r = _run(nc, [arrays], core_ids=[0])
    got = tuple(r.results[0][f"out_{i}_dram"] for i in range(len(_OUTS)))
    return got[0]
```

```python
from contextlib import ExitStack

import concourse.bass as bass
from concourse import mybir

F32 = mybir.dt.float32
I32 = mybir.dt.int32
ALU = mybir.AluOpType
ACT = mybir.ActivationFunctionType
AX_X = mybir.AxisListType.X

P = 128
BANK = 512
D = 1024
S = 256
T = S // P
KT = D // P
EPS = 1e-6
HEADS = 16
HEAD_P = 64
GROUPS = 4
X_HEADS = 4
X_SCALE = float(D // X_HEADS) ** -0.5
RG_C = 8.0
EXPERTS = 32
TOP_K = 4
SLOTS = 64
PAIRS = EXPERTS // 2
SPILLS = 16
LIMIT = 7.0
ALPHA = 1.702

SLOT = 2048
RING = 12
CHUNK_COLS = SLOT // KT
DENSE_RING = 4
IN_CHUNKS, KV_CHUNKS, OUT_CHUNKS, Q_CHUNKS, O_CHUNKS = 20, 8, 8, 4, 4
KV0 = IN_CHUNKS
OUT0 = KV0 + KV_CHUNKS
Q0 = OUT0 + OUT_CHUNKS
O0 = Q0 + Q_CHUNKS
DENSE = O0 + O_CHUNKS
UP_CHUNKS, DOWN_CHUNKS = 8, 4
PAIR_CHUNKS = 2 * (UP_CHUNKS + DOWN_CHUNKS)

LCW, SCW, SCB, LCB, BA = 0, 32, 96, 112, 120
BX, LAM, SNORM, NMIX, NX, NMEM, NMOE = 128, 136, 144, 152, 160, 168, 176
PAR = 184

MISC_USES = ([("params", "dve")]
             + [(f"norm0_{n}", "dve" if n % 2 == 0 else "act") for n in range(4)]
             + [("dt", "dve"), ("cumsum", "dve")]
             + [(f"norm1_{n}", "dve" if n % 2 == 0 else "act") for n in range(4)]
             + [(f"lru{j}", "act") for j in range(8)]
             + [(f"xdt{n}", "dve") for n in range(4)]
             + [("rows0", "dve")]
             + [(f"cb{g}", "dve") for g in range(4)]
             + [x for q in range(8) for x in ([(f"rows{q + 1}", "dve")] if q < 7 else []) + [(f"y{q}", "dve")]]
             + [(f"power{n}", "dve") for n in range(2)]
             + [(f"norm2_{n}", "dve" if n % 2 == 0 else "act") for n in range(4)]
             + [(n, "act") for n in "score0 score1 probT0 score2 probT1 o0 score3 probT2 o1 probT3 o2 o3".split()]
             + [(f"norm3_{n}", "dve" if n % 2 == 0 else "act") for n in range(4)]
             + [("logits", "dve"), ("rank", "dve")])
MISC_AT = {name: n for n, (name, _) in enumerate(MISC_USES)}


def hybrid_trunk_kernel(nc, x, mem, norm_mix, w_in, ssd_conv_w, ssd_conv_b, ssd_dt_bias, ssd_a_log, ssd_d,
                        ssd_norm, lru_conv_w, lru_conv_b, lru_wa, lru_ba, lru_wx, lru_bx, lru_lambda, w_out,
                        norm_xattn, norm_mem, w_q, w_kv, w_o, norm_moe, w_router, b_router,
                        w_gate_up, b_gate_up, w_down, b_down, norm_final, out):
    with ExitStack() as ctx:
        def sb(name, shape, dt=F32):
            return ctx.enter_context(nc.sbuf_tensor(name, shape, dt))

        def sem(name):
            return ctx.enter_context(nc.semaphore(name))

        ring = sb("ring", [P, RING, SLOT])
        h = sb("h", [P, T, D])
        xn = sb("xn", [P, T, D])
        xT = sb("xT", [P, KT, S])
        xbc = sb("xbc", [P, 16, S])
        zs = sb("zs", [P, KT, S])
        kT = sb("kT", [P, KT, S])
        v = sb("v", [P, T, D])
        gain_row = sb("gain_row", [P, D])
        scratch = sb("scratch", [P, 6400])
        ident = sb("ident", [P, P])
        mask3 = sb("mask3", [P, 3 * P])
        before = sb("before", [P, P])
        slot_id = sb("slot_id", [P, P])
        spill_id = sb("spill_id", [P, SPILLS])
        spill_base = sb("spill_base", [P, SPILLS])
        part_id = sb("part_id", [P, 1])
        rowsA = sb("rowsA", [P, P])
        rowsB = sb("rowsB", [PAR - P, P])
        par = sb("par", [P, PAR])
        w_dt = sb("w_dt", [P, KT, HEADS])
        heads_bc = sb("heads_bc", [P, 3, HEADS])
        d_col = sb("d_col", [P, KT])
        sp = sb("sp", [P, 8, 40])
        dt = sb("dt", [P, T, HEADS])
        dtA = sb("dtA", [P, T, HEADS])
        expA = sb("expA", [P, HEADS])
        lru_rate = sb("lru_rate", [P, KT])
        seg_bias = sb("seg_bias", [P, 3, HEADS])
        stats = sb("stats", [P, 5, 6, T])
        spare = sb("spare", [P, 16])
        soft = sb("soft", [P, X_HEADS, 4, T])
        lg = sb("lg", [P, T, EXPERTS])
        top8 = sb("top8", [P, T, 8])
        top_neg = sb("top_neg", [P, T])
        rest = sb("rest", [P, T, EXPERTS])
        sel = sb("sel", [P, T, EXPERTS])
        gsum = sb("gsum", [P, 2, T])
        rank_tab = sb("rank_tab", [P, T, EXPERTS + SPILLS + 2])
        gate_tab = sb("gate_tab", [P, T, EXPERTS + SPILLS + 2])
        spill_cols = sb("spill_cols", [EXPERTS, 8])
        one_hot = sb("one_hot", [EXPERTS, 2, SPILLS])
        rgT = sb("rgT", [EXPERTS, 2, S])
        spill_int = sb("spill_int", [1, SPILLS + 1], I32)

        tri = mask3[:, 0:P]
        ones = mask3[:, P:2 * P]

        def slot_view(n):
            return ring[:, n, :].rearrange("p (k s) -> p k s", k=KT)

        mnT, rb, ib, ab, gg, xr = (slot_view(n) for n in range(4, 10))
        xdt = ring[:, 10, :].rearrange("p (t c) -> p t c", t=T)
        mem_sb = ring[:, 11, :].rearrange("p (t c) -> p t c", t=T)
        junk = zs[:, :, :].rearrange("p k s -> p (k s)")
        xsT, bcT = xbc[:, 0:8, :], xbc[:, 8:16, :]
        group_scale = xbc[:, 8:12, :]
        qT, oT = xbc[:, 0:8, :], xbc[:, 8:16, :]
        wr = junk[:, 0:KT * EXPERTS].rearrange("p (k e) -> p k e", k=KT)
        br = junk[:, KT * EXPERTS:(KT + 1) * EXPERTS]
        bd = scratch[:, 0:2048].rearrange("p (w j c) -> p w j c", w=2, j=KT)
        xpad = scratch[:, 2048:2048 + 4 * (S + 3)].rearrange("p (b j s) -> p b j s", b=2, j=2)
        cbm = scratch[:, 3088:3088 + 1536].rearrange("p (g l) -> p g l", g=GROUPS)
        mt = scratch[:, 4624:4624 + 1536].rearrange("p (b h l) -> p b h l", b=2, h=2)
        prob = scratch[:, 0:2048].rearrange("p (b t m) -> p b t m", b=4, t=T)
        probT = scratch[:, 2048:4096].rearrange("p (b t m) -> p b t m", b=4, t=T)
        pick = scratch[:, 0:256].rearrange("p (t c) -> p t c", t=T)
        pick_gate = scratch[:, 256:512].rearrange("p (t c) -> p t c", t=T)
        put = scratch[:, 512:768]
        xsel = scratch[:, 768:1792].rearrange("p (k c) -> p k c", k=KT)
        g_sb, sig, u_sb = (scratch[:, 1792 + 512 * n:2304 + 512 * n] for n in range(3))
        act_sb = scratch[:, 3328:4352].rearrange("p (b c) -> p b c", b=2)
        actT = scratch[:, 4352:5376].rearrange("p (b j c) -> p b j c", b=2, j=4)
        y_sb = scratch[:, 5376:6400]
        bias_rows = xbc[:, 0:12, :].rearrange("p k s -> p (k s)")

        wide = ctx.enter_context(nc.psum_tensor("wide", [P, 4, BANK], F32))
        misc = ctx.enter_context(nc.psum_tensor("misc", [P, 4, BANK], F32))
        pair_ps = [misc[:, 2 * n:2 * n + 2, :].rearrange("p b n -> p (b n)") for n in range(2)]

        def misc_bank(name):
            return misc[:, MISC_AT[name] % 4, :]

        consts_made = sem("consts_made")
        x_landed, mem_landed = sem("x_landed"), sem("mem_landed")
        params_landed, heads_landed, gates_landed = sem("params_landed"), sem("heads_landed"), sem("gates_landed")
        router_landed = sem("router_landed")
        ring_landed = [sem(f"ring_landed{n}") for n in range(RING)]
        bias_landed, bias_used = [sem(f"bias_landed{n}") for n in range(2)], sem("bias_used")
        chunk_used = sem("chunk_used")
        misc_filled = sem("misc_filled")
        misc_freed = {"dve": sem("misc_freed_dve"), "act": sem("misc_freed_act")}
        squared = {"dve": sem("squared_dve"), "act": sem("squared_act")}
        mean_made, root_made, rstd_made = sem("mean_made"), sem("root_made"), sem("rstd_made")
        normed = {"dve": sem("normed_dve"), "act": sem("normed_act")}
        dve_step = sem("dve_step")
        sp_step, sp_act = sem("sp_step"), sem("sp_act")
        dtA_made, seg_made, rate_made = sem("dtA_made"), sem("seg_made"), sem("rate_made")
        padded, pad_filled, tap_done, convolved = sem("padded"), sem("pad_filled"), sem("tap_done"), sem("convolved")
        wide_freed = sem("wide_freed")
        silu_made = sem("silu_made")
        decay_made, lru_poly, lru_root, lru_out = (sem(n) for n in ("decay_made", "lru_poly", "lru_root", "lru_out"))
        seg_exp, mt_made, power_made, ssd_root, ssd_out = (
            sem(n) for n in ("seg_exp", "mt_made", "power_made", "ssd_root", "ssd_out"))
        ssd_squares = sem("ssd_squares")
        h_added = sem("h_added")
        score_max, prob_exp, prob_made = sem("score_max"), sem("prob_exp"), sem("prob_made")
        logits_made, gate_exp, sel_made, spill_made, spill_filled, hot_made, tables_made = (
            sem(n) for n in ("logits_made", "gate_exp", "sel_made", "spill_made", "spill_filled", "hot_made",
                             "tables_made"))
        pick_made, pick_gate_made, picked, xsel_made = (
            sem(n) for n in ("pick_made", "pick_gate_made", "picked", "xsel_made"))
        g_made, sig_made, gu_freed, act_made = (sem(n) for n in ("g_made", "sig_made", "gu_freed", "act_made"))
        put_turned, put_made, act_turned, actT_made = (
            sem(n) for n in ("put_turned", "put_made", "act_turned", "actT_made"))
        y_made = {"dve": sem("y_made_dve"), "act": sem("y_made_act")}
        gated = sem("gated")
        combined = sem("combined")
        out_made, stored = sem("out_made"), sem("stored")

        def wait_misc_filled(eng, name):
            eng.wait_ge(misc_filled, MISC_AT[name] + 1)

        def wait_misc_free(pe, name):
            n = MISC_AT[name] - 4
            if n >= 0:
                who = MISC_USES[n][1]
                pe.wait_ge(misc_freed[who], sum(e == who for _, e in MISC_USES[:n + 1]))

        def dense_landed(pe, c):
            pe.wait_ge(ring_landed[c % DENSE_RING], 16 * (c // DENSE_RING + 1))

        def slot_of(n):
            return n % RING

        def pair_landed(pe, p, n):
            dense = DENSE // DENSE_RING if slot_of(n) < DENSE_RING else 0
            pe.wait_ge(ring_landed[slot_of(n)], p * 32 + 16 * (dense + 1 + n // RING))

        def used(eng, p, n):
            eng.wait_ge(chunk_used, p * PAIR_CHUNKS + (DENSE + n + 1))

        w_in_v, w_kv_v, w_q_v, w_o_v = (w[0].rearrange("(k p) n -> p k n", p=P) for w in (w_in, w_kv, w_q, w_o))
        w_out_v = w_out[0].rearrange("(h k p) n -> h p k n", h=2, p=P)
        up_v = w_gate_up[0].rearrange("e (k p) n -> e k p n", p=P)
        down_v = w_down[0].rearrange("e (c k p) n -> e c p k n", k=2, p=P)

        block = ctx.enter_context(nc.Block())

        @block.sync
        def _(sp_):
            def fill(slot, src):
                sp_.dma_start(slot_view(slot), src).then_inc(ring_landed[slot], 16)

            def rows(dst, at, src):
                sp_.dma_start(dst[at:at + src.shape[0], :], src).then_inc(params_landed, 16)

            rows(rowsA, LCW, lru_conv_w[0].rearrange("k (j p) -> (k j) p", p=P))
            rows(rowsA, SCW, ssd_conv_w[0].rearrange("k (j p) -> (k j) p", p=P))
            for at, w in ((SCB, ssd_conv_b), (LCB, lru_conv_b), (BA, lru_ba)):
                rows(rowsA, at, w[0].rearrange("(j p) -> j p", p=P))
            for at, w in ((BX, lru_bx), (LAM, lru_lambda), (SNORM, ssd_norm), (NMIX, norm_mix), (NX, norm_xattn),
                          (NMEM, norm_mem), (NMOE, norm_moe)):
                rows(rowsB, at - P, w[0].rearrange("(j p) -> j p", p=P))

            XR = 3 * D + HEADS
            for c in range(DENSE_RING):
                fill(c, w_in_v[:, :, XR + c * CHUNK_COLS:XR + (c + 1) * CHUNK_COLS])
            for c in range(DENSE_RING):
                sp_.wait_ge(chunk_used, c + 1)
                fill(c, w_in_v[:, :, XR + D + c * CHUNK_COLS:XR + D + (c + 1) * CHUNK_COLS])
            with sp_.Fori(0, 3) as g:
                for c in range(DENSE_RING):
                    sp_.wait_ge(chunk_used, g * DENSE_RING + (DENSE_RING + c + 1))
                    fill(c, w_in_v[:, :, bass.ds(g * D + c * CHUNK_COLS, CHUNK_COLS)])
            rest_of_dense = ([w_kv_v[:, :, n * CHUNK_COLS:(n + 1) * CHUNK_COLS] for n in range(KV_CHUNKS)]
                             + [w_out_v[half, :, :, n * CHUNK_COLS:(n + 1) * CHUNK_COLS]
                                for half in (1, 0) for n in range(4)]
                             + [w_q_v[:, :, n * CHUNK_COLS:(n + 1) * CHUNK_COLS] for n in range(Q_CHUNKS)]
                             + [w_o_v[:, :, n * CHUNK_COLS:(n + 1) * CHUNK_COLS] for n in range(O_CHUNKS)])
            for c, src in enumerate(rest_of_dense, KV0):
                sp_.wait_ge(chunk_used, c - (DENSE_RING - 1))
                fill(c % DENSE_RING, src)

            def expert_chunk(experts, n):
                if n < 2 * UP_CHUNKS:
                    e, c = experts[n // UP_CHUNKS], n % UP_CHUNKS
                    dst = ring[:, slot_of(n), :]
                    src = up_v[bass.ds(e, 1), c].rearrange("e p n -> p (e n)")
                else:
                    e, c = experts[n % 2], (n - 2 * UP_CHUNKS) // 2
                    dst = ring[:, slot_of(n), :].rearrange("p (k n) -> p k n", k=2)
                    src = down_v[bass.ds(e, 1), c].rearrange("e p k n -> p (e k) n")
                sp_.dma_start(dst, src).then_inc(ring_landed[slot_of(n)], 16)

            def bias_chunk(experts):
                for b, e in enumerate(experts):
                    row = bias_rows[32 * b:32 * b + 1, :]
                    sp_.dma_start(row[:, 0:2 * D], b_gate_up[0, bass.ds(e, 1), :]).then_inc(bias_landed[b], 16)
                    sp_.dma_start(row[:, 2 * D:3 * D], b_down[0, bass.ds(e, 1), :]).then_inc(bias_landed[b], 16)

            sp_.wait_ge(chunk_used, OUT0 + 4)
            for n in range(DENSE_RING, RING):
                expert_chunk((0, 1), n)
            for n in range(DENSE_RING):
                sp_.wait_ge(chunk_used, DENSE - DENSE_RING + 1 + n)
                expert_chunk((0, 1), n)
            bias_chunk((0, 1))
            for n in range(RING, PAIR_CHUNKS):
                used(sp_, 0, n - RING)
                expert_chunk((0, 1), n)

            def refill(p, experts):
                for n in range(PAIR_CHUNKS):
                    used(sp_, p - 1, n + RING) if n < RING else used(sp_, p, n - RING)
                    expert_chunk(experts, n)
                    if n == 0:
                        sp_.wait_ge(bias_used, p)
                        bias_chunk(experts)

            with sp_.Fori(1, PAIRS) as p:
                refill(p, (p * 2, p * 2 + 1))
            sp_.wait_ge(tables_made, 1)
            spills = sp_.value_load(spill_int[0:1, SPILLS:SPILLS + 1], min_val=0, max_val=SPILLS // 2)
            with sp_.If(spills > 0):
                with sp_.Fori(0, spills) as j:
                    refill(j + PAIRS, [sp_.value_load(spill_int[0:1, bass.ds(j * 2 + b, 1)], min_val=0,
                                                      max_val=EXPERTS - 1) for b in range(2)])
            out_v = out[0].rearrange("(t p) d -> p t d", p=P)
            for t in range(T):
                sp_.wait_ge(out_made, t + 1)
                sp_.dma_start(out_v[:, t, :], xn[:, t, :]).then_inc(stored, 16)
            sp_.wait_ge(stored, 16 * T)

        @block.gpsimd
        def _(pool):
            pool.memset(ident[:, :], 0.0).then_inc(consts_made, 1)
            pool.memset(mask3[:, :], 1.0).then_inc(consts_made, 1)
            pool.memset(before[:, :], 1.0).then_inc(consts_made, 1)
            pool.memset(bd, 0.0).then_inc(consts_made, 1)
            pool.memset(spare[:, 0:1], 1.0).then_inc(consts_made, 1)
            pool.wait_ge(consts_made, 5)
            pool.affine_select(out=ident[:, :], in_=ident[:, :], compare_op=ALU.not_equal, fill=1.0, base=0,
                               pattern=[[-1, P]], channel_multiplier=1).then_inc(consts_made, 1)
            for n in (0, 2):
                m = mask3[:, n * P:(n + 1) * P]
                pool.affine_select(out=m, in_=m, compare_op=ALU.is_ge, fill=0.0, base=0, pattern=[[1, P]],
                                   channel_multiplier=-1).then_inc(consts_made, 1)
            pool.affine_select(out=before[:, :], in_=before[:, :], compare_op=ALU.is_ge, fill=0.0, base=-1,
                               pattern=[[1, P]], channel_multiplier=-1).then_inc(consts_made, 1)
            pool.iota(slot_id[:, :], pattern=[[0, 2], [1, SLOTS]], base=0, channel_multiplier=0,
                      allow_small_or_imprecise_dtypes=True).then_inc(consts_made, 1)
            pool.iota(spill_id[:, :], pattern=[[1, SPILLS]], base=0, channel_multiplier=0,
                      allow_small_or_imprecise_dtypes=True).then_inc(consts_made, 1)
            pool.iota(spill_base[:, :], pattern=[[SLOTS, SPILLS]], base=SLOTS, channel_multiplier=0,
                      allow_small_or_imprecise_dtypes=True).then_inc(consts_made, 1)
            pool.iota(part_id[:, :], pattern=[[0, 1]], base=0, channel_multiplier=1,
                      allow_small_or_imprecise_dtypes=True).then_inc(consts_made, 1)
            pool.memset(xpad[:, :, :, 0:3], 0.0).then_inc(padded, 1)
            for w, src in enumerate((lru_wa, lru_wx)):
                blocks = src[0].rearrange("(j b) i o -> b i j o", b=2)
                for b in range(2):
                    pool.dma_start(bd[64 * b:64 * b + 64, w, :, 64 * b:64 * b + 64], blocks[b]).then_inc(gates_landed, 16)
            pool.dma_start(gain_row[:, :], norm_final.rearrange("(a d) -> a d", a=1).broadcast_to([P, D]))\
                .then_inc(router_landed, 16)
            pool.wait_ge(chunk_used, OUT0 + OUT_CHUNKS)
            pool.dma_start(wr, w_router[0].rearrange("(k p) e -> p k e", p=P)).then_inc(router_landed, 16)
            pool.dma_start(br, b_router[0:1, :].broadcast_to([P, EXPERTS])).then_inc(router_landed, 16)

        CONSTS = 13

        def norm_stage(n):
            if n == 1:
                return mem_sb, junk.rearrange("p (t d) -> p t d", t=T), mem_sb
            return h, xn, xn

        NORM_GAIN = {0: NMIX, 1: NMEM, 2: NX, 3: NMOE}

        def norm_T(n):
            return mnT if n == 1 else xT

        @block.scalar
        def _(act):
            h_v = x[0].rearrange("(t p) d -> p t d", p=P)
            act.dma_start(h[:, :, :], h_v).then_inc(x_landed, 16)
            act.dma_start(w_dt[:, :, :], w_in_v[:, :, 3 * D:3 * D + HEADS]).then_inc(heads_landed, 16)
            for n, w in enumerate((ssd_dt_bias, ssd_a_log, ssd_d)):
                act.dma_start(heads_bc[:, n, :], w[0:1, :].broadcast_to([P, HEADS])).then_inc(heads_landed, 16)
            act.dma_start(mem_sb, mem[0].rearrange("(t p) d -> p t d", p=P)).then_inc(mem_landed, 16)

            preloads = [0]

            def preload(func):
                preloads[0] += 1
                act.activation(spare[:, preloads[0]:preloads[0] + 1], spare[:, 0:1], func)

            def norm(n):
                src, sq, dst = norm_stage(n)
                preload(ACT.Sqrt)
                for half in range(2):
                    if n >= 2:
                        act.wait_ge(h_added, 4 * (n - 2) + 2 * half + 1)
                    at = slice(half * BANK, (half + 1) * BANK)
                    act.activation(sq[:, 0, at], src[:, 0, at], ACT.Square, accum_out=stats[:, n, half, 0:1])\
                        .then_inc(squared["act"], 1)
                act.wait_ge(mean_made, n + 1)
                act.activation(stats[:, n, 4, :], stats[:, n, 3, :], ACT.Sqrt).then_inc(root_made, 1)
                act.wait_ge(rstd_made, n + 1)
                act.activation(dst[:, 0, :], src[:, 0, :], ACT.Copy, scale=stats[:, n, 5, 0:1])\
                    .then_inc(normed["act"], 1)

            def norm_turned(n):
                for b in (1, 3):
                    wait_misc_filled(act, f"norm{n}_{b}")
                    bank = misc_bank(f"norm{n}_{b}")
                    for j in range(2):
                        k = 2 * b + j
                        last = act.activation(norm_T(n)[:, k, :], bank[:, j * S:(j + 1) * S], ACT.Copy,
                                              scale=par[:, NORM_GAIN[n] + k:NORM_GAIN[n] + k + 1])
                    last.then_inc(misc_freed["act"], 1)

            def bank_of(c):
                return wide[:, c % DENSE_RING, :].rearrange("p (j s) -> p j s", j=2)

            act.wait_ge(consts_made, 5)
            act.wait_ge(x_landed, 16)
            norm(0)
            act.wait_ge(misc_freed["dve"], 1)
            norm_turned(0)
            act.wait_ge(sp_step, 1)
            act.activation(sp[:, 2, :], sp[:, 1, :], ACT.Exp).then_inc(sp_act, 1)
            act.wait_ge(heads_landed, 64)
            act.activation(expA[:, :], heads_bc[:, 1, :], ACT.Exp).then_inc(sp_act, 1)
            act.wait_ge(sp_step, 2)
            act.activation(sp[:, 4, :], sp[:, 3, :], ACT.Ln).then_inc(sp_act, 1)
            act.wait_ge(mem_landed, 16)
            norm(1)

            def pad_copy(c, n):
                act.wait_ge(chunk_used, c + 1)
                if n >= 2:
                    act.wait_ge(convolved, n - 1)
                act.activation(xpad[:, n % 2, :, 3:3 + S], bank_of(c), ACT.Copy).then_inc(pad_filled, 1)

            act.wait_ge(padded, 1)
            for c in range(4):
                pad_copy(c, c)
            for c in range(4, 8):
                act.wait_ge(chunk_used, c + 1)
                j = 2 * (c - 4)
                act.activation(gg[:, j:j + 2, :], bank_of(c), ACT.Gelu_apprx_tanh).then_inc(wide_freed, 1)
            norm_turned(1)
            for j in range(KT):
                wait_misc_filled(act, f"lru{j}")
                bank = misc_bank(f"lru{j}")
                act.activation(rb[:, j, :], bank[:, 0:S], ACT.Sigmoid, bias=par[:, BA + j:BA + j + 1])
                act.activation(ib[:, j, :], bank[:, S:2 * S], ACT.Sigmoid, bias=par[:, BX + j:BX + j + 1])\
                    .then_inc(misc_freed["act"], 1)
            act.wait_ge(rate_made, 1)
            act.wait_ge(misc_freed["act"], 4 + KT)
            for j in range(KT):
                act.activation(ab[:, j, :], rb[:, j, :], ACT.Exp, scale=lru_rate[:, j:j + 1])
                last = act.activation(rb[:, j, :], rb[:, j, :], ACT.Tanh, scale=lru_rate[:, j:j + 1])
            last.then_inc(decay_made, 1)
            act.wait_ge(lru_poly, 1)
            act.activation(rb, rb, ACT.Sqrt, scale=-1.0).then_inc(lru_root, 1)

            for c in range(8, 12):
                act.wait_ge(chunk_used, c + 1)
                j = 2 * (c - 8)
                act.activation(zs[:, j:j + 2, :], bank_of(c), ACT.Silu).then_inc(wide_freed, 1)

            def silu(n):
                act.wait_ge(convolved, 4 + n + 1)
                act.activation(xbc[:, 2 * n:2 * n + 2, :], xbc[:, 2 * n:2 * n + 2, :], ACT.Silu).then_inc(silu_made, 1)

            for c in range(12, 20):
                pad_copy(c, c - 8)
                if c > 12:
                    silu(c - 13)
            silu(7)
            act.wait_ge(seg_made, 1 + 1)
            act.activation(mt[:, 0, :, :], mt[:, 0, :, :], ACT.Exp).then_inc(seg_exp, 1)

            for q in range(KV_CHUNKS):
                act.wait_ge(chunk_used, KV0 + q + 1)
                dst = kT[:, 2 * q:2 * q + 2, :] if q < 4 else v[:, :, (q - 4) * CHUNK_COLS:(q - 3) * CHUNK_COLS]
                act.activation(dst, bank_of(KV0 + q), ACT.Copy).then_inc(wide_freed, 1)
                if q + 1 < 8:
                    act.wait_ge(seg_made, q + 3)
                    act.activation(mt[:, (q + 1) % 2, :, :], mt[:, (q + 1) % 2, :, :], ACT.Exp).then_inc(seg_exp, 1)
            preload(ACT.Sqrt)
            act.wait_ge(power_made, 1)
            act.activation(group_scale, group_scale, ACT.Sqrt).then_inc(ssd_root, 1)

            norm(2)
            preload(ACT.Exp)
            norm_turned(2)

            def q_copy(c):
                act.wait_ge(chunk_used, Q0 + c + 1)
                act.activation(qT[:, 2 * c:2 * c + 2, :], bank_of(Q0 + c), ACT.Copy).then_inc(wide_freed, 1)

            def prob_exps(hd):
                act.wait_ge(score_max, hd + 1)
                bank = misc_bank(f"score{hd}")
                for t in range(T):
                    last = act.activation(prob[:, hd, t, :], bank[:, t * S:(t + 1) * S], ACT.Exp,
                                          bias=soft[:, hd, 1, t:t + 1], scale=X_SCALE,
                                          accum_out=soft[:, hd, 2, t:t + 1])
                last.then_inc(misc_freed["act"], 1)

            def copy_out(name, dst):
                wait_misc_filled(act, name)
                act.activation(dst, misc_bank(name).rearrange("p (j s) -> p j s", j=2), ACT.Copy)\
                    .then_inc(misc_freed["act"], 1)

            q_copy(0)
            q_copy(1)
            prob_exps(0)
            q_copy(2)
            prob_exps(1)
            copy_out("probT0", probT[:, 0, :, :])
            q_copy(3)
            prob_exps(2)
            copy_out("probT1", probT[:, 1, :, :])
            copy_out("o0", oT[:, 0:2, :])
            prob_exps(3)
            copy_out("probT2", probT[:, 2, :, :])
            copy_out("o1", oT[:, 2:4, :])
            copy_out("probT3", probT[:, 3, :, :])
            copy_out("o2", oT[:, 4:6, :])
            copy_out("o3", oT[:, 6:8, :])

            norm(3)
            preload(ACT.Exp)
            norm_turned(3)
            for t in range(T):
                act.wait_ge(logits_made, t + 1)
                act.activation(rest[:, t, :], lg[:, t, :], ACT.Exp, bias=top_neg[:, t:t + 1]).then_inc(gate_exp, 1)
            preload(ACT.Sigmoid)

            def experts(p):
                act.wait_ge(g_made, p * 2 + 1)
                act.activation(sig, g_sb, ACT.Sigmoid, scale=ALPHA).then_inc(sig_made, 1)
                act.wait_ge(act_turned, p * 2 + 1)
                act.activation(actT[:, 0, :, :].rearrange("p j c -> p (j c)"), pair_ps[0][:, 0:BANK], ACT.Copy)\
                    .then_inc(actT_made, 1)
                act.wait_ge(put_turned, p + 1)
                act.activation(put, pair_ps[0][:, BANK:BANK + S], ACT.Copy).then_inc(put_made, 1)
                act.wait_ge(g_made, p * 2 + 2)
                act.activation(sig, g_sb, ACT.Sigmoid, scale=ALPHA).then_inc(sig_made, 1)
                act.wait_ge(act_turned, p * 2 + 2)
                act.activation(actT[:, 1, :, :].rearrange("p j c -> p (j c)"), pair_ps[0][:, 0:BANK], ACT.Copy)\
                    .then_inc(actT_made, 1)
                used(act, p, PAIR_CHUNKS - 1)
                act.activation(y_sb[:, 0:BANK], pair_ps[0][:, 0:BANK], ACT.Copy).then_inc(y_made["act"], 1)

            experts(0)
            with act.Fori(1, PAIRS) as p:
                experts(p)
            act.wait_ge(tables_made, 1)
            spills = act.value_load(spill_int[0:1, SPILLS:SPILLS + 1], min_val=0, max_val=SPILLS // 2)
            with act.If(spills > 0):
                with act.Fori(0, spills) as j:
                    experts(j + PAIRS)
            preload(ACT.Sqrt)
            for t in range(T):
                act.wait_ge(combined, spills + (PAIRS - 1 + t + 1))
                act.activation(xn[:, t, :], wide[:, 2 * t:2 * t + 2, :].rearrange("p b n -> p (b n)"), ACT.Square,
                               accum_out=stats[:, 4, 0, t:t + 1]).then_inc(squared["act"], 1)
            for t in range(T):
                act.wait_ge(mean_made, 4 + t + 1)
                act.activation(stats[:, 4, 4, t:t + 1], stats[:, 4, 3, t:t + 1], ACT.Sqrt).then_inc(root_made, 1)

        @block.tensor
        def _(pe):
            def norm_turn(n):
                dst = norm_stage(n)[2]
                pe.wait_ge(normed["act"], n + 1)
                pe.wait_ge(normed["dve"], n + 1)
                for b in range(4):
                    name = f"norm{n}_{b}"
                    wait_misc_free(pe, name)
                    for j in range(2):
                        k = 2 * b + j
                        for t in range(T):
                            last = pe.transpose(misc_bank(name)[:, j * S + t * P:j * S + (t + 1) * P],
                                                dst[:, t, k * P:(k + 1) * P], ident[:, :])
                    last.then_inc(misc_filled, 1)

            def project_T(slot, actT_):
                for j in range(2):
                    for k in range(KT):
                        last = pe.matmul(wide[:, slot, j * S:(j + 1) * S], slot_view(slot)[:, k, j * P:(j + 1) * P],
                                         actT_[:, k, :], start=(k == 0), stop=(k == KT - 1))
                last.then_inc(chunk_used, 1)

            def project_rows(c, src, n, first, last_pass):
                slot = c % DENSE_RING
                for t in range(T):
                    at = n % 2 * CHUNK_COLS
                    for k in range(KT):
                        last = pe.matmul(wide[:, 2 * t + n // 2, at:at + CHUNK_COLS], src[:, k, t * P:(t + 1) * P],
                                         slot_view(slot)[:, k, :], start=(first and n % 2 == 0 and k == 0),
                                         stop=(last_pass and k == KT - 1), skip_group_check=True)
                last.then_inc(chunk_used, 1)

            pe.wait_ge(consts_made, CONSTS)
            pe.wait_ge(params_landed, 16 * 12)
            bank = misc_bank("params")
            pe.transpose(bank[:, 0:P], rowsA[:, :], ident[:, :])
            pe.transpose(bank[:, P:PAR], rowsB[:, :], ident[0:PAR - P, 0:PAR - P]).then_inc(misc_filled, 1)
            norm_turn(0)
            wait_misc_free(pe, "dt")
            pe.wait_ge(heads_landed, 64)
            pe.wait_ge(misc_freed["dve"], 3)
            pe.wait_ge(misc_freed["act"], 2)
            for t in range(T):
                for k in range(KT):
                    last = pe.matmul(misc_bank("dt")[:, t * HEADS:(t + 1) * HEADS], xT[:, k, t * P:(t + 1) * P],
                                     w_dt[:, k, :], start=(k == 0), stop=(k == KT - 1))
            last.then_inc(misc_filled, 1)

            def in_chunk(g, s):
                pe.wait_ge(ring_landed[s], (g + 1) * 16)
                project_T(s, xT)

            for s in range(DENSE_RING):
                in_chunk(0, s)
            for s in range(DENSE_RING):
                pe.wait_ge(pad_filled, s + 1)
                in_chunk(1, s)
            wait_misc_free(pe, "cumsum")
            pe.wait_ge(dtA_made, 1)
            bank = misc_bank("cumsum")
            for t in range(T):
                pe.matmul(bank[:, t * HEADS:(t + 1) * HEADS], tri, dtA[:, t, :], start=True, stop=True)
            pe.matmul(bank[:, 2 * HEADS:3 * HEADS], ones, dtA[:, 0, :], start=True, stop=True).then_inc(misc_filled, 1)
            norm_turn(1)
            pe.wait_ge(gates_landed, 64)
            pe.wait_ge(convolved, 4)
            for j in range(KT):
                wait_misc_free(pe, f"lru{j}")
                bank = misc_bank(f"lru{j}")
                for w in range(2):
                    last = pe.matmul(bank[:, w * S:(w + 1) * S], bd[:, w, j, :], xr[:, j, :], start=True, stop=True)
                last.then_inc(misc_filled, 1)
            for s in range(DENSE_RING):
                pe.wait_ge(wide_freed, s + 1)
                in_chunk(2, s)
            for s in range(DENSE_RING):
                pe.wait_ge(wide_freed, 4 + s + 1)
                in_chunk(3, s)
            for s in range(DENSE_RING):
                pe.wait_ge(pad_filled, 4 + s + 1)
                in_chunk(4, s)

            pe.wait_ge(silu_made, 4)
            for t in range(T):
                for half in range(2):
                    name = f"xdt{2 * t + half}"
                    wait_misc_free(pe, name)
                    for j in range(4):
                        last = pe.transpose(misc_bank(name)[:, j * P:(j + 1) * P],
                                            xsT[:, 4 * half + j, t * P:(t + 1) * P], ident[:, :])
                    last.then_inc(misc_filled, 1)

            def decay_rows(q):
                name = f"rows{q}"
                wait_misc_free(pe, name)
                for hh in range(2):
                    for t in range(T):
                        at = hh * S + t * P
                        last = pe.matmul(misc_bank(name)[:, at:at + P],
                                         dtA[:, t, 2 * q + hh:2 * q + hh + 1].broadcast_to([P, P]), tri,
                                         start=True, stop=True)
                last.then_inc(misc_filled, 1)

            def ssd_heads(q):
                name = f"y{q}"
                wait_misc_free(pe, name)
                pe.wait_ge(mt_made, q + 1)
                bank = misc_bank(name)
                for t in range(T):
                    for hh in range(2):
                        at = (2 * q + hh) * HEAD_P
                        m = mt[:, q % 2, hh, 0:S] if t == 0 else mt[:, q % 2, hh, S:S + P]
                        last = pe.matmul(bank[HEAD_P * hh:HEAD_P * (hh + 1), t * P:S], xdt[:, t, at:at + HEAD_P], m,
                                         start=(t == 0), stop=(t == 1), skip_group_check=True)
                last.then_inc(misc_filled, 1)

            decay_rows(0)
            pe.wait_ge(silu_made, 8)
            for g in range(GROUPS):
                wait_misc_free(pe, f"cb{g}")
                bank = misc_bank(f"cb{g}")
                pe.matmul(bank[:, 0:S], bcT[:, g, 0:P], bcT[:, GROUPS + g, :], start=True, stop=True)
                pe.matmul(bank[:, S:S + P], bcT[:, g, P:S], bcT[:, GROUPS + g, P:S], start=True, stop=True)\
                    .then_inc(misc_filled, 1)
            for q in range(KV_CHUNKS):
                c = KV0 + q
                dense_landed(pe, c)
                if q < 4:
                    pe.wait_ge(pad_filled, 8 + q + 1)
                    project_T(c % DENSE_RING, mnT)
                else:
                    pe.wait_ge(wide_freed, 8 + q - 3)
                    for t in range(T):
                        for k in range(KT):
                            last = pe.matmul(wide[:, c % DENSE_RING, t * S:(t + 1) * S], mnT[:, k, t * P:(t + 1) * P],
                                             slot_view(c % DENSE_RING)[:, k, :], start=(k == 0), stop=(k == KT - 1))
                    last.then_inc(chunk_used, 1)
                if q < 7:
                    decay_rows(q + 1)
                ssd_heads(q)
            for n in range(2):
                name = f"power{n}"
                wait_misc_free(pe, name)
                pe.wait_ge(ssd_squares, 4 * (n + 1))
                for g in range(2):
                    for j in range(2):
                        last = pe.matmul(misc_bank(name)[:, g * S:(g + 1) * S], ones, xsT[:, 4 * n + 2 * g + j, :],
                                         start=(j == 0), stop=(j == 1))
                last.then_inc(misc_filled, 1)
            pe.wait_ge(wide_freed, 16)
            pe.wait_ge(lru_out, 1)
            for n in range(4):
                dense_landed(pe, OUT0 + n)
                project_rows(OUT0 + n, gg, n, True, False)
            pe.wait_ge(ssd_out, 1)
            for n in range(4):
                dense_landed(pe, OUT0 + 4 + n)
                project_rows(OUT0 + 4 + n, zs, n, False, True)
            norm_turn(2)

            def q_chunk(c):
                dense_landed(pe, Q0 + c)
                project_T(c, xT)

            def score(hd):
                name = f"score{hd}"
                wait_misc_free(pe, name)
                pe.wait_ge(wide_freed, 16 + hd + 1)
                for t in range(T):
                    for k in range(2):
                        last = pe.matmul(misc_bank(name)[:, t * S:(t + 1) * S], qT[:, 2 * hd + k, t * P:(t + 1) * P],
                                         kT[:, 2 * hd + k, :], start=(k == 0), stop=(k == 1))
                last.then_inc(misc_filled, 1)

            def prob_turn(hd):
                name = f"probT{hd}"
                wait_misc_free(pe, name)
                pe.wait_ge(prob_made, hd + 1)
                for m in range(T):
                    for t in range(T):
                        at = m * S + t * P
                        last = pe.transpose(misc_bank(name)[:, at:at + P], prob[:, hd, t, m * P:(m + 1) * P], ident[:, :])
                last.then_inc(misc_filled, 1)

            def attend(hd):
                name = f"o{hd}"
                wait_misc_free(pe, name)
                who = MISC_AT[f"probT{hd}"]
                pe.wait_ge(misc_freed["act"], sum(e == "act" for _, e in MISC_USES[:who + 1]))
                for d in range(2):
                    for m in range(T):
                        at = (2 * hd + d) * P
                        last = pe.matmul(misc_bank(name)[:, d * S:(d + 1) * S], v[:, m, at:at + P], probT[:, hd, m, :],
                                         start=(m == 0), stop=(m == 1))
                last.then_inc(misc_filled, 1)

            pe.wait_ge(h_added, 2 * T)
            pe.wait_ge(misc_freed["dve"], sum(e == "dve" for _, e in MISC_USES[:MISC_AT["norm2_3"] + 1]))
            pe.wait_ge(misc_freed["act"], sum(e == "act" for _, e in MISC_USES[:MISC_AT["norm2_3"] + 1]))
            q_chunk(0)
            q_chunk(1)
            score(0)
            q_chunk(2)
            score(1)
            prob_turn(0)
            q_chunk(3)
            score(2)
            prob_turn(1)
            attend(0)
            score(3)
            prob_turn(2)
            attend(1)
            prob_turn(3)
            attend(2)
            attend(3)
            pe.wait_ge(misc_freed["act"], sum(e == "act" for _, e in MISC_USES[:MISC_AT["o3"] + 1]))
            for n in range(4):
                dense_landed(pe, O0 + n)
                project_rows(O0 + n, oT, n, True, True)
            pe.wait_ge(h_added, 4 * T)
            for t in range(T):
                for half in range(2):
                    pe.matmul(wide[:, 2 * t + half, :], ident[:, :], h[:, t, half * BANK:(half + 1) * BANK], start=True,
                              stop=False, skip_group_check=True)
            norm_turn(3)

            pe.wait_ge(misc_freed["dve"], sum(e == "dve" for _, e in MISC_USES[:MISC_AT["norm3_3"] + 1]))
            pe.wait_ge(misc_freed["act"], sum(e == "act" for _, e in MISC_USES[:MISC_AT["norm3_3"] + 1]))
            pe.wait_ge(router_landed, 48)
            wait_misc_free(pe, "logits")
            for t in range(T):
                for k in range(KT):
                    last = pe.matmul(misc_bank("logits")[:, t * EXPERTS:(t + 1) * EXPERTS], xT[:, k, t * P:(t + 1) * P],
                                     wr[:, k, :], start=(k == 0), stop=(k == KT - 1))
            last.then_inc(misc_filled, 1)
            wait_misc_free(pe, "rank")
            pe.wait_ge(sel_made, T)
            bank = misc_bank("rank")
            pe.matmul(bank[:, 0:EXPERTS], before[:, :], sel[:, 0, :], start=True, stop=True)
            pe.matmul(bank[:, EXPERTS:2 * EXPERTS], ones, sel[:, 0, :], start=True, stop=False)
            pe.matmul(bank[:, EXPERTS:2 * EXPERTS], before[:, :], sel[:, 1, :], start=False, stop=True)
            for t in range(T):
                last = pe.matmul(bank[0:EXPERTS, 2 * EXPERTS:2 * EXPERTS + 1], sel[:, t, :], ones[:, 0:1],
                                 start=(t == 0), stop=(t == 1))
            last.then_inc(misc_filled, 1)

            def gather(p):
                pe.wait_ge(pick_made, p + 1)
                for k in range(KT):
                    for t in range(T):
                        last = pe.matmul(pair_ps[1][:, k * P:(k + 1) * P], xn[:, t, k * P:(k + 1) * P],
                                         pick[:, t, :], start=(t == 0), stop=(t == T - 1))
                last.then_inc(picked, 1)

            def combine(t):
                for half in range(2):
                    last = pe.matmul(wide[:, 2 * t + half, :], put[:, t * P:(t + 1) * P],
                                     y_sb[:, half * BANK:(half + 1) * BANK],
                                     start=False, stop=False, skip_group_check=True)
                return last

            def gate_up(p, b):
                ps = pair_ps[b]
                pe.wait_ge(bias_landed[b], p * 32 + 32)
                for n in range(2):
                    for half in range(2):
                        at = half * D + n * BANK
                        pe.matmul(ps[SLOTS * half:SLOTS * (half + 1), n * BANK:(n + 1) * BANK],
                                  ones[32 * b:32 * b + 1, 0:SLOTS], bias_rows[32 * b:32 * b + 1, at:at + BANK],
                                  start=True, stop=False, skip_group_check=True)
                for k in range(UP_CHUNKS):
                    chunk = UP_CHUNKS * b + k
                    pair_landed(pe, p, chunk)
                    for n in range(2):
                        for half in range(2):
                            at = half * D + n * BANK
                            last = pe.matmul(ps[SLOTS * half:SLOTS * (half + 1), n * BANK:(n + 1) * BANK],
                                             xsel[:, k, SLOTS * b:SLOTS * (b + 1)], ring[:, slot_of(chunk), at:at + BANK],
                                             start=False, stop=(k == UP_CHUNKS - 1), skip_group_check=True)
                    last.then_inc(chunk_used, 1)
                    if b == 1 and k == 1 and not (isinstance(p, int) and p == 0):
                        pe.wait_ge(y_made["act"], p)
                        pe.wait_ge(y_made["dve"], p)
                        pe.wait_ge(put_made, p)
                        for t in range(T):
                            last = combine(t)
                        last.then_inc(combined, 1)

            def turn_act(p, b):
                pe.wait_ge(act_made, p * 2 + b + 1)
                for j in range(4):
                    last = pe.transpose(pair_ps[0][:, j * P:(j + 1) * P], act_sb[:, b, j * P:(j + 1) * P], ident[:, :])
                last.then_inc(act_turned, 1)

            def experts(p):
                pe.wait_ge(xsel_made, p + 1)
                if not (isinstance(p, int) and p == 0):
                    pe.wait_ge(y_made["act"], p)
                    pe.wait_ge(y_made["dve"], p)
                gate_up(p, 0)
                gate_up(p, 1)
                pe.wait_ge(gu_freed, p * 2 + 1)
                turn_act(p, 0)
                pe.wait_ge(pick_gate_made, p + 1)
                for t in range(T):
                    last = pe.transpose(pair_ps[0][:, BANK + t * P:BANK + (t + 1) * P], pick_gate[:, t, :], ident[:, :])
                last.then_inc(put_turned, 1)
                pe.wait_ge(gu_freed, p * 2 + 2)
                gather(p + 1)
                pe.wait_ge(actT_made, p * 2 + 1)
                turn_act(p, 1)
                pe.wait_ge(actT_made, p * 2 + 2)
                pe.wait_ge(put_made, p + 1)
                for n in range(2):
                    for b in range(2):
                        at = 2 * D + n * BANK
                        last = pe.matmul(pair_ps[0][SLOTS * b:SLOTS * (b + 1), n * BANK:(n + 1) * BANK],
                                         ones[32 * b:32 * b + 1, 0:SLOTS], bias_rows[32 * b:32 * b + 1, at:at + BANK],
                                         start=True, stop=False, skip_group_check=True)
                last.then_inc(bias_used, 1)
                for c in range(DOWN_CHUNKS):
                    chunk = 2 * UP_CHUNKS + 2 * c
                    pair_landed(pe, p, chunk)
                    pair_landed(pe, p, chunk + 1)
                    for kk in range(2):
                        f = 2 * c + kk
                        for n in range(2):
                            for b in range(2):
                                at = kk * D + n * BANK
                                last = pe.matmul(pair_ps[0][SLOTS * b:SLOTS * (b + 1), n * BANK:(n + 1) * BANK],
                                                 actT[:, b, f % 4, SLOTS * (f // 4):SLOTS * (f // 4 + 1)],
                                                 ring[:, slot_of(chunk + b), at:at + BANK], start=False, stop=(f == 7),
                                                 skip_group_check=True)
                                if kk == 1 and n == 1:
                                    last.then_inc(chunk_used, 1)

            gather(0)
            experts(0)
            sums, turned = misc[:, 2, :], misc[:, 3, :]
            pe.wait_ge(spill_made, 1)
            pe.wait_ge(xsel_made, 2)
            pe.matmul(sums[0:EXPERTS, 0:1], before[0:EXPERTS, 0:EXPERTS], spill_cols[:, 4:5], start=True, stop=True)
            pe.matmul(sums[0:1, 1:2], spill_cols[:, 4:5], ones[0:EXPERTS, 0:1], start=True, stop=True)
            for t in range(T):
                pe.transpose(turned[0:EXPERTS, t * P:(t + 1) * P], rank_tab[:, t, 0:EXPERTS], ident[:, :])
                last = pe.transpose(turned[0:EXPERTS, S + t * P:S + (t + 1) * P], gate_tab[:, t, 0:EXPERTS], ident[:, :])
            last.then_inc(spill_filled, 1)
            pe.wait_ge(hot_made, 1)
            for w in range(2):
                for t in range(T):
                    at = (2 * w + t) * SPILLS
                    pe.matmul(sums[:, at:at + SPILLS], rgT[:, w, t * P:(t + 1) * P], one_hot[:, 1, :],
                              start=True, stop=True)
            pe.matmul(sums[0:1, 4 * SPILLS:5 * SPILLS], part_id[0:EXPERTS, :], one_hot[:, 1, :], start=True, stop=True)\
                .then_inc(spill_filled, 1)
            pe.wait_ge(tables_made, 1)
            with pe.Fori(1, PAIRS) as p:
                experts(p)
            spills = pe.value_load(spill_int[0:1, SPILLS:SPILLS + 1], min_val=0, max_val=SPILLS // 2)
            with pe.If(spills > 0):
                with pe.Fori(0, spills) as j:
                    experts(j + PAIRS)
            pe.wait_ge(y_made["act"], spills + PAIRS)
            pe.wait_ge(y_made["dve"], spills + PAIRS)
            pe.wait_ge(put_made, spills + PAIRS)
            for t in range(T):
                combine(t).then_inc(combined, 1)

        @block.vector
        def _(dve):
            steps = [0]

            def step(ins):
                steps[0] += 1
                ins.then_inc(dve_step, 1)
                dve.wait_ge(dve_step, steps[0])

            def norm(n):
                src, sq, dst = norm_stage(n)
                if n < 2:
                    square_half(n, 0)
                square_half(n, 1)
                dve.wait_ge(squared["dve"], 2 * n + 2)
                dve.wait_ge(squared["act"], 2 * n + 2)
                step(dve.tensor_tensor(stats[:, n, 2, :], stats[:, n, 0, :], stats[:, n, 1, :], ALU.add))
                dve.tensor_scalar(stats[:, n, 3, :], stats[:, n, 2, :], 1.0 / D, EPS, ALU.mult, ALU.add)\
                    .then_inc(mean_made, 1)
                dve.wait_ge(root_made, n + 1)
                dve.reciprocal(stats[:, n, 5, :], stats[:, n, 4, :]).then_inc(rstd_made, 1)
                dve.wait_ge(rstd_made, n + 1)
                dve.tensor_scalar(dst[:, 1, :], src[:, 1, :], stats[:, n, 5, 1:2], None, ALU.mult)\
                    .then_inc(normed["dve"], 1)

            def square_half(n, half):
                src, sq, dst = norm_stage(n)
                at = slice(half * BANK, (half + 1) * BANK)
                dve.tensor_tensor_reduce(sq[:, 1, at], src[:, 1, at], src[:, 1, at], 1.0, 0.0, ALU.mult, ALU.add,
                                         stats[:, n, half, 1:2]).then_inc(squared["dve"], 1)

            def norm_turned(n):
                for b in (0, 2):
                    wait_misc_filled(dve, f"norm{n}_{b}")
                    bank = misc_bank(f"norm{n}_{b}")
                    for j in range(2):
                        k = 2 * b + j
                        last = dve.tensor_scalar(norm_T(n)[:, k, :], bank[:, j * S:(j + 1) * S],
                                                 par[:, NORM_GAIN[n] + k:NORM_GAIN[n] + k + 1], None, ALU.mult)
                    last.then_inc(misc_freed["dve"], 1)

            def freed(ins):
                ins.then_inc(misc_freed["dve"], 1)

            dve.wait_ge(x_landed, 16)
            norm(0)
            wait_misc_filled(dve, "params")
            freed(dve.tensor_copy(par[:, :], misc_bank("params")[:, 0:PAR]))
            dve.wait_ge(misc_freed["dve"], 1)
            norm_turned(0)

            dve.wait_ge(heads_landed, 64)
            wait_misc_filled(dve, "dt")
            step(dve.tensor_scalar(sp[:, 0, 32:40], par[:, LAM:LAM + KT], -1.0, None, ALU.mult))
            for t in range(T):
                last = dve.tensor_tensor(sp[:, 0, t * HEADS:(t + 1) * HEADS], misc_bank("dt")[:, t * HEADS:(t + 1) * HEADS],
                                         heads_bc[:, 0, :], ALU.add)
            freed(last)
            dve.wait_ge(misc_freed["dve"], 4)
            dve.scalar_tensor_tensor(out=sp[:, 1, :], in0=sp[:, 0, :], scalar=-1.0, in1=sp[:, 0, :], op0=ALU.mult,
                                     op1=ALU.min).then_inc(sp_step, 1)
            dve.wait_ge(sp_act, 1)
            dve.tensor_scalar(sp[:, 3, :], sp[:, 2, :], 1.0, None, ALU.add).then_inc(sp_step, 1)
            dve.wait_ge(sp_step, 2)
            step(dve.tensor_scalar(sp[:, 5, :], sp[:, 3, :], -1.0, None, ALU.add))
            step(dve.tensor_scalar(sp[:, 6, :], sp[:, 5, :], 0.0, None, ALU.is_equal))
            step(dve.tensor_tensor(sp[:, 5, :], sp[:, 5, :], sp[:, 6, :], ALU.add))
            step(dve.reciprocal(sp[:, 7, :], sp[:, 5, :]))
            dve.wait_ge(sp_act, 3)
            step(dve.tensor_tensor(sp[:, 7, :], sp[:, 7, :], sp[:, 4, :], ALU.mult))
            step(dve.tensor_tensor(sp[:, 7, :], sp[:, 7, :], sp[:, 6, :], ALU.add))
            step(dve.tensor_tensor(sp[:, 7, :], sp[:, 7, :], sp[:, 2, :], ALU.mult))
            step(dve.scalar_tensor_tensor(out=sp[:, 5, :], in0=sp[:, 0, :], scalar=0.0, in1=sp[:, 7, :], op0=ALU.max,
                                          op1=ALU.add))
            dve.tensor_scalar(lru_rate[:, :], sp[:, 5, 32:40], -RG_C, None, ALU.mult).then_inc(rate_made, 1)
            for t in range(T):
                part = sp[:, 5, t * HEADS:(t + 1) * HEADS]
                dve.tensor_copy(dt[:, t, :], part)
                last = dve.scalar_tensor_tensor(out=dtA[:, t, :], in0=part, scalar=-1.0, in1=expA[:, :], op0=ALU.mult,
                                                op1=ALU.mult)
            last.then_inc(dtA_made, 1)
            pairs = heads_bc[:, 2, :].rearrange("p (j b) -> p b j", b=2)
            for b in range(2):
                step(dve.tensor_copy(d_col[64 * b:64 * b + 64, :], pairs[64 * b:64 * b + 64, b, :]))

            dve.wait_ge(mem_landed, 16)
            norm(1)

            def convolve(n, buf, dst, j, taps, tap_step, bias):
                dve.wait_ge(pad_filled, n + 1)
                for tap in range(4):
                    if tap:
                        dve.wait_ge(tap_done, n * 3 + tap)
                    for b in range(2):
                        o = dst[:, j + b, :]
                        src = xpad[:, buf, b, tap:tap + S]
                        col = taps + tap * tap_step + j + b
                        if tap == 0:
                            last = dve.tensor_scalar(o, src, par[:, col:col + 1], par[:, bias + j + b:bias + j + b + 1],
                                                     ALU.mult, ALU.add)
                        else:
                            last = dve.scalar_tensor_tensor(out=o, in0=src, scalar=par[:, col:col + 1], in1=o,
                                                            op0=ALU.mult, op1=ALU.add)
                    last.then_inc(convolved if tap == 3 else tap_done, 1)

            for n in range(4):
                convolve(n, n % 2, xr, 2 * n, LCW, 8, LCB)

            wait_misc_filled(dve, "cumsum")
            bank = misc_bank("cumsum")
            dve.tensor_copy(seg_bias[:, 1, :], bank[:, 2 * HEADS:3 * HEADS]).then_inc(dve_step, 1)
            steps[0] += 1
            dve.tensor_scalar(seg_bias[:, 0, :], bank[:, 0:HEADS], -1.0, None, ALU.mult)
            dve.tensor_scalar(seg_bias[:, 2, :], bank[:, HEADS:2 * HEADS], -1.0, None, ALU.mult).then_inc(misc_freed["dve"], 1)
            dve.wait_ge(misc_freed["dve"], 5)
            dve.tensor_tensor(seg_bias[:, 1, :], seg_bias[:, 1, :], seg_bias[:, 0, :], ALU.add).then_inc(seg_made, 1)
            dve.wait_ge(seg_made, 1)
            norm_turned(1)

            squares = xn[:, :, :].rearrange("p t (k s) -> p (t k) s", s=S)
            dve.wait_ge(decay_made, 1)
            dve.wait_ge(misc_filled, MISC_AT["norm0_3"] + 1)
            step(dve.tensor_tensor(squares, ab, ab, ALU.mult))
            dve.scalar_tensor_tensor(out=rb, in0=squares, scalar=1.0, in1=rb, op0=ALU.add, op1=ALU.mult)\
                .then_inc(lru_poly, 1)
            step(dve.tensor_tensor(ib, ib, xr, ALU.mult))
            dve.wait_ge(lru_root, 1)
            step(dve.tensor_tensor(ib, ib, rb, ALU.mult))
            for j in range(KT):
                last = dve.tensor_tensor_scan(rb[:, j, :], ab[:, j, :], ib[:, j, :], 0.0, ALU.mult, ALU.add)
            step(last)
            dve.tensor_tensor(gg, gg, rb, ALU.mult).then_inc(lru_out, 1)

            for n in range(8):
                convolve(4 + n, n % 2, xbc, 2 * n, SCW, 16, SCB)

            for t in range(T):
                for half in range(2):
                    name = f"xdt{2 * t + half}"
                    wait_misc_filled(dve, name)
                    freed(dve.tensor_tensor(
                        xdt[:, t, half * BANK:(half + 1) * BANK].rearrange("p (h c) -> p h c", c=HEAD_P),
                        misc_bank(name).rearrange("p (h c) -> p h c", c=HEAD_P),
                        dt[:, t, 8 * half:8 * half + 8].unsqueeze(2).broadcast_to([P, 8, HEAD_P]), ALU.mult))
            def exponents(q):
                name = f"rows{q}"
                wait_misc_filled(dve, name)
                if q >= 2:
                    wait_misc_filled(dve, f"y{q - 2}")
                bank = misc_bank(name)
                for hh in range(2):
                    for part in range(3):
                        at = hh * S + (P if part else 0)
                        hd = 2 * q + hh
                        last = dve.tensor_scalar(mt[:, q % 2, hh, part * P:(part + 1) * P], bank[:, at:at + P],
                                                 seg_bias[:, part, hd:hd + 1], 0.0, ALU.add, ALU.min)
                        if part == 2 and hh == 0:
                            last.then_inc(dve_step, 1)
                            steps[0] += 1
                last.then_inc(misc_freed["dve"], 1)

            def exponents_done(q):
                dve.wait_ge(misc_freed["dve"], sum(e == "dve" for _, e in MISC_USES[:MISC_AT[f"rows{q}"] + 1]))
                dve.tensor_copy(sp[:, 0, q:q + 1], seg_bias[:, 0, 0:1]).then_inc(seg_made, 1)

            exponents(0)
            exponents_done(0)
            for g in range(GROUPS):
                wait_misc_filled(dve, f"cb{g}")
                last = dve.tensor_tensor(cbm[:, g, :], misc_bank(f"cb{g}")[:, 0:3 * P], mask3[:, :], ALU.mult)
                freed(last)
            dve.wait_ge(misc_freed["dve"], sum(e == "dve" for _, e in MISC_USES[:MISC_AT["cb3"] + 1]))

            for q in range(8):
                dve.wait_ge(seg_exp, q + 1)
                m = mt[:, q % 2, :, :]
                dve.tensor_tensor(m, m, cbm[:, q // 2, :].unsqueeze(1).broadcast_to([P, 2, 3 * P]), ALU.mult)\
                    .then_inc(mt_made, 1)
                if q + 1 < 8:
                    exponents(q + 1)
                    exponents_done(q + 1)
                name = f"y{q}"
                wait_misc_filled(dve, name)
                xs = xsT[:, q, :]
                freed(dve.scalar_tensor_tensor(out=xs, in0=xs, scalar=d_col[:, q:q + 1], in1=misc_bank(name)[:, 0:S],
                                               op0=ALU.mult, op1=ALU.add))
                dve.wait_ge(misc_freed["dve"], sum(e == "dve" for _, e in MISC_USES[:MISC_AT[name] + 1]))
                step(dve.tensor_tensor(zs[:, q, :], zs[:, q, :], xs, ALU.mult))
                dve.tensor_tensor(xs, zs[:, q, :], zs[:, q, :], ALU.mult).then_inc(ssd_squares, 1)
            for n in range(2):
                name = f"power{n}"
                wait_misc_filled(dve, name)
                last = dve.tensor_scalar(group_scale[:, 2 * n:2 * n + 2, :],
                                         misc_bank(name).rearrange("p (g s) -> p g s", g=2), 1.0 / 256, EPS,
                                         ALU.mult, ALU.add)
                freed(last)
            dve.wait_ge(misc_freed["dve"], sum(e == "dve" for _, e in MISC_USES[:MISC_AT["power1"] + 1]))
            dve.tensor_copy(sp[:, 0, 0:1], seg_bias[:, 0, 0:1]).then_inc(power_made, 1)
            dve.wait_ge(ssd_root, 1)
            step(dve.reciprocal(group_scale, group_scale))
            for j in range(KT):
                last = dve.scalar_tensor_tensor(out=zs[:, j, :], in0=zs[:, j, :], scalar=par[:, SNORM + j:SNORM + j + 1],
                                                in1=group_scale[:, j // 2, :], op0=ALU.mult, op1=ALU.mult)
            last.then_inc(ssd_out, 1)

            def add_to_h(n, last_chunk):
                for half in range(2):
                    dve.wait_ge(chunk_used, last_chunk - 2 + 2 * half)
                    at = slice(half * BANK, (half + 1) * BANK)
                    for t in range(T):
                        dve.tensor_tensor(h[:, t, at], h[:, t, at], wide[:, 2 * t + half, :], ALU.add)\
                            .then_inc(h_added, 1)
                    dve.wait_ge(h_added, 4 * (n - 2) + 2 * half + 2)
                    if half == 0:
                        square_half(n, 0)

            add_to_h(2, Q0)
            norm(2)
            norm_turned(2)

            for hd in range(X_HEADS):
                name = f"score{hd}"
                wait_misc_filled(dve, name)
                step(dve.tensor_reduce(soft[:, hd, 0, :], misc_bank(name).rearrange("p (t m) -> p t m", t=T), AX_X, ALU.max))
                dve.tensor_scalar(soft[:, hd, 1, :], soft[:, hd, 0, :], -X_SCALE, None, ALU.mult).then_inc(score_max, 1)
                dve.wait_ge(misc_freed["act"], sum(e == "act" for _, e in MISC_USES[:MISC_AT[name] + 1]))
                step(dve.reciprocal(soft[:, hd, 3, :], soft[:, hd, 2, :]))
                for t in range(T):
                    last = dve.tensor_scalar(prob[:, hd, t, :], prob[:, hd, t, :], soft[:, hd, 3, t:t + 1], None, ALU.mult)
                last.then_inc(prob_made, 1)

            add_to_h(3, DENSE)
            norm(3)
            norm_turned(3)

            dve.wait_ge(router_landed, 48)
            wait_misc_filled(dve, "logits")
            for t in range(T):
                last = dve.tensor_tensor(lg[:, t, :], misc_bank("logits")[:, t * EXPERTS:(t + 1) * EXPERTS], br, ALU.add)
            freed(last)
            dve.wait_ge(misc_freed["dve"], sum(e == "dve" for _, e in MISC_USES[:MISC_AT["logits"] + 1]))
            for t in range(T):
                step(dve.max(top8[:, t, :], lg[:, t, :]))
            for t in range(T):
                dve.tensor_scalar(top_neg[:, t:t + 1], top8[:, t, 0:1], -1.0, None, ALU.mult).then_inc(logits_made, 1)
            step(dve.memset(top8[:, :, TOP_K:8], 3.0e38))
            for t in range(T):
                last = dve.match_replace(sel[:, t, :], top8[:, t, :], lg[:, t, :], -3.0e38)
            step(last)
            for t in range(T):
                dve.tensor_tensor(sel[:, t, :], sel[:, t, :], lg[:, t, :], ALU.not_equal).then_inc(sel_made, 1)
            dve.wait_ge(sel_made, T)
            for t in range(T):
                dve.wait_ge(gate_exp, t + 1)
                step(dve.tensor_tensor_reduce(rest[:, t, :], rest[:, t, :], sel[:, t, :], 1.0, 0.0, ALU.mult, ALU.add,
                                              gsum[:, 0, t:t + 1]))
            step(dve.reciprocal(gsum[:, 1, :], gsum[:, 0, :]))
            wait_misc_filled(dve, "rank")
            bank = misc_bank("rank")
            for t in range(T):
                step(dve.scalar_tensor_tensor(out=rank_tab[:, t, 0:EXPERTS], in0=sel[:, t, :], scalar=-4096.0,
                                              in1=bank[:, t * EXPERTS:(t + 1) * EXPERTS], op0=ALU.mult, op1=ALU.add))
            step(dve.tensor_scalar(rank_tab[:, :, 0:EXPERTS], rank_tab[:, :, 0:EXPERTS], 4096.0, None, ALU.add))
            freed(dve.tensor_copy(spill_cols[:, 0:1], bank[0:EXPERTS, 2 * EXPERTS:2 * EXPERTS + 1]))
            dve.wait_ge(misc_freed["dve"], sum(e == "dve" for _, e in MISC_USES[:MISC_AT["rank"] + 1]))
            for t in range(T):
                last = dve.tensor_scalar(gate_tab[:, t, 0:EXPERTS], rest[:, t, :], gsum[:, 1, t:t + 1], None, ALU.mult)
            step(last)

            def make_pick(p):
                for t in range(T):
                    for b in range(2):
                        at = slice(SLOTS * b, SLOTS * (b + 1))
                        last = dve.tensor_scalar(pick[:, t, at], slot_id[:, at], rank_tab[:, t, bass.ds(p * 2 + b, 1)],
                                                 None, ALU.is_equal)
                last.then_inc(pick_made, 1)

            def make_pick_gate(p):
                for t in range(T):
                    for b in range(2):
                        at = slice(SLOTS * b, SLOTS * (b + 1))
                        last = dve.tensor_scalar(pick_gate[:, t, at], slot_id[:, at],
                                                 rank_tab[:, t, bass.ds(p * 2 + b, 1)],
                                                 gate_tab[:, t, bass.ds(p * 2 + b, 1)], ALU.is_equal, ALU.mult)
                last.then_inc(pick_gate_made, 1)

            def take_xsel(p):
                dve.wait_ge(picked, p + 1)
                dve.tensor_tensor(xsel, pair_ps[1].rearrange("p (k c) -> p k c", k=KT),
                                  par[:, NMOE:NMOE + KT].unsqueeze(2).broadcast_to([P, KT, P]), ALU.mult)\
                    .then_inc(xsel_made, 1)

            def swiglu(p, b):
                used(dve, p, UP_CHUNKS * (b + 1) - 1)
                if b == 1:
                    dve.wait_ge(act_made, p * 2 + 1)
                halves = pair_ps[b].rearrange("p (f w) -> p w f", w=2)
                dve.tensor_scalar(g_sb, halves[:, 0, :], LIMIT, None, ALU.min).then_inc(g_made, 1)
                dve.tensor_scalar(u_sb, halves[:, 1, :], LIMIT, -LIMIT, ALU.min, ALU.max).then_inc(gu_freed, 1)
                dve.wait_ge(sig_made, p * 2 + b + 1)
                dve.tensor_tensor(g_sb, g_sb, sig, ALU.mult).then_inc(gated, 1)
                dve.wait_ge(gated, p * 2 + b + 1)
                dve.scalar_tensor_tensor(out=act_sb[:, b, :], in0=u_sb, scalar=1.0, in1=g_sb, op0=ALU.add, op1=ALU.mult)\
                    .then_inc(act_made, 1)

            def experts(p):
                make_pick(p + 1)
                swiglu(p, 0)
                swiglu(p, 1)
                take_xsel(p + 1)
                dve.wait_ge(put_turned, p + 1)
                make_pick_gate(p + 1)
                used(dve, p, PAIR_CHUNKS - 1)
                dve.tensor_copy(y_sb[:, BANK:2 * BANK], pair_ps[0][:, BANK:2 * BANK]).then_inc(y_made["dve"], 1)

            make_pick(0)
            make_pick_gate(0)
            take_xsel(0)
            for n in range(3):
                step(dve.tensor_scalar(spill_cols[:, 1 + n:2 + n], spill_cols[:, 0:1], float(SLOTS * (n + 1)), None,
                                       ALU.is_gt))
            dve.tensor_reduce(spill_cols[:, 4:5], spill_cols[:, 1:4], AX_X, ALU.add).then_inc(spill_made, 1)
            experts(0)

            sums, turned = misc[:, 2, :], misc[:, 3, :]
            dve.wait_ge(spill_made, 1)
            dve.wait_ge(spill_filled, 1)
            step(dve.tensor_copy(spill_cols[:, 5:6], sums[0:EXPERTS, 0:1]))
            dve.tensor_scalar(spill_int[:, SPILLS:SPILLS + 1], sums[0:1, 1:2], 0.5, 0.25, ALU.mult, ALU.add)
            step(dve.tensor_tensor(spill_cols[:, 6:7], spill_cols[:, 5:6], spill_cols[:, 4:5], ALU.add))
            step(dve.tensor_scalar(spill_cols[:, 7:8], spill_cols[:, 5:6], float(SLOTS), None, ALU.mult))
            step(dve.tensor_scalar(one_hot[:, 0, :], spill_id[0:EXPERTS, :], spill_cols[:, 5:6], None, ALU.is_ge))
            dve.scalar_tensor_tensor(out=one_hot[:, 1, :], in0=spill_id[0:EXPERTS, :], scalar=spill_cols[:, 6:7],
                                     in1=one_hot[:, 0, :], op0=ALU.is_lt, op1=ALU.mult)
            dve.tensor_scalar(rgT[:, 0, :], turned[0:EXPERTS, 0:S], spill_cols[:, 7:8], None, ALU.add)
            dve.tensor_copy(rgT[:, 1, :], turned[0:EXPERTS, S:2 * S]).then_inc(hot_made, 1)
            n0, n1 = EXPERTS, EXPERTS + SPILLS
            dve.memset(rank_tab[:, :, n1:n1 + 2], -1.0)
            dve.memset(gate_tab[:, :, n1:n1 + 2], 0.0)
            dve.wait_ge(spill_filled, 2)
            for t in range(T):
                dve.tensor_tensor(rank_tab[:, t, n0:n1], sums[:, t * SPILLS:(t + 1) * SPILLS], spill_base[:, :],
                                  ALU.subtract)
                dve.tensor_copy(gate_tab[:, t, n0:n1], sums[:, (2 + t) * SPILLS:(3 + t) * SPILLS])
            dve.tensor_copy(spill_int[:, 0:SPILLS], sums[0:1, 4 * SPILLS:5 * SPILLS]).then_inc(tables_made, 1)
            dve.wait_ge(tables_made, 1)

            with dve.Fori(1, PAIRS) as p:
                experts(p)
            spills = dve.value_load(spill_int[0:1, SPILLS:SPILLS + 1], min_val=0, max_val=SPILLS // 2)
            with dve.If(spills > 0):
                with dve.Fori(0, spills) as j:
                    experts(j + PAIRS)
            dve.wait_ge(router_landed, 48)
            for t in range(T):
                dve.wait_ge(squared["act"], 8 + t + 1)
                dve.tensor_scalar(stats[:, 4, 3, t:t + 1], stats[:, 4, 0, t:t + 1], 1.0 / D, EPS, ALU.mult, ALU.add)\
                    .then_inc(mean_made, 1)
                dve.wait_ge(root_made, 4 + t + 1)
                dve.reciprocal(stats[:, 4, 5, t:t + 1], stats[:, 4, 4, t:t + 1]).then_inc(rstd_made, 1)
                dve.wait_ge(rstd_made, 4 + t + 1)
                dve.scalar_tensor_tensor(out=xn[:, t, :], in0=wide[:, 2 * t:2 * t + 2, :].rearrange("p b n -> p (b n)"),
                                         scalar=stats[:, 4, 5, t:t + 1], in1=gain_row[:, :], op0=ALU.mult, op1=ALU.mult)\
                    .then_inc(out_made, 1)


_INS = ['x', 'mem', 'norm_mix', 'w_in', 'ssd_conv_w', 'ssd_conv_b', 'ssd_dt_bias', 'ssd_a_log', 'ssd_d', 'ssd_norm',
        'lru_conv_w', 'lru_conv_b', 'lru_wa', 'lru_ba', 'lru_wx', 'lru_bx', 'lru_lambda', 'w_out',
        'norm_xattn', 'norm_mem', 'w_q', 'w_kv', 'w_o', 'norm_moe', 'w_router', 'b_router',
        'w_gate_up', 'b_gate_up', 'w_down', 'b_down', 'norm_final']
_OUTS = [((1, 256, 1024), 'float32')]


def kernel(**inputs):
    import numpy as _np
    import concourse.bacc as _bacc
    from concourse import mybir as _mybir
    from concourse.bass_utils import run_bass_kernel_spmd as _run

    nc = _bacc.Bacc("TRN2", target_bir_lowering=False, num_devices=1)
    arrays, args = {}, []
    for name in _INS:
        a = _np.ascontiguousarray(inputs[name])
        arrays[f"in_{name}_dram"] = a
        args.append(nc.dram_tensor(f"in_{name}_dram", a.shape, _mybir.dt.from_np(a.dtype), kind="ExternalInput").ap())
    for i, (shape, dtype) in enumerate(_OUTS):
        dt = _mybir.dt.from_np(_np.dtype(dtype))
        args.append(nc.dram_tensor(f"out_{i}_dram", shape, dt, kind="ExternalOutput").ap())
    hybrid_trunk_kernel(nc, *args)
    r = _run(nc, [arrays], core_ids=[0])
    got = tuple(r.results[0][f"out_{i}_dram"] for i in range(len(_OUTS)))
    return got[0]
```

```python
from contextlib import ExitStack

import concourse.bass as bass
from concourse import mybir

F32 = mybir.dt.float32
F32R = mybir.dt.float32r
I32 = mybir.dt.int32
ALU = mybir.AluOpType
ACT = mybir.ActivationFunctionType
AX_X = mybir.AxisListType.X

P = 128
BANK = 512
D = 1024
S = 256
T = S // P
KT = D // P
EPS = 1e-6
HEADS = 16
HEAD_P = 64
GROUPS = 4
X_HEADS = 4
X_SCALE = float(D // X_HEADS) ** -0.5
RG_C = 8.0
EXPERTS = 32
TOP_K = 4
SLOTS = 64
PAIRS = EXPERTS // 2
SPILLS = 16
LIMIT = 7.0
ALPHA = 1.702

SLOT = 2048
RING = 12
CHUNK_COLS = SLOT // KT
DENSE_RING = 3
WIDE = 4
UNITS = 3
KH = KT // 2
IN_CHUNKS, KV_CHUNKS, OUT_CHUNKS, Q_CHUNKS, O_CHUNKS = 20, 8, 8, 4, 4
KV0 = IN_CHUNKS
OUT0 = KV0 + KV_CHUNKS
Q0 = OUT0 + OUT_CHUNKS
O0 = Q0 + Q_CHUNKS
DENSE = O0 + O_CHUNKS
UP_CHUNKS, DOWN_CHUNKS = 8, 4
PAIR_CHUNKS = 2 * (UP_CHUNKS + DOWN_CHUNKS)

LCW, SCW, SCB, LCB, BA = 0, 32, 96, 112, 120
BX, LAM, SNORM, NMIX, NX, NMEM, NMOE = 128, 136, 144, 152, 160, 168, 176
PAR = 184

MISC_USES = ([("params", "dve")]
             + [(f"norm0_{n}", "dve") for n in range(4)]
             + [("dtT", "dve"), ("dt", "dve"), ("cumsum", "dve")]
             + [(f"norm1_{n}", "dve") for n in range(4)]
             + [(f"lru{j}", "act") for j in range(8)]
             + [(f"xdt{n}", "dve") for n in range(4)]
             + [("rows0", "dve")]
             + [(f"cb{g}", "dve") for g in range(4)]
             + [x for q in range(8) for x in ([(f"rows{q + 1}", "dve")] if q < 7 else []) + [(f"y{q}", "dve")]]
             + [(f"power{n}", "dve") for n in range(2)]
             + [(f"norm2_{n}", "dve") for n in range(4)]
             + [(n, "dve" if n[0] == "o" else "act") for n in
                "score0 score1 probT0 score2 probT1 o0 score3 probT2 o1 probT3 o2 o3".split()]
             + [(f"norm3_{n}", "dve" if n % 2 == 0 else "act") for n in range(4)]
             + [("logits", "dve"), ("rank", "dve")])
MISC_AT = {name: n for n, (name, _) in enumerate(MISC_USES)}


def frees(who, name):
    return sum(e == who for _, e in MISC_USES[:MISC_AT[name] + 1])


def hybrid_trunk_kernel(nc, x, mem, norm_mix, w_in, ssd_conv_w, ssd_conv_b, ssd_dt_bias, ssd_a_log, ssd_d,
                        ssd_norm, lru_conv_w, lru_conv_b, lru_wa, lru_ba, lru_wx, lru_bx, lru_lambda, w_out,
                        norm_xattn, norm_mem, w_q, w_kv, w_o, norm_moe, w_router, b_router,
                        w_gate_up, b_gate_up, w_down, b_down, norm_final, out):
    with ExitStack() as ctx:
        def sb(name, shape, dt=F32):
            return ctx.enter_context(nc.sbuf_tensor(name, shape, dt))

        def sem(name):
            return ctx.enter_context(nc.semaphore(name))

        with ExitStack() as early:
            def split(name, shape):
                return early.enter_context(nc.sbuf_tensor(name, shape, F32R))

            early.enter_context(nc.sbuf_tensor("staging", [P, DENSE_RING, SLOT], F32))
            w_hi, w_lo = split("w_hi", [P, UNITS, KH, CHUNK_COLS]), split("w_lo", [P, UNITS, KH, CHUNK_COLS])
            mT_hi, mT_lo = split("mT_hi", [P, KT, S]), split("mT_lo", [P, KT, S])
            aT_hi, aT_lo = split("aT_hi", [P, KT, S]), split("aT_lo", [P, KT, S])
        ring = sb("ring", [P, RING, SLOT])
        h = sb("h", [P, T, D])
        xn = sb("xn", [P, T, D])
        xbc = sb("xbc", [P, 16, S])
        zs = sb("zs", [P, KT, S])
        kT = sb("kT", [P, KT, S])
        v = sb("v", [P, T, D])
        gain_row = sb("gain_row", [P, D])
        scratch = sb("scratch", [P, 6400])
        ident = sb("ident", [P, P])
        mask3 = sb("mask3", [P, 3 * P])
        before = sb("before", [P, P])
        slot_id = sb("slot_id", [P, P])
        spill_id = sb("spill_id", [P, SPILLS])
        spill_base = sb("spill_base", [P, SPILLS])
        part_id = sb("part_id", [P, 1])
        rowsA = sb("rowsA", [P, P])
        rowsB = sb("rowsB", [PAR - P, P])
        par = sb("par", [P, PAR])
        w_dt = sb("w_dt", [P, KT, HEADS])
        w_dt_hi, w_dt_lo = sb("w_dt_hi", [P, KT, HEADS], F32R), sb("w_dt_lo", [P, KT, HEADS], F32R)
        heads_bc = sb("heads_bc", [P, 3, HEADS])
        dtT = sb("dtT", [HEADS, S])
        d_col = sb("d_col", [P, KT])
        sp = sb("sp", [P, 8, 40])
        dt = sb("dt", [P, T, HEADS])
        dtA = sb("dtA", [P, T, HEADS])
        expA = sb("expA", [P, HEADS])
        lru_rate = sb("lru_rate", [P, KT])
        seg_bias = sb("seg_bias", [P, 3, HEADS])
        stats = sb("stats", [P, 5, 6, T])
        spare = sb("spare", [P, 16])
        soft = sb("soft", [P, X_HEADS, 4, T])
        lg = sb("lg", [P, T, EXPERTS])
        top8 = sb("top8", [P, T, 8])
        top_neg = sb("top_neg", [P, T])
        rest = sb("rest", [P, T, EXPERTS])
        sel = sb("sel", [P, T, EXPERTS])
        gsum = sb("gsum", [P, 2, T])
        rank_tab = sb("rank_tab", [P, T, EXPERTS + SPILLS + 2])
        gate_tab = sb("gate_tab", [P, T, EXPERTS + SPILLS + 2])
        spill_cols = sb("spill_cols", [EXPERTS, 8])
        one_hot = sb("one_hot", [EXPERTS, 2, SPILLS])
        rgT = sb("rgT", [EXPERTS, 2, S])
        spill_int = sb("spill_int", [1, SPILLS + 1], I32)

        tri = mask3[:, 0:P]
        ones = mask3[:, P:2 * P]

        def slot_view(n):
            return ring[:, n, :].rearrange("p (k s) -> p k s", k=KT)

        gg = slot_view(10)
        rb, ib = kT[:, :, :], v[:, :, :].rearrange("p t (k s) -> p (t k) s", s=S)
        xr, ab = xbc[:, 0:8, :], xbc[:, 8:16, :]
        xT = kT
        xdt = ring[:, 11, :].rearrange("p (t c) -> p t c", t=T)
        mem_sb = ring[:, 11, :].rearrange("p (t c) -> p t c", t=T)
        junk = zs[:, :, :].rearrange("p k s -> p (k s)")
        xsT, bcT = xbc[:, 0:8, :], xbc[:, 8:16, :]
        group_scale = xbc[:, 8:12, :]
        qT = xbc[:, 0:8, :]
        wr = junk[:, 0:KT * EXPERTS].rearrange("p (k e) -> p k e", k=KT)
        br = junk[:, KT * EXPERTS:(KT + 1) * EXPERTS]
        bd = scratch[:, 0:2048].rearrange("p (w j c) -> p w j c", w=2, j=KT)
        xpad = scratch[:, 2048:2048 + 4 * (S + 3)].rearrange("p (b j s) -> p b j s", b=2, j=2)
        cbm = scratch[:, 3088:3088 + 1536].rearrange("p (g l) -> p g l", g=GROUPS)
        mt = scratch[:, 4624:4624 + 1536].rearrange("p (b h l) -> p b h l", b=2, h=2)
        prob = scratch[:, 0:2048].rearrange("p (b t m) -> p b t m", b=4, t=T)
        probT = scratch[:, 2048:4096].rearrange("p (b t m) -> p b t m", b=4, t=T)
        pick = scratch[:, 0:256].rearrange("p (t c) -> p t c", t=T)
        pick_gate = scratch[:, 256:512].rearrange("p (t c) -> p t c", t=T)
        put = scratch[:, 512:768]
        xsel = scratch[:, 768:1792].rearrange("p (k c) -> p k c", k=KT)
        g_sb, sig, u_sb = (scratch[:, 1792 + 512 * n:2304 + 512 * n] for n in range(3))
        act_sb = scratch[:, 3328:4352].rearrange("p (b c) -> p b c", b=2)
        actT = scratch[:, 4352:5376].rearrange("p (b j c) -> p b j c", b=2, j=4)
        y_sb = scratch[:, 5376:6400]
        bias_up = kT[:, :, :].rearrange("p k s -> p (k s)")
        bias_down = junk[:, D:2 * D]
        extra = [v[:, :, :].rearrange("p t d -> p (t d)"), xbc[:, 0:8, :].rearrange("p k s -> p (k s)"),
                 xbc[:, 8:16, :].rearrange("p k s -> p (k s)"), h[:, :, :].rearrange("p t d -> p (t d)")]

        wide = ctx.enter_context(nc.psum_tensor("wide", [P, 4, BANK], F32))
        misc = ctx.enter_context(nc.psum_tensor("misc", [P, 4, BANK], F32))
        pair_ps = [misc[:, 2 * n:2 * n + 2, :].rearrange("p b n -> p (b n)") for n in range(2)]

        def misc_bank(name):
            return misc[:, MISC_AT[name] % 4, :]

        consts_made = sem("consts_made")
        x_landed, mem_landed = sem("x_landed"), sem("mem_landed")
        params_landed, heads_landed, gates_landed = sem("params_landed"), sem("heads_landed"), sem("gates_landed")
        router_landed, gain_landed = sem("router_landed"), sem("gain_landed")
        extra_landed = [sem(f"extra_landed{n}") for n in range(4)]
        ring_landed = [sem(f"ring_landed{n}") for n in range(RING)]
        bias_landed, bias_used = [sem(f"bias_landed{n}") for n in range(2)], sem("bias_used")
        chunk_used = sem("chunk_used")
        half_used = sem("half_used")
        hi_made, lo_made = sem("hi_made"), sem("lo_made")
        norm_hi, dt_hi, dt_lo = sem("norm_hi"), sem("dt_hi"), sem("dt_lo")
        lru_hi, lru_split, ssd_hi, ssd_split, o_hi = (
            sem(n) for n in ("lru_hi", "lru_split", "ssd_hi", "ssd_split", "o_hi"))
        misc_filled = sem("misc_filled")
        misc_freed = {"dve": sem("misc_freed_dve"), "act": sem("misc_freed_act")}
        squared = {"dve": sem("squared_dve"), "act": sem("squared_act")}
        mean_made, root_made, rstd_made = sem("mean_made"), sem("root_made"), sem("rstd_made")
        normed = {"dve": sem("normed_dve"), "act": sem("normed_act")}
        dve_step = sem("dve_step")
        sp_step, sp_act = sem("sp_step"), sem("sp_act")
        dtA_made, seg_made, rate_made = sem("dtA_made"), sem("seg_made"), sem("rate_made")
        padded, pad_filled, tap_done, convolved = sem("padded"), sem("pad_filled"), sem("tap_done"), sem("convolved")
        wide_freed = sem("wide_freed")
        silu_made = sem("silu_made")
        rate_applied = sem("rate_applied")
        decay_made, lru_poly, lru_root, lru_out = (sem(n) for n in ("decay_made", "lru_poly", "lru_root", "lru_out"))
        seg_exp, mt_made, power_made, ssd_root, ssd_out = (
            sem(n) for n in ("seg_exp", "mt_made", "power_made", "ssd_root", "ssd_out"))
        ssd_squares = sem("ssd_squares")
        h_added = sem("h_added")
        score_max, prob_exp, prob_made = sem("score_max"), sem("prob_exp"), sem("prob_made")
        logits_made, gate_exp, sel_made, spill_made, spill_filled, hot_made, tables_made = (
            sem(n) for n in ("logits_made", "gate_exp", "sel_made", "spill_made", "spill_filled", "hot_made",
                             "tables_made"))
        pick_made, pick_gate_made, picked, xsel_made = (
            sem(n) for n in ("pick_made", "pick_gate_made", "picked", "xsel_made"))
        g_made, sig_made, gu_freed, act_made = (sem(n) for n in ("g_made", "sig_made", "gu_freed", "act_made"))
        put_turned, put_made, act_turned, actT_made = (
            sem(n) for n in ("put_turned", "put_made", "act_turned", "actT_made"))
        y_made = {"dve": sem("y_made_dve"), "act": sem("y_made_act")}
        gated = sem("gated")
        combined = sem("combined")
        out_made, stored = sem("out_made"), sem("stored")

        def wait_misc_filled(eng, name):
            eng.wait_ge(misc_filled, MISC_AT[name] + 1)

        def wait_misc_free(pe, name):
            n = MISC_AT[name] - 4
            if n >= 0:
                name, who = MISC_USES[n]
                pe.wait_ge(misc_freed[who], frees(who, name))

        def slot_of(n):
            return n % RING

        def first(p):
            return isinstance(p, int) and p == 0

        def extra_of(p, n):
            at = {0: RING, 1: len(extra)}.get(p, PAIR_CHUNKS) if isinstance(p, int) else PAIR_CHUNKS
            return n - at if at <= n < at + len(extra) else None

        def weights(p, n):
            at = extra_of(p, n)
            return ring[:, slot_of(n), :] if at is None else extra[at]

        def pair_landed(pe, p, n):
            at = extra_of(p, n)
            if at is not None:
                pe.wait_ge(extra_landed[at], 16 * (p + 1))
                return
            slot = slot_of(n)
            fills = len(range(slot, DENSE, DENSE_RING)) if slot < DENSE_RING else 0
            if slot < 2 * len(extra) and not first(p):
                fills -= 1
            pe.wait_ge(ring_landed[slot], p * 32 + 16 * (fills + 1 + n // RING))

        def used(eng, p, n):
            eng.wait_ge(chunk_used, p * PAIR_CHUNKS + (DENSE + n + 1))

        w_in_v, w_kv_v, w_q_v, w_o_v = (w[0].rearrange("(k p) n -> p k n", p=P) for w in (w_in, w_kv, w_q, w_o))
        w_out_v = w_out[0].rearrange("(h k p) n -> h p k n", h=2, p=P)
        up_v = w_gate_up[0].rearrange("e (k p) n -> e k p n", p=P)
        down_v = w_down[0].rearrange("e (c k p) n -> e c p k n", k=2, p=P)

        block = ctx.enter_context(nc.Block())

        @block.sync
        def _(sp_):
            def fill(slot, src):
                sp_.dma_start(slot_view(slot), src).then_inc(ring_landed[slot], 16)

            def rows(dst, at, src):
                sp_.dma_start(dst[at:at + src.shape[0], :], src).then_inc(params_landed, 16)

            rows(rowsA, LCW, lru_conv_w[0].rearrange("k (j p) -> (k j) p", p=P))
            rows(rowsA, SCW, ssd_conv_w[0].rearrange("k (j p) -> (k j) p", p=P))
            for at, w in ((SCB, ssd_conv_b), (LCB, lru_conv_b), (BA, lru_ba)):
                rows(rowsA, at, w[0].rearrange("(j p) -> j p", p=P))
            for at, w in ((BX, lru_bx), (LAM, lru_lambda), (SNORM, ssd_norm), (NMIX, norm_mix), (NX, norm_xattn),
                          (NMEM, norm_mem), (NMOE, norm_moe)):
                rows(rowsB, at - P, w[0].rearrange("(j p) -> j p", p=P))

            XR = 3 * D + HEADS
            def staged(c):
                sp_.wait_ge(lo_made, 2 * c + (2 - 2 * DENSE_RING))

            for c in range(8):
                if c >= DENSE_RING:
                    staged(c)
                if c == 5:
                    sp_.dma_start(mem_sb, mem[0].rearrange("(t p) d -> p t d", p=P)).then_inc(mem_landed, 16)
                fill(c % DENSE_RING, w_in_v[:, :, XR + c * CHUNK_COLS:XR + (c + 1) * CHUNK_COLS])
            with sp_.Fori(0, 4) as g:
                for n in range(DENSE_RING):
                    staged(g * DENSE_RING + (8 + n))
                    fill((8 + n) % DENSE_RING, w_in_v[:, :, bass.ds(g * (DENSE_RING * CHUNK_COLS) + n * CHUNK_COLS,
                                                                    CHUNK_COLS)])
            rest_of_dense = ([w_kv_v[:, :, n * CHUNK_COLS:(n + 1) * CHUNK_COLS] for n in range(KV_CHUNKS)]
                             + [w_out_v[half, :, :, n * CHUNK_COLS:(n + 1) * CHUNK_COLS]
                                for half in (1, 0) for n in range(4)]
                             + [w_q_v[:, :, n * CHUNK_COLS:(n + 1) * CHUNK_COLS] for n in range(Q_CHUNKS)]
                             + [w_o_v[:, :, n * CHUNK_COLS:(n + 1) * CHUNK_COLS] for n in range(O_CHUNKS)])
            for c, src in enumerate(rest_of_dense, KV0):
                staged(c)
                fill(c % DENSE_RING, src)

            def expert_chunk(experts, n, dst, landed):
                if n < 2 * UP_CHUNKS:
                    e, c = experts[n // UP_CHUNKS], n % UP_CHUNKS
                    src = up_v[bass.ds(e, 1), c].rearrange("e p n -> p (e n)")
                else:
                    e, c = experts[n % 2], (n - 2 * UP_CHUNKS) // 2
                    dst = dst.rearrange("p (k n) -> p k n", k=2)
                    src = down_v[bass.ds(e, 1), c].rearrange("e p k n -> p (e k) n")
                sp_.dma_start(dst, src).then_inc(landed, 16)

            def ring_chunk(experts, n):
                expert_chunk(experts, n, ring[:, slot_of(n), :], ring_landed[slot_of(n)])

            def load_biases(experts):
                for b, e in enumerate(experts):
                    row = slice(32 * b, 32 * b + 1)
                    sp_.dma_start(bias_up[row, :], b_gate_up[0, bass.ds(e, 1), :]).then_inc(bias_landed[b], 16)
                    sp_.dma_start(bias_down[row, :], b_down[0, bass.ds(e, 1), :]).then_inc(bias_landed[b], 16)

            sp_.wait_ge(lru_split, 1)
            sp_.wait_ge(chunk_used, O0)
            for n in (10, 11, 8, 9):
                ring_chunk((0, 1), n)
            sp_.wait_ge(chunk_used, O0 + 1)
            for n in range(3):
                expert_chunk((0, 1), RING + n, extra[n], extra_landed[n])
            for n in range(DENSE_RING):
                staged(DENSE + n)
                ring_chunk((0, 1), (DENSE + n) % DENSE_RING)
            sp_.wait_ge(chunk_used, DENSE)
            for n in range(DENSE_RING, 8):
                ring_chunk((0, 1), n)
            sp_.wait_ge(misc_filled, MISC_AT["norm3_0"] + 1)
            expert_chunk((0, 1), RING + 3, extra[3], extra_landed[3])
            sp_.wait_ge(misc_filled, MISC_AT["logits"] + 1)
            load_biases((0, 1))
            for n in range(len(extra)):
                used(sp_, 0, n)
                ring_chunk((2, 3), n)
            for n in range(RING + len(extra), PAIR_CHUNKS):
                used(sp_, 0, n - RING)
                ring_chunk((0, 1), n)

            def refill(p, experts, start=0, biases_after=0):
                for n in range(start, PAIR_CHUNKS):
                    used(sp_, p - 1, n + RING) if n < RING else used(sp_, p, n - RING)
                    ring_chunk(experts, n)
                    if n == biases_after:
                        sp_.wait_ge(bias_used, p)
                        load_biases(experts)

            for n in range(len(extra)):
                used(sp_, 0, RING + n)
                expert_chunk((2, 3), len(extra) + n, extra[n], extra_landed[n])
            refill(1, (2, 3), 2 * len(extra), 2 * len(extra))
            refill(2, (4, 5), 0, 5)
            with sp_.Fori(3, PAIRS) as p:
                refill(p, (p * 2, p * 2 + 1))
            sp_.wait_ge(tables_made, 1)
            spills = sp_.value_load(spill_int[0:1, SPILLS:SPILLS + 1], min_val=0, max_val=SPILLS // 2)
            with sp_.If(spills > 0):
                with sp_.Fori(0, spills) as j:
                    refill(j + PAIRS, [sp_.value_load(spill_int[0:1, bass.ds(j * 2 + b, 1)], min_val=0,
                                                      max_val=EXPERTS - 1) for b in range(2)])
            out_v = out[0].rearrange("(t p) d -> p t d", p=P)
            for t in range(T):
                for half in range(2):
                    at = slice(half * BANK, (half + 1) * BANK)
                    sp_.wait_ge(out_made, 2 * t + half + 1)
                    sp_.dma_start(out_v[:, t, at], xn[:, t, at]).then_inc(stored, 16)
            sp_.wait_ge(stored, 16 * 2 * T)

        @block.gpsimd
        def _(pool):
            pool.memset(ident[:, :], 0.0).then_inc(consts_made, 1)
            pool.memset(mask3[:, :], 1.0).then_inc(consts_made, 1)
            pool.memset(before[:, :], 1.0).then_inc(consts_made, 1)
            pool.memset(bd, 0.0).then_inc(consts_made, 1)
            pool.memset(spare[:, 0:1], 1.0).then_inc(consts_made, 1)
            pool.wait_ge(consts_made, 5)
            pool.affine_select(out=ident[:, :], in_=ident[:, :], compare_op=ALU.not_equal, fill=1.0, base=0,
                               pattern=[[-1, P]], channel_multiplier=1).then_inc(consts_made, 1)
            for n in (0, 2):
                m = mask3[:, n * P:(n + 1) * P]
                pool.affine_select(out=m, in_=m, compare_op=ALU.is_ge, fill=0.0, base=0, pattern=[[1, P]],
                                   channel_multiplier=-1).then_inc(consts_made, 1)
            pool.affine_select(out=before[:, :], in_=before[:, :], compare_op=ALU.is_ge, fill=0.0, base=-1,
                               pattern=[[1, P]], channel_multiplier=-1).then_inc(consts_made, 1)
            pool.iota(slot_id[:, :], pattern=[[0, 2], [1, SLOTS]], base=0, channel_multiplier=0,
                      allow_small_or_imprecise_dtypes=True).then_inc(consts_made, 1)
            pool.iota(spill_id[:, :], pattern=[[1, SPILLS]], base=0, channel_multiplier=0,
                      allow_small_or_imprecise_dtypes=True).then_inc(consts_made, 1)
            pool.iota(spill_base[:, :], pattern=[[SLOTS, SPILLS]], base=SLOTS, channel_multiplier=0,
                      allow_small_or_imprecise_dtypes=True).then_inc(consts_made, 1)
            pool.iota(part_id[:, :], pattern=[[0, 1]], base=0, channel_multiplier=1,
                      allow_small_or_imprecise_dtypes=True).then_inc(consts_made, 1)
            pool.memset(xpad[:, :, :, 0:3], 0.0).then_inc(padded, 1)
            pool.wait_ge(ring_landed[0], 16)
            for w, src in enumerate((lru_wa, lru_wx)):
                blocks = src[0].rearrange("(j b) i o -> b i j o", b=2)
                for b in range(2):
                    pool.dma_start(bd[64 * b:64 * b + 64, w, :, 64 * b:64 * b + 64], blocks[b]).then_inc(gates_landed, 16)
            def make_lo(u, n):
                pool.wait_ge(hi_made, u + (n + 1))
                slot, half = n // 2, n % 2
                pool.tensor_tensor(w_lo[:, n % UNITS, :, :], slot_view(slot)[:, KH * half:KH * (half + 1), :],
                                   w_hi[:, n % UNITS, :, :], ALU.subtract).then_inc(lo_made, 1)

            ROUND = 2 * DENSE_RING
            with pool.Fori(0, 2 * DENSE // ROUND) as g:
                for n in range(ROUND):
                    make_lo(g * ROUND, n)
            for n in range(2 * DENSE % ROUND):
                make_lo(2 * DENSE // ROUND * ROUND, n)
            pool.wait_ge(ssd_split, 2)
            pool.dma_start(wr, w_router[0].rearrange("(k p) e -> p k e", p=P)).then_inc(router_landed, 16)
            pool.dma_start(br, b_router[0:1, :].broadcast_to([P, EXPERTS])).then_inc(router_landed, 16)
            pool.dma_start(gain_row[:, :], norm_final.rearrange("(a d) -> a d", a=1).broadcast_to([P, D]))\
                .then_inc(gain_landed, 16)

        CONSTS = 13

        def norm_stage(n):
            if n == 1:
                return mem_sb, junk.rearrange("p (t d) -> p t d", t=T), mem_sb
            return h, xn, xn

        NORM_GAIN = {0: NMIX, 1: NMEM, 2: NX, 3: NMOE}

        def split_T(n):
            return (mT_hi, mT_lo) if n == 1 else (aT_hi, aT_lo)

        @block.scalar
        def _(act):
            h_v = x[0].rearrange("(t p) d -> p t d", p=P)
            act.dma_start(h[:, :, :], h_v).then_inc(x_landed, 16)
            act.dma_start(w_dt[:, :, :], w_in_v[:, :, 3 * D:3 * D + HEADS]).then_inc(heads_landed, 16)
            for n, w in enumerate((ssd_dt_bias, ssd_a_log, ssd_d)):
                act.dma_start(heads_bc[:, n, :], w[0:1, :].broadcast_to([P, HEADS])).then_inc(heads_landed, 16)

            preloads = [0]

            def preload(func):
                preloads[0] += 1
                act.activation(spare[:, preloads[0]:preloads[0] + 1], spare[:, 0:1], func)

            def norm_squares(n):
                src, sq, dst = norm_stage(n)
                for half in range(2):
                    if n >= 2:
                        act.wait_ge(h_added, 4 * (n - 2) + 2 * half + 1)
                    at = slice(half * BANK, (half + 1) * BANK)
                    act.activation(sq[:, 0, at], src[:, 0, at], ACT.Square, accum_out=stats[:, n, half, 0:1])\
                        .then_inc(squared["act"], 1)

            def norm_scale(n):
                src, sq, dst = norm_stage(n)
                act.wait_ge(mean_made, n + 1)
                act.activation(stats[:, n, 4, :], stats[:, n, 3, :], ACT.Sqrt).then_inc(root_made, 1)
                act.wait_ge(rstd_made, n + 1)
                act.activation(dst[:, 0, :], src[:, 0, :], ACT.Copy, scale=stats[:, n, 5, 0:1])\
                    .then_inc(normed["act"], 1)

            def norm(n):
                preload(ACT.Sqrt)
                norm_squares(n)
                norm_scale(n)

            def norm_turned(n):
                for b in range(4):
                    wait_misc_filled(act, f"norm{n}_{b}")
                    bank = misc_bank(f"norm{n}_{b}")
                    for j in range(2):
                        k = 2 * b + j
                        last = act.activation(split_T(n)[0][:, k, :], bank[:, j * S:(j + 1) * S], ACT.Copy,
                                              scale=par[:, NORM_GAIN[n] + k:NORM_GAIN[n] + k + 1])
                    last.then_inc(norm_hi, 1)

            units = [0]

            def make_hi(end):
                for u in range(units[0], end):
                    c, half = u // 2, u % 2
                    old = u - UNITS
                    if old >= 0:
                        act.wait_ge(half_used if old % 2 == 0 else chunk_used, old // 2 + 1)
                    act.wait_ge(ring_landed[c % DENSE_RING], 16 * (c // DENSE_RING + 1))
                    act.activation(w_hi[:, u % UNITS, :, :],
                                   slot_view(c % DENSE_RING)[:, KH * half:KH * (half + 1), :], ACT.Copy)\
                        .then_inc(hi_made, 1)
                units[0] = max(units[0], end)

            def bank_of(c):
                return wide[:, c % WIDE, :].rearrange("p (j s) -> p j s", j=2)

            def leave(c, dst, func, done):
                make_hi(2 * c + 5)
                act.wait_ge(chunk_used, c + 1)
                act.activation(dst, bank_of(c), func).then_inc(done, 1)
                if c not in (7, 19):
                    make_hi(2 * c + 6)

            act.wait_ge(consts_made, 5)
            act.wait_ge(x_landed, 16)
            norm(0)
            act.wait_ge(misc_freed["dve"], 1)
            norm_turned(0)
            make_hi(2)
            act.wait_ge(heads_landed, 64)
            act.activation(w_dt_hi[:, :, :], w_dt[:, :, :], ACT.Copy).then_inc(dt_hi, 1)
            make_hi(UNITS + 1)
            def pad_copy(c, n):
                make_hi(2 * c + 5)
                if n >= 2:
                    act.wait_ge(convolved, n - 1)
                leave(c, xpad[:, n % 2, :, 3:3 + S], ACT.Copy, pad_filled)

            act.wait_ge(padded, 1)
            for c in range(4):
                pad_copy(c, c)
                if c == 0:
                    act.wait_ge(sp_step, 1)
                    act.activation(sp[:, 2, :], sp[:, 1, :], ACT.Exp).then_inc(sp_act, 1)
                    act.activation(expA[:, :], heads_bc[:, 1, :], ACT.Exp).then_inc(sp_act, 1)
                    act.wait_ge(sp_step, 2)
                    act.activation(sp[:, 4, :], sp[:, 3, :], ACT.Ln).then_inc(sp_act, 1)
            act.wait_ge(mem_landed, 16)
            norm_squares(1)
            for c in range(4, 8):
                if c == 5:
                    norm_scale(1)
                j = 2 * (c - 4)
                leave(c, gg[:, j:j + 2, :], ACT.Gelu_apprx_tanh, wide_freed)
            norm_turned(1)
            for j in range(KT):
                wait_misc_filled(act, f"lru{j}")
                bank = misc_bank(f"lru{j}")
                act.activation(rb[:, j, :], bank[:, 0:S], ACT.Sigmoid, bias=par[:, BA + j:BA + j + 1])
                act.activation(ib[:, j, :], bank[:, S:2 * S], ACT.Sigmoid, bias=par[:, BX + j:BX + j + 1])\
                    .then_inc(misc_freed["act"], 1)
            make_hi(2 * 8 + 5)
            act.wait_ge(rate_applied, 1)
            act.activation(ab, rb, ACT.Exp)
            make_hi(2 * 8 + 6)
            act.activation(rb, rb, ACT.Tanh).then_inc(decay_made, 1)
            for c in range(8, 12):
                if c == 9:
                    preload(ACT.Sqrt)
                    make_hi(2 * 9 + 6)
                    act.wait_ge(lru_poly, 1)
                    act.activation(rb, rb, ACT.Sqrt, scale=-1.0).then_inc(lru_root, 1)
                j = 2 * (c - 8)
                leave(c, zs[:, j:j + 2, :], ACT.Silu, wide_freed)

            def silu(n):
                act.wait_ge(convolved, 4 + n + 1)
                act.activation(xbc[:, 2 * n:2 * n + 2, :], xbc[:, 2 * n:2 * n + 2, :], ACT.Silu).then_inc(silu_made, 1)

            for c in range(12, 20):
                pad_copy(c, c - 8)
                if c > 12:
                    silu(c - 13)
            silu(7)
            make_hi(2 * 20 + 5)
            act.wait_ge(seg_made, 1 + 1)
            act.activation(mt[:, 0, :, :], mt[:, 0, :, :], ACT.Exp).then_inc(seg_exp, 1)

            for q in range(KV_CHUNKS):
                if q == 0:
                    act.wait_ge(lru_out, 1)
                    act.activation(aT_hi[:, :, :], gg, ACT.Copy).then_inc(lru_hi, 1)
                dst = kT[:, 2 * q:2 * q + 2, :] if q < 4 else v[:, :, (q - 4) * CHUNK_COLS:(q - 3) * CHUNK_COLS]
                leave(KV0 + q, dst, ACT.Copy, wide_freed)
                if q + 1 < 8:
                    act.wait_ge(seg_made, q + 3)
                    act.activation(mt[:, (q + 1) % 2, :, :], mt[:, (q + 1) % 2, :, :], ACT.Exp).then_inc(seg_exp, 1)
            preload(ACT.Sqrt)
            act.wait_ge(power_made, 1)
            act.activation(group_scale, group_scale, ACT.Sqrt).then_inc(ssd_root, 1)

            for half in range(2):
                make_hi(2 * OUT0 + 7 + half)
                at = slice(KH * half, KH * (half + 1))
                act.wait_ge(ssd_out, half + 1)
                act.activation(mT_hi[:, at, :], zs[:, at, :], ACT.Copy).then_inc(ssd_hi, 1)
            make_hi(2 * Q0 + 2)

            norm(2)
            norm_turned(2)
            make_hi(2 * Q0 + 4)
            preload(ACT.Exp)

            def q_copy(c):
                make_hi(2 * (Q0 + c) + 5)
                act.wait_ge(chunk_used, Q0 + c + 1)
                act.activation(qT[:, 2 * c:2 * c + 2, :], bank_of(Q0 + c), ACT.Copy).then_inc(wide_freed, 1)

            def prob_exps(hd):
                act.wait_ge(score_max, hd + 1)
                bank = misc_bank(f"score{hd}")
                for t in range(T):
                    last = act.activation(prob[:, hd, t, :], bank[:, t * S:(t + 1) * S], ACT.Exp,
                                          bias=soft[:, hd, 1, t:t + 1], scale=X_SCALE,
                                          accum_out=soft[:, hd, 2, t:t + 1])
                last.then_inc(misc_freed["act"], 1)

            def attended(hd):
                name = f"o{hd}"
                wait_misc_filled(act, name)
                act.activation(mT_hi[:, 2 * hd:2 * hd + 2, :], misc_bank(name).rearrange("p (j s) -> p j s", j=2),
                               ACT.Copy).then_inc(o_hi, 1)

            def copy_out(name, dst):
                wait_misc_filled(act, name)
                act.activation(dst, misc_bank(name).rearrange("p (j s) -> p j s", j=2), ACT.Copy)\
                    .then_inc(misc_freed["act"], 1)

            q_copy(0)
            make_hi(2 * Q0 + 6)
            q_copy(1)
            prob_exps(0)
            make_hi(2 * Q0 + 8)
            q_copy(2)
            prob_exps(1)
            copy_out("probT0", probT[:, 0, :, :])
            make_hi(2 * Q0 + 10)
            q_copy(3)
            prob_exps(2)
            copy_out("probT1", probT[:, 1, :, :])
            attended(0)
            prob_exps(3)
            copy_out("probT2", probT[:, 2, :, :])
            attended(1)
            copy_out("probT3", probT[:, 3, :, :])
            attended(2)
            attended(3)
            make_hi(2 * DENSE)

            norm(3)
            preload(ACT.Exp)
            for b in (1, 3):
                wait_misc_filled(act, f"norm3_{b}")
                bank = misc_bank(f"norm3_{b}")
                for j in range(2):
                    k = 2 * b + j
                    last = act.activation(xT[:, k, :], bank[:, j * S:(j + 1) * S], ACT.Copy,
                                          scale=par[:, NMOE + k:NMOE + k + 1])
                last.then_inc(misc_freed["act"], 1)
            for t in range(T):
                act.wait_ge(logits_made, t + 1)
                act.activation(rest[:, t, :], lg[:, t, :], ACT.Exp, bias=top_neg[:, t:t + 1]).then_inc(gate_exp, 1)
            preload(ACT.Sigmoid)

            def experts(p):
                act.wait_ge(g_made, p * 2 + 1)
                act.activation(sig, g_sb, ACT.Sigmoid, scale=ALPHA).then_inc(sig_made, 1)
                act.wait_ge(act_turned, p * 2 + 1)
                act.activation(actT[:, 0, :, :].rearrange("p j c -> p (j c)"), pair_ps[0][:, 0:BANK], ACT.Copy)\
                    .then_inc(actT_made, 1)
                act.wait_ge(put_turned, p + 1)
                act.activation(put, pair_ps[0][:, BANK:BANK + S], ACT.Copy).then_inc(put_made, 1)
                act.wait_ge(g_made, p * 2 + 2)
                act.activation(sig, g_sb, ACT.Sigmoid, scale=ALPHA).then_inc(sig_made, 1)
                act.wait_ge(act_turned, p * 2 + 2)
                act.activation(actT[:, 1, :, :].rearrange("p j c -> p (j c)"), pair_ps[0][:, 0:BANK], ACT.Copy)\
                    .then_inc(actT_made, 1)
                used(act, p, PAIR_CHUNKS - 1)
                act.activation(y_sb[:, 0:BANK], pair_ps[0][:, 0:BANK], ACT.Copy).then_inc(y_made["act"], 1)

            experts(0)
            with act.Fori(1, PAIRS) as p:
                experts(p)
            act.wait_ge(tables_made, 1)
            spills = act.value_load(spill_int[0:1, SPILLS:SPILLS + 1], min_val=0, max_val=SPILLS // 2)
            with act.If(spills > 0):
                with act.Fori(0, spills) as j:
                    experts(j + PAIRS)
            preload(ACT.Sqrt)
            for t in range(T):
                act.wait_ge(combined, spills + (PAIRS - 1 + t + 1))
                act.activation(xn[:, t, :], wide[:, 2 * t:2 * t + 2, :].rearrange("p b n -> p (b n)"), ACT.Square,
                               accum_out=stats[:, 4, 0, t:t + 1]).then_inc(squared["act"], 1)
                act.wait_ge(mean_made, 4 + t + 1)
                act.activation(stats[:, 4, 4, t:t + 1], stats[:, 4, 3, t:t + 1], ACT.Sqrt).then_inc(root_made, 1)

        @block.tensor
        def _(pe):
            def norm_turn(n):
                dst = norm_stage(n)[2]
                pe.wait_ge(normed["act"], n + 1)
                pe.wait_ge(normed["dve"], n + 1)
                for b in range(4):
                    name = f"norm{n}_{b}"
                    wait_misc_free(pe, name)
                    for j in range(2):
                        k = 2 * b + j
                        for t in range(T):
                            last = pe.transpose(misc_bank(name)[:, j * S + t * P:j * S + (t + 1) * P],
                                                dst[:, t, k * P:(k + 1) * P], ident[:, :])
                    last.then_inc(misc_filled, 1)

            def split_product(c, half, src, product, needs):
                u = 2 * c + half
                if needs:
                    pe.wait_ge(misc_freed["dve"], frees("dve", needs[half]))
                hi, lo = w_hi[:, u % UNITS, :, :], w_lo[:, u % UNITS, :, :]
                pe.wait_ge(hi_made, u + 1)
                for kk in range(KH):
                    for acts in src:
                        product(KH * half + kk, hi[:, kk, :], acts, acts is src[0], False)
                pe.wait_ge(lo_made, u + 1)
                for kk in range(KH):
                    last = product(KH * half + kk, lo[:, kk, :], src[0], False, True)
                last.then_inc(half_used if half == 0 else chunk_used, 1)

            def project_T(c, src, needs=None):
                def product(k, w, acts, first, last_pass):
                    for j in range(2):
                        last = pe.matmul(wide[:, c % WIDE, j * S:(j + 1) * S], w[:, j * P:(j + 1) * P], acts[:, k, :],
                                         start=(first and k == 0 and j == 0), stop=(last_pass and k == KT - 1),
                                         skip_group_check=True)
                    return last

                for half in range(2):
                    split_product(c, half, src, product, needs)

            def project_v(c, src):
                def product(k, w, acts, first, last_pass):
                    for t in range(T):
                        last = pe.matmul(wide[:, c % WIDE, t * S:(t + 1) * S], acts[:, k, t * P:(t + 1) * P], w,
                                         start=(first and k == 0 and t == 0), stop=(last_pass and k == KT - 1),
                                         skip_group_check=True)
                    return last

                for half in range(2):
                    split_product(c, half, src, product, None)

            def project_rows(c, src, n, first_half, last_half, needs=None):
                def product(k, w, acts, first, last_pass):
                    at = n % 2 * CHUNK_COLS
                    for t in range(T):
                        last = pe.matmul(wide[:, 2 * t + n // 2, at:at + CHUNK_COLS], acts[:, k, t * P:(t + 1) * P], w,
                                         start=(first_half and n % 2 == 0 and first and k == 0),
                                         stop=(last_half and last_pass and k == KT - 1), skip_group_check=True)
                    return last

                for half in range(2):
                    split_product(c, half, src, product, needs)

            x_T, mem_T = (aT_hi, aT_lo), (mT_hi, mT_lo)
            lru_T, ssd_T, o_T = (aT_hi, aT_lo), (mT_hi, mT_lo), (mT_hi, mT_lo)

            pe.wait_ge(consts_made, CONSTS)
            pe.wait_ge(params_landed, 16 * 12)
            bank = misc_bank("params")
            pe.transpose(bank[:, 0:P], rowsA[:, :], ident[:, :])
            pe.transpose(bank[:, P:PAR], rowsB[:, :], ident[0:PAR - P, 0:PAR - P]).then_inc(misc_filled, 1)
            norm_turn(0)
            def in_chunk(g, s):
                project_T(g * WIDE + s, x_T, ("norm0_1", "norm0_3") if g == 0 and s == 0 else None)

            for s in range(WIDE):
                in_chunk(0, s)
                if s == 0:
                    wait_misc_free(pe, "dtT")
                    pe.wait_ge(dt_lo, 1)
                    for k in range(KT):
                        for n, (a, w) in enumerate(((aT_hi, w_dt_hi), (aT_lo, w_dt_hi), (aT_hi, w_dt_lo))):
                            last = pe.matmul(misc_bank("dtT")[0:HEADS, 0:S], w[:, k, :], a[:, k, :],
                                             start=(k == 0 and n == 0), stop=(k == KT - 1 and n == 2))
                    last.then_inc(misc_filled, 1)
                if s == 1:
                    wait_misc_free(pe, "dt")
                    pe.wait_ge(misc_freed["dve"], frees("dve", "dtT"))
                    for t in range(T):
                        last = pe.transpose(misc_bank("dt")[:, t * HEADS:(t + 1) * HEADS], dtT[:, t * P:(t + 1) * P],
                                            ident[0:HEADS, 0:HEADS])
                    last.then_inc(misc_filled, 1)
            for s in range(WIDE):
                pe.wait_ge(pad_filled, s + 1)
                in_chunk(1, s)
            wait_misc_free(pe, "cumsum")
            pe.wait_ge(dtA_made, 1)
            bank = misc_bank("cumsum")
            for t in range(T):
                pe.matmul(bank[:, t * HEADS:(t + 1) * HEADS], tri, dtA[:, t, :], start=True, stop=True)
            pe.matmul(bank[:, 2 * HEADS:3 * HEADS], ones, dtA[:, 0, :], start=True, stop=True).then_inc(misc_filled, 1)
            norm_turn(1)
            pe.wait_ge(gates_landed, 64)
            pe.wait_ge(convolved, 4)
            for j in range(KT):
                wait_misc_free(pe, f"lru{j}")
                bank = misc_bank(f"lru{j}")
                for w in range(2):
                    last = pe.matmul(bank[:, w * S:(w + 1) * S], bd[:, w, j, :], xr[:, j, :], start=True, stop=True)
                last.then_inc(misc_filled, 1)
            for s in range(WIDE):
                pe.wait_ge(wide_freed, s + 1)
                in_chunk(2, s)
            for s in range(WIDE):
                pe.wait_ge(wide_freed, 4 + s + 1)
                in_chunk(3, s)
            for s in range(WIDE):
                pe.wait_ge(pad_filled, 4 + s + 1)
                in_chunk(4, s)

            pe.wait_ge(pad_filled, 8 + 1)
            pe.wait_ge(misc_freed["dve"], frees("dve", "norm1_3"))
            project_T(KV0, mem_T)

            pe.wait_ge(silu_made, 4)
            for t in range(T):
                for half in range(2):
                    name = f"xdt{2 * t + half}"
                    wait_misc_free(pe, name)
                    for j in range(4):
                        last = pe.transpose(misc_bank(name)[:, j * P:(j + 1) * P],
                                            xsT[:, 4 * half + j, t * P:(t + 1) * P], ident[:, :])
                    last.then_inc(misc_filled, 1)

            def decay_rows(q):
                name = f"rows{q}"
                wait_misc_free(pe, name)
                for hh in range(2):
                    for t in range(T):
                        at = hh * S + t * P
                        last = pe.matmul(misc_bank(name)[:, at:at + P],
                                         dtA[:, t, 2 * q + hh:2 * q + hh + 1].broadcast_to([P, P]), tri,
                                         start=True, stop=True)
                last.then_inc(misc_filled, 1)

            def ssd_heads(q):
                name = f"y{q}"
                wait_misc_free(pe, name)
                pe.wait_ge(mt_made, q + 1)
                bank = misc_bank(name)
                for t in range(T):
                    for hh in range(2):
                        at = (2 * q + hh) * HEAD_P
                        m = mt[:, q % 2, hh, 0:S] if t == 0 else mt[:, q % 2, hh, S:S + P]
                        last = pe.matmul(bank[HEAD_P * hh:HEAD_P * (hh + 1), t * P:S], xdt[:, t, at:at + HEAD_P], m,
                                         start=(t == 0), stop=(t == 1), skip_group_check=True)
                last.then_inc(misc_filled, 1)

            decay_rows(0)
            pe.wait_ge(silu_made, 8)
            for g in range(GROUPS):
                wait_misc_free(pe, f"cb{g}")
                bank = misc_bank(f"cb{g}")
                pe.matmul(bank[:, 0:S], bcT[:, g, 0:P], bcT[:, GROUPS + g, :], start=True, stop=True)
                pe.matmul(bank[:, S:S + P], bcT[:, g, P:S], bcT[:, GROUPS + g, P:S], start=True, stop=True)\
                    .then_inc(misc_filled, 1)
            for q in range(KV_CHUNKS):
                c = KV0 + q
                if 0 < q < 4:
                    pe.wait_ge(pad_filled, 8 + q + 1)
                    project_T(c, mem_T)
                elif q >= 4:
                    pe.wait_ge(wide_freed, 8 + q - 3)
                    project_v(c, mem_T)
                if q < 7:
                    decay_rows(q + 1)
                ssd_heads(q)
            for n in range(2):
                name = f"power{n}"
                wait_misc_free(pe, name)
                pe.wait_ge(ssd_squares, 4 * (n + 1))
                for g in range(2):
                    for j in range(2):
                        last = pe.matmul(misc_bank(name)[:, g * S:(g + 1) * S], ones, xsT[:, 4 * n + 2 * g + j, :],
                                         start=(j == 0), stop=(j == 1))
                last.then_inc(misc_filled, 1)
            pe.wait_ge(wide_freed, 16)
            pe.wait_ge(lru_split, 1)
            for n in range(4):
                project_rows(OUT0 + n, lru_T, n, True, False)
            pe.wait_ge(ssd_split, 2)
            for n in range(4):
                project_rows(OUT0 + 4 + n, ssd_T, n, False, True)
            norm_turn(2)

            def q_chunk(c):
                project_T(Q0 + c, x_T, ("norm2_1", "norm2_3") if c == 0 else None)

            def score(hd):
                name = f"score{hd}"
                wait_misc_free(pe, name)
                pe.wait_ge(wide_freed, 16 + hd + 1)
                for t in range(T):
                    for k in range(2):
                        last = pe.matmul(misc_bank(name)[:, t * S:(t + 1) * S], qT[:, 2 * hd + k, t * P:(t + 1) * P],
                                         kT[:, 2 * hd + k, :], start=(k == 0), stop=(k == 1))
                last.then_inc(misc_filled, 1)

            def prob_turn(hd):
                name = f"probT{hd}"
                wait_misc_free(pe, name)
                pe.wait_ge(prob_made, hd + 1)
                for m in range(T):
                    for t in range(T):
                        at = m * S + t * P
                        last = pe.transpose(misc_bank(name)[:, at:at + P], prob[:, hd, t, m * P:(m + 1) * P], ident[:, :])
                last.then_inc(misc_filled, 1)

            def attend(hd):
                name = f"o{hd}"
                wait_misc_free(pe, name)
                pe.wait_ge(misc_freed["act"], frees("act", f"probT{hd}"))
                for d in range(2):
                    for m in range(T):
                        at = (2 * hd + d) * P
                        last = pe.matmul(misc_bank(name)[:, d * S:(d + 1) * S], v[:, m, at:at + P], probT[:, hd, m, :],
                                         start=(m == 0), stop=(m == 1))
                last.then_inc(misc_filled, 1)

            pe.wait_ge(h_added, 2 * T)
            q_chunk(0)
            q_chunk(1)
            score(0)
            q_chunk(2)
            score(1)
            prob_turn(0)
            q_chunk(3)
            score(2)
            prob_turn(1)
            attend(0)
            score(3)
            prob_turn(2)
            attend(1)
            prob_turn(3)
            attend(2)
            attend(3)
            for n in range(4):
                project_rows(O0 + n, o_T, n, True, True, ("o1", "o3") if n == 0 else None)
            def start_sum(half):
                pe.wait_ge(h_added, 4 * T - 2 + 2 * half)
                for t in range(T):
                    pe.matmul(wide[:, 2 * t + half, :], ident[:, :], h[:, t, half * BANK:(half + 1) * BANK], start=True,
                              stop=False, skip_group_check=True)

            start_sum(0)
            start_sum(1)
            norm_turn(3)

            pe.wait_ge(misc_freed["dve"], frees("dve", "norm3_3"))
            pe.wait_ge(misc_freed["act"], frees("act", "norm3_3"))
            pe.wait_ge(router_landed, 32)
            wait_misc_free(pe, "logits")
            for t in range(T):
                for k in range(KT):
                    last = pe.matmul(misc_bank("logits")[:, t * EXPERTS:(t + 1) * EXPERTS], xT[:, k, t * P:(t + 1) * P],
                                     wr[:, k, :], start=(k == 0), stop=(k == KT - 1))
            last.then_inc(misc_filled, 1)
            wait_misc_free(pe, "rank")
            pe.wait_ge(sel_made, T)
            bank = misc_bank("rank")
            pe.matmul(bank[:, 0:EXPERTS], before[:, :], sel[:, 0, :], start=True, stop=True)
            pe.matmul(bank[:, EXPERTS:2 * EXPERTS], ones, sel[:, 0, :], start=True, stop=False)
            pe.matmul(bank[:, EXPERTS:2 * EXPERTS], before[:, :], sel[:, 1, :], start=False, stop=True)
            for t in range(T):
                last = pe.matmul(bank[0:EXPERTS, 2 * EXPERTS:2 * EXPERTS + 1], sel[:, t, :], ones[:, 0:1],
                                 start=(t == 0), stop=(t == 1))
            last.then_inc(misc_filled, 1)

            def gather(p):
                pe.wait_ge(pick_made, p + 1)
                for k in range(KT):
                    for t in range(T):
                        last = pe.matmul(pair_ps[1][:, k * P:(k + 1) * P], xn[:, t, k * P:(k + 1) * P],
                                         pick[:, t, :], start=(t == 0), stop=(t == T - 1))
                last.then_inc(picked, 1)

            def combine(t):
                for half in range(2):
                    last = pe.matmul(wide[:, 2 * t + half, :], put[:, t * P:(t + 1) * P],
                                     y_sb[:, half * BANK:(half + 1) * BANK],
                                     start=False, stop=False, skip_group_check=True)
                return last

            def up_bias(p, b):
                ps = pair_ps[b]
                pe.wait_ge(bias_landed[b], p * 32 + 32)
                for n in range(2):
                    for half in range(2):
                        at = half * D + n * BANK
                        pe.matmul(ps[SLOTS * half:SLOTS * (half + 1), n * BANK:(n + 1) * BANK],
                                  ones[32 * b:32 * b + 1, 0:SLOTS], bias_up[32 * b:32 * b + 1, at:at + BANK],
                                  start=True, stop=False, skip_group_check=True)

            def gate_up(p, b):
                ps = pair_ps[b]
                for k in range(UP_CHUNKS):
                    chunk = UP_CHUNKS * b + k
                    pair_landed(pe, p, chunk)
                    for n in range(2):
                        for half in range(2):
                            at = half * D + n * BANK
                            last = pe.matmul(ps[SLOTS * half:SLOTS * (half + 1), n * BANK:(n + 1) * BANK],
                                             xsel[:, k, SLOTS * b:SLOTS * (b + 1)], weights(p, chunk)[:, at:at + BANK],
                                             start=False, stop=(k == UP_CHUNKS - 1), skip_group_check=True)
                    last.then_inc(chunk_used, 1)
                    if b == 1 and k == 1 and not first(p):
                        pe.wait_ge(y_made["act"], p)
                        pe.wait_ge(y_made["dve"], p)
                        pe.wait_ge(put_made, p)
                        for t in range(T):
                            last = combine(t)
                        last.then_inc(combined, 1)

            def turn_act(p, b):
                pe.wait_ge(act_made, p * 2 + b + 1)
                for j in range(4):
                    last = pe.transpose(pair_ps[0][:, j * P:(j + 1) * P], act_sb[:, b, j * P:(j + 1) * P], ident[:, :])
                last.then_inc(act_turned, 1)

            def experts(p):
                if not first(p):
                    pe.wait_ge(y_made["act"], p)
                    pe.wait_ge(y_made["dve"], p)
                up_bias(p, 0)
                pe.wait_ge(xsel_made, p + 1)
                gate_up(p, 0)
                up_bias(p, 1)
                gate_up(p, 1)
                pe.wait_ge(gu_freed, p * 2 + 1)
                turn_act(p, 0)
                pe.wait_ge(pick_gate_made, p + 1)
                for t in range(T):
                    last = pe.transpose(pair_ps[0][:, BANK + t * P:BANK + (t + 1) * P], pick_gate[:, t, :], ident[:, :])
                last.then_inc(put_turned, 1)
                pe.wait_ge(gu_freed, p * 2 + 2)
                gather(p + 1)
                pe.wait_ge(actT_made, p * 2 + 1)
                turn_act(p, 1)
                pe.wait_ge(actT_made, p * 2 + 2)
                pe.wait_ge(put_made, p + 1)
                for n in range(2):
                    for b in range(2):
                        at = n * BANK
                        last = pe.matmul(pair_ps[0][SLOTS * b:SLOTS * (b + 1), n * BANK:(n + 1) * BANK],
                                         ones[32 * b:32 * b + 1, 0:SLOTS], bias_down[32 * b:32 * b + 1, at:at + BANK],
                                         start=True, stop=False, skip_group_check=True)
                last.then_inc(bias_used, 1)
                for c in range(DOWN_CHUNKS):
                    chunk = 2 * UP_CHUNKS + 2 * c
                    pair_landed(pe, p, chunk)
                    pair_landed(pe, p, chunk + 1)
                    for kk in range(2):
                        f = 2 * c + kk
                        for n in range(2):
                            for b in range(2):
                                at = kk * D + n * BANK
                                last = pe.matmul(pair_ps[0][SLOTS * b:SLOTS * (b + 1), n * BANK:(n + 1) * BANK],
                                                 actT[:, b, f % 4, SLOTS * (f // 4):SLOTS * (f // 4 + 1)],
                                                 weights(p, chunk + b)[:, at:at + BANK], start=False, stop=(f == 7),
                                                 skip_group_check=True)
                                if kk == 1 and n == 1:
                                    last.then_inc(chunk_used, 1)

            gather(0)
            experts(0)
            sums, turned = misc[:, 2, :], misc[:, 3, :]
            pe.wait_ge(spill_made, 1)
            pe.wait_ge(xsel_made, 2)
            pe.matmul(sums[0:EXPERTS, 0:1], before[0:EXPERTS, 0:EXPERTS], spill_cols[:, 4:5], start=True, stop=True)
            pe.matmul(sums[0:1, 1:2], spill_cols[:, 4:5], ones[0:EXPERTS, 0:1], start=True, stop=True)
            for t in range(T):
                pe.transpose(turned[0:EXPERTS, t * P:(t + 1) * P], rank_tab[:, t, 0:EXPERTS], ident[:, :])
                last = pe.transpose(turned[0:EXPERTS, S + t * P:S + (t + 1) * P], gate_tab[:, t, 0:EXPERTS], ident[:, :])
            last.then_inc(spill_filled, 1)
            pe.wait_ge(hot_made, 1)
            for w in range(2):
                for t in range(T):
                    at = (2 * w + t) * SPILLS
                    pe.matmul(sums[:, at:at + SPILLS], rgT[:, w, t * P:(t + 1) * P], one_hot[:, 1, :],
                              start=True, stop=True)
            pe.matmul(sums[0:1, 4 * SPILLS:5 * SPILLS], part_id[0:EXPERTS, :], one_hot[:, 1, :], start=True, stop=True)\
                .then_inc(spill_filled, 1)
            pe.wait_ge(tables_made, 1)
            experts(1)
            with pe.Fori(2, PAIRS) as p:
                experts(p)
            spills = pe.value_load(spill_int[0:1, SPILLS:SPILLS + 1], min_val=0, max_val=SPILLS // 2)
            with pe.If(spills > 0):
                with pe.Fori(0, spills) as j:
                    experts(j + PAIRS)
            pe.wait_ge(y_made["act"], spills + PAIRS)
            pe.wait_ge(y_made["dve"], spills + PAIRS)
            pe.wait_ge(put_made, spills + PAIRS)
            for t in range(T):
                combine(t).then_inc(combined, 1)

        @block.vector
        def _(dve):
            steps = [0]

            def step(ins):
                steps[0] += 1
                ins.then_inc(dve_step, 1)
                dve.wait_ge(dve_step, steps[0])

            def norm(n):
                src, sq, dst = norm_stage(n)
                if n < 2:
                    square_half(n, 0)
                square_half(n, 1)
                dve.wait_ge(squared["dve"], 2 * n + 2)
                dve.wait_ge(squared["act"], 2 * n + 2)
                step(dve.tensor_tensor(stats[:, n, 2, :], stats[:, n, 0, :], stats[:, n, 1, :], ALU.add))
                dve.tensor_scalar(stats[:, n, 3, :], stats[:, n, 2, :], 1.0 / D, EPS, ALU.mult, ALU.add)\
                    .then_inc(mean_made, 1)
                dve.wait_ge(root_made, n + 1)
                dve.reciprocal(stats[:, n, 5, :], stats[:, n, 4, :]).then_inc(rstd_made, 1)
                dve.wait_ge(rstd_made, n + 1)
                dve.tensor_scalar(dst[:, 1, :], src[:, 1, :], stats[:, n, 5, 1:2], None, ALU.mult)\
                    .then_inc(normed["dve"], 1)

            def square_half(n, half):
                src, sq, dst = norm_stage(n)
                at = slice(half * BANK, (half + 1) * BANK)
                dve.tensor_tensor_reduce(sq[:, 1, at], src[:, 1, at], src[:, 1, at], 1.0, 0.0, ALU.mult, ALU.add,
                                         stats[:, n, half, 1:2]).then_inc(squared["dve"], 1)

            def norm_turned(n):
                hi, lo = split_T(n)
                for b in range(4):
                    dve.wait_ge(norm_hi, 4 * n + b + 1)
                    bank = misc_bank(f"norm{n}_{b}")
                    for j in range(2):
                        k = 2 * b + j
                        last = dve.scalar_tensor_tensor(out=lo[:, k, :], in0=bank[:, j * S:(j + 1) * S],
                                                        scalar=par[:, NORM_GAIN[n] + k:NORM_GAIN[n] + k + 1],
                                                        in1=hi[:, k, :], op0=ALU.mult, op1=ALU.subtract)
                    last.then_inc(misc_freed["dve"], 1)

            def freed(ins):
                ins.then_inc(misc_freed["dve"], 1)

            dve.wait_ge(x_landed, 16)
            norm(0)
            wait_misc_filled(dve, "params")
            freed(dve.tensor_copy(par[:, :], misc_bank("params")[:, 0:PAR]))
            dve.wait_ge(misc_freed["dve"], 1)
            norm_turned(0)
            dve.wait_ge(dt_hi, 1)
            dve.tensor_tensor(w_dt_lo[:, :, :], w_dt[:, :, :], w_dt_hi[:, :, :], ALU.subtract).then_inc(dt_lo, 1)

            wait_misc_filled(dve, "dtT")
            freed(dve.tensor_copy(dtT[:, :], misc_bank("dtT")[0:HEADS, 0:S]))
            dve.wait_ge(heads_landed, 64)
            wait_misc_filled(dve, "dt")
            step(dve.tensor_scalar(sp[:, 0, 32:40], par[:, LAM:LAM + KT], -1.0, None, ALU.mult))
            for t in range(T):
                last = dve.tensor_tensor(sp[:, 0, t * HEADS:(t + 1) * HEADS], misc_bank("dt")[:, t * HEADS:(t + 1) * HEADS],
                                         heads_bc[:, 0, :], ALU.add)
            freed(last)
            dve.wait_ge(misc_freed["dve"], frees("dve", "dt"))
            dve.scalar_tensor_tensor(out=sp[:, 1, :], in0=sp[:, 0, :], scalar=-1.0, in1=sp[:, 0, :], op0=ALU.mult,
                                     op1=ALU.min).then_inc(sp_step, 1)
            dve.wait_ge(sp_act, 1)
            dve.tensor_scalar(sp[:, 3, :], sp[:, 2, :], 1.0, None, ALU.add).then_inc(sp_step, 1)
            dve.wait_ge(sp_step, 2)
            step(dve.tensor_scalar(sp[:, 5, :], sp[:, 3, :], -1.0, None, ALU.add))
            step(dve.tensor_scalar(sp[:, 6, :], sp[:, 5, :], 0.0, None, ALU.is_equal))
            step(dve.tensor_tensor(sp[:, 5, :], sp[:, 5, :], sp[:, 6, :], ALU.add))
            step(dve.reciprocal(sp[:, 7, :], sp[:, 5, :]))
            dve.wait_ge(sp_act, 3)
            step(dve.tensor_tensor(sp[:, 7, :], sp[:, 7, :], sp[:, 4, :], ALU.mult))
            step(dve.tensor_tensor(sp[:, 7, :], sp[:, 7, :], sp[:, 6, :], ALU.add))
            step(dve.tensor_tensor(sp[:, 7, :], sp[:, 7, :], sp[:, 2, :], ALU.mult))
            step(dve.scalar_tensor_tensor(out=sp[:, 5, :], in0=sp[:, 0, :], scalar=0.0, in1=sp[:, 7, :], op0=ALU.max,
                                          op1=ALU.add))
            dve.tensor_scalar(lru_rate[:, :], sp[:, 5, 32:40], -RG_C, None, ALU.mult).then_inc(rate_made, 1)
            for t in range(T):
                part = sp[:, 5, t * HEADS:(t + 1) * HEADS]
                dve.tensor_copy(dt[:, t, :], part)
                last = dve.scalar_tensor_tensor(out=dtA[:, t, :], in0=part, scalar=-1.0, in1=expA[:, :], op0=ALU.mult,
                                                op1=ALU.mult)
            last.then_inc(dtA_made, 1)
            pairs = heads_bc[:, 2, :].rearrange("p (j b) -> p b j", b=2)
            for b in range(2):
                step(dve.tensor_copy(d_col[64 * b:64 * b + 64, :], pairs[64 * b:64 * b + 64, b, :]))

            def convolve(n, buf, dst, j, taps, tap_step, bias):
                dve.wait_ge(pad_filled, n + 1)
                for tap in range(4):
                    if tap:
                        dve.wait_ge(tap_done, n * 3 + tap)
                    for b in range(2):
                        o = dst[:, j + b, :]
                        src = xpad[:, buf, b, tap:tap + S]
                        col = taps + tap * tap_step + j + b
                        if tap == 0:
                            last = dve.tensor_scalar(o, src, par[:, col:col + 1], par[:, bias + j + b:bias + j + b + 1],
                                                     ALU.mult, ALU.add)
                        else:
                            last = dve.scalar_tensor_tensor(out=o, in0=src, scalar=par[:, col:col + 1], in1=o,
                                                            op0=ALU.mult, op1=ALU.add)
                    last.then_inc(convolved if tap == 3 else tap_done, 1)

            for n in range(4):
                convolve(n, n % 2, xr, 2 * n, LCW, 8, LCB)
            dve.wait_ge(mem_landed, 16)
            norm(1)

            wait_misc_filled(dve, "cumsum")
            bank = misc_bank("cumsum")
            dve.tensor_copy(seg_bias[:, 1, :], bank[:, 2 * HEADS:3 * HEADS]).then_inc(dve_step, 1)
            steps[0] += 1
            dve.tensor_scalar(seg_bias[:, 0, :], bank[:, 0:HEADS], -1.0, None, ALU.mult)
            dve.tensor_scalar(seg_bias[:, 2, :], bank[:, HEADS:2 * HEADS], -1.0, None, ALU.mult).then_inc(misc_freed["dve"], 1)
            dve.wait_ge(misc_freed["dve"], frees("dve", "cumsum"))
            dve.tensor_tensor(seg_bias[:, 1, :], seg_bias[:, 1, :], seg_bias[:, 0, :], ALU.add).then_inc(seg_made, 1)
            dve.wait_ge(seg_made, 1)
            norm_turned(1)

            squares = xn[:, :, :].rearrange("p t (k s) -> p (t k) s", s=S)
            dve.wait_ge(misc_freed["act"], frees("act", "lru7"))
            dve.wait_ge(rate_made, 1)
            dve.tensor_tensor(rb, rb, lru_rate[:, :].unsqueeze(2).broadcast_to([P, KT, S]), ALU.mult)\
                .then_inc(rate_applied, 1)
            dve.wait_ge(decay_made, 1)
            dve.wait_ge(misc_filled, MISC_AT["norm0_3"] + 1)
            step(dve.tensor_tensor(squares, ab, ab, ALU.mult))
            dve.scalar_tensor_tensor(out=rb, in0=squares, scalar=1.0, in1=rb, op0=ALU.add, op1=ALU.mult)\
                .then_inc(lru_poly, 1)
            step(dve.tensor_tensor(ib, ib, xr, ALU.mult))
            dve.wait_ge(lru_root, 1)
            step(dve.tensor_tensor(ib, ib, rb, ALU.mult))
            for j in range(KT):
                last = dve.tensor_tensor_scan(rb[:, j, :], ab[:, j, :], ib[:, j, :], 0.0, ALU.mult, ALU.add)
            step(last)
            dve.tensor_tensor(gg, gg, rb, ALU.mult).then_inc(lru_out, 1)

            for n in range(8):
                convolve(4 + n, n % 2, xbc, 2 * n, SCW, 16, SCB)

            for t in range(T):
                for half in range(2):
                    name = f"xdt{2 * t + half}"
                    wait_misc_filled(dve, name)
                    freed(dve.tensor_tensor(
                        xdt[:, t, half * BANK:(half + 1) * BANK].rearrange("p (h c) -> p h c", c=HEAD_P),
                        misc_bank(name).rearrange("p (h c) -> p h c", c=HEAD_P),
                        dt[:, t, 8 * half:8 * half + 8].unsqueeze(2).broadcast_to([P, 8, HEAD_P]), ALU.mult))
            def exponents(q):
                name = f"rows{q}"
                wait_misc_filled(dve, name)
                if q >= 2:
                    wait_misc_filled(dve, f"y{q - 2}")
                bank = misc_bank(name)
                for hh in range(2):
                    for part in range(3):
                        at = hh * S + (P if part else 0)
                        hd = 2 * q + hh
                        last = dve.tensor_scalar(mt[:, q % 2, hh, part * P:(part + 1) * P], bank[:, at:at + P],
                                                 seg_bias[:, part, hd:hd + 1], 0.0, ALU.add, ALU.min)
                        if part == 2 and hh == 0:
                            last.then_inc(dve_step, 1)
                            steps[0] += 1
                last.then_inc(misc_freed["dve"], 1)

            def exponents_done(q):
                dve.wait_ge(misc_freed["dve"], frees("dve", f"rows{q}"))
                dve.tensor_copy(sp[:, 0, q:q + 1], seg_bias[:, 0, 0:1]).then_inc(seg_made, 1)

            exponents(0)
            exponents_done(0)
            for g in range(GROUPS):
                wait_misc_filled(dve, f"cb{g}")
                last = dve.tensor_tensor(cbm[:, g, :], misc_bank(f"cb{g}")[:, 0:3 * P], mask3[:, :], ALU.mult)
                freed(last)
            dve.wait_ge(misc_freed["dve"], frees("dve", "cb3"))

            for q in range(8):
                if q == 1:
                    dve.wait_ge(lru_hi, 1)
                    dve.tensor_tensor(aT_lo[:, :, :], gg, aT_hi[:, :, :], ALU.subtract).then_inc(lru_split, 1)
                dve.wait_ge(seg_exp, q + 1)
                m = mt[:, q % 2, :, :]
                dve.tensor_tensor(m, m, cbm[:, q // 2, :].unsqueeze(1).broadcast_to([P, 2, 3 * P]), ALU.mult)\
                    .then_inc(mt_made, 1)
                if q + 1 < 8:
                    exponents(q + 1)
                    exponents_done(q + 1)
                name = f"y{q}"
                wait_misc_filled(dve, name)
                xs = xsT[:, q, :]
                freed(dve.scalar_tensor_tensor(out=xs, in0=xs, scalar=d_col[:, q:q + 1], in1=misc_bank(name)[:, 0:S],
                                               op0=ALU.mult, op1=ALU.add))
                dve.wait_ge(misc_freed["dve"], frees("dve", name))
                step(dve.tensor_tensor(zs[:, q, :], zs[:, q, :], xs, ALU.mult))
                dve.tensor_tensor(xs, zs[:, q, :], zs[:, q, :], ALU.mult).then_inc(ssd_squares, 1)
            for n in range(2):
                name = f"power{n}"
                wait_misc_filled(dve, name)
                last = dve.tensor_scalar(group_scale[:, 2 * n:2 * n + 2, :],
                                         misc_bank(name).rearrange("p (g s) -> p g s", g=2), 1.0 / 256, EPS,
                                         ALU.mult, ALU.add)
                freed(last)
            dve.wait_ge(misc_freed["dve"], frees("dve", "power1"))
            dve.tensor_copy(sp[:, 0, 0:1], seg_bias[:, 0, 0:1]).then_inc(power_made, 1)
            dve.wait_ge(ssd_root, 1)
            step(dve.reciprocal(group_scale, group_scale))
            for half in range(2):
                for j in range(KH * half, KH * (half + 1)):
                    last = dve.scalar_tensor_tensor(out=zs[:, j, :], in0=zs[:, j, :],
                                                    scalar=par[:, SNORM + j:SNORM + j + 1],
                                                    in1=group_scale[:, j // 2, :], op0=ALU.mult, op1=ALU.mult)
                last.then_inc(ssd_out, 1)
            for half in range(2):
                at = slice(KH * half, KH * (half + 1))
                dve.wait_ge(ssd_hi, half + 1)
                dve.tensor_tensor(mT_lo[:, at, :], zs[:, at, :], mT_hi[:, at, :], ALU.subtract).then_inc(ssd_split, 1)

            def add_to_h(n, last_chunk):
                for half in range(2):
                    dve.wait_ge(chunk_used, last_chunk - 2 + 2 * half)
                    at = slice(half * BANK, (half + 1) * BANK)
                    for t in range(T):
                        dve.tensor_tensor(h[:, t, at], h[:, t, at], wide[:, 2 * t + half, :], ALU.add)\
                            .then_inc(h_added, 1)
                    dve.wait_ge(h_added, 4 * (n - 2) + 2 * half + 2)
                    if half == 0:
                        square_half(n, 0)

            add_to_h(2, Q0)
            norm(2)
            norm_turned(2)

            def attended(hd):
                dve.wait_ge(o_hi, hd + 1)
                at = slice(2 * hd, 2 * hd + 2)
                freed(dve.tensor_tensor(mT_lo[:, at, :], misc_bank(f"o{hd}").rearrange("p (j s) -> p j s", j=2),
                                        mT_hi[:, at, :], ALU.subtract))

            for hd in range(X_HEADS):
                if hd == 3:
                    attended(0)
                name = f"score{hd}"
                wait_misc_filled(dve, name)
                step(dve.tensor_reduce(soft[:, hd, 0, :], misc_bank(name).rearrange("p (t m) -> p t m", t=T), AX_X, ALU.max))
                dve.tensor_scalar(soft[:, hd, 1, :], soft[:, hd, 0, :], -X_SCALE, None, ALU.mult).then_inc(score_max, 1)
                dve.wait_ge(misc_freed["act"], frees("act", name))
                step(dve.reciprocal(soft[:, hd, 3, :], soft[:, hd, 2, :]))
                for t in range(T):
                    last = dve.tensor_scalar(prob[:, hd, t, :], prob[:, hd, t, :], soft[:, hd, 3, t:t + 1], None, ALU.mult)
                last.then_inc(prob_made, 1)

            for hd in range(1, X_HEADS):
                attended(hd)

            add_to_h(3, DENSE)
            norm(3)
            for b in (0, 2):
                wait_misc_filled(dve, f"norm3_{b}")
                bank = misc_bank(f"norm3_{b}")
                for j in range(2):
                    k = 2 * b + j
                    last = dve.tensor_scalar(xT[:, k, :], bank[:, j * S:(j + 1) * S], par[:, NMOE + k:NMOE + k + 1],
                                             None, ALU.mult)
                last.then_inc(misc_freed["dve"], 1)

            dve.wait_ge(router_landed, 32)
            wait_misc_filled(dve, "logits")
            for t in range(T):
                last = dve.tensor_tensor(lg[:, t, :], misc_bank("logits")[:, t * EXPERTS:(t + 1) * EXPERTS], br, ALU.add)
            freed(last)
            dve.wait_ge(misc_freed["dve"], frees("dve", "logits"))
            for t in range(T):
                step(dve.max(top8[:, t, :], lg[:, t, :]))
            for t in range(T):
                dve.tensor_scalar(top_neg[:, t:t + 1], top8[:, t, 0:1], -1.0, None, ALU.mult).then_inc(logits_made, 1)
            step(dve.memset(top8[:, :, TOP_K:8], 3.0e38))
            for t in range(T):
                last = dve.match_replace(sel[:, t, :], top8[:, t, :], lg[:, t, :], -3.0e38)
            step(last)
            for t in range(T):
                dve.tensor_tensor(sel[:, t, :], sel[:, t, :], lg[:, t, :], ALU.not_equal).then_inc(sel_made, 1)
            dve.wait_ge(sel_made, T)
            for t in range(T):
                dve.wait_ge(gate_exp, t + 1)
                step(dve.tensor_tensor_reduce(rest[:, t, :], rest[:, t, :], sel[:, t, :], 1.0, 0.0, ALU.mult, ALU.add,
                                              gsum[:, 0, t:t + 1]))
            step(dve.reciprocal(gsum[:, 1, :], gsum[:, 0, :]))
            wait_misc_filled(dve, "rank")
            bank = misc_bank("rank")
            for t in range(T):
                step(dve.scalar_tensor_tensor(out=rank_tab[:, t, 0:EXPERTS], in0=sel[:, t, :], scalar=-4096.0,
                                              in1=bank[:, t * EXPERTS:(t + 1) * EXPERTS], op0=ALU.mult, op1=ALU.add))
            step(dve.tensor_scalar(rank_tab[:, :, 0:EXPERTS], rank_tab[:, :, 0:EXPERTS], 4096.0, None, ALU.add))
            freed(dve.tensor_copy(spill_cols[:, 0:1], bank[0:EXPERTS, 2 * EXPERTS:2 * EXPERTS + 1]))
            dve.wait_ge(misc_freed["dve"], frees("dve", "rank"))
            for t in range(T):
                last = dve.tensor_scalar(gate_tab[:, t, 0:EXPERTS], rest[:, t, :], gsum[:, 1, t:t + 1], None, ALU.mult)
            step(last)

            def make_pick(p):
                for t in range(T):
                    for b in range(2):
                        at = slice(SLOTS * b, SLOTS * (b + 1))
                        last = dve.tensor_scalar(pick[:, t, at], slot_id[:, at], rank_tab[:, t, bass.ds(p * 2 + b, 1)],
                                                 None, ALU.is_equal)
                last.then_inc(pick_made, 1)

            def make_pick_gate(p):
                for t in range(T):
                    for b in range(2):
                        at = slice(SLOTS * b, SLOTS * (b + 1))
                        last = dve.tensor_scalar(pick_gate[:, t, at], slot_id[:, at],
                                                 rank_tab[:, t, bass.ds(p * 2 + b, 1)],
                                                 gate_tab[:, t, bass.ds(p * 2 + b, 1)], ALU.is_equal, ALU.mult)
                last.then_inc(pick_gate_made, 1)

            def take_xsel(p):
                dve.wait_ge(picked, p + 1)
                dve.tensor_tensor(xsel, pair_ps[1].rearrange("p (k c) -> p k c", k=KT),
                                  par[:, NMOE:NMOE + KT].unsqueeze(2).broadcast_to([P, KT, P]), ALU.mult)\
                    .then_inc(xsel_made, 1)

            def swiglu(p, b):
                used(dve, p, UP_CHUNKS * (b + 1) - 1)
                if b == 1:
                    dve.wait_ge(act_made, p * 2 + 1)
                halves = pair_ps[b].rearrange("p (f w) -> p w f", w=2)
                dve.tensor_scalar(g_sb, halves[:, 0, :], LIMIT, None, ALU.min).then_inc(g_made, 1)
                dve.tensor_scalar(u_sb, halves[:, 1, :], LIMIT, -LIMIT, ALU.min, ALU.max).then_inc(gu_freed, 1)
                dve.wait_ge(sig_made, p * 2 + b + 1)
                dve.tensor_tensor(g_sb, g_sb, sig, ALU.mult).then_inc(gated, 1)
                dve.wait_ge(gated, p * 2 + b + 1)
                dve.scalar_tensor_tensor(out=act_sb[:, b, :], in0=u_sb, scalar=1.0, in1=g_sb, op0=ALU.add, op1=ALU.mult)\
                    .then_inc(act_made, 1)

            def experts(p):
                make_pick(p + 1)
                swiglu(p, 0)
                swiglu(p, 1)
                take_xsel(p + 1)
                dve.wait_ge(put_turned, p + 1)
                make_pick_gate(p + 1)
                used(dve, p, PAIR_CHUNKS - 1)
                dve.tensor_copy(y_sb[:, BANK:2 * BANK], pair_ps[0][:, BANK:2 * BANK]).then_inc(y_made["dve"], 1)

            make_pick(0)
            make_pick_gate(0)
            take_xsel(0)
            for n in range(3):
                step(dve.tensor_scalar(spill_cols[:, 1 + n:2 + n], spill_cols[:, 0:1], float(SLOTS * (n + 1)), None,
                                       ALU.is_gt))
            dve.tensor_reduce(spill_cols[:, 4:5], spill_cols[:, 1:4], AX_X, ALU.add).then_inc(spill_made, 1)
            experts(0)

            sums, turned = misc[:, 2, :], misc[:, 3, :]
            dve.wait_ge(spill_made, 1)
            dve.wait_ge(spill_filled, 1)
            step(dve.tensor_copy(spill_cols[:, 5:6], sums[0:EXPERTS, 0:1]))
            dve.tensor_scalar(spill_int[:, SPILLS:SPILLS + 1], sums[0:1, 1:2], 0.5, 0.25, ALU.mult, ALU.add)
            step(dve.tensor_tensor(spill_cols[:, 6:7], spill_cols[:, 5:6], spill_cols[:, 4:5], ALU.add))
            step(dve.tensor_scalar(spill_cols[:, 7:8], spill_cols[:, 5:6], float(SLOTS), None, ALU.mult))
            step(dve.tensor_scalar(one_hot[:, 0, :], spill_id[0:EXPERTS, :], spill_cols[:, 5:6], None, ALU.is_ge))
            dve.scalar_tensor_tensor(out=one_hot[:, 1, :], in0=spill_id[0:EXPERTS, :], scalar=spill_cols[:, 6:7],
                                     in1=one_hot[:, 0, :], op0=ALU.is_lt, op1=ALU.mult)
            dve.tensor_scalar(rgT[:, 0, :], turned[0:EXPERTS, 0:S], spill_cols[:, 7:8], None, ALU.add)
            dve.tensor_copy(rgT[:, 1, :], turned[0:EXPERTS, S:2 * S]).then_inc(hot_made, 1)
            n0, n1 = EXPERTS, EXPERTS + SPILLS
            dve.memset(rank_tab[:, :, n1:n1 + 2], -1.0)
            dve.memset(gate_tab[:, :, n1:n1 + 2], 0.0)
            dve.wait_ge(spill_filled, 2)
            for t in range(T):
                dve.tensor_tensor(rank_tab[:, t, n0:n1], sums[:, t * SPILLS:(t + 1) * SPILLS], spill_base[:, :],
                                  ALU.subtract)
                dve.tensor_copy(gate_tab[:, t, n0:n1], sums[:, (2 + t) * SPILLS:(3 + t) * SPILLS])
            dve.tensor_copy(spill_int[:, 0:SPILLS], sums[0:1, 4 * SPILLS:5 * SPILLS]).then_inc(tables_made, 1)
            dve.wait_ge(tables_made, 1)

            with dve.Fori(1, PAIRS) as p:
                experts(p)
            spills = dve.value_load(spill_int[0:1, SPILLS:SPILLS + 1], min_val=0, max_val=SPILLS // 2)
            with dve.If(spills > 0):
                with dve.Fori(0, spills) as j:
                    experts(j + PAIRS)
            dve.wait_ge(gain_landed, 16)
            for t in range(T):
                dve.wait_ge(squared["act"], 8 + t + 1)
                dve.tensor_scalar(stats[:, 4, 3, t:t + 1], stats[:, 4, 0, t:t + 1], 1.0 / D, EPS, ALU.mult, ALU.add)\
                    .then_inc(mean_made, 1)
                dve.wait_ge(root_made, 4 + t + 1)
                dve.reciprocal(stats[:, 4, 5, t:t + 1], stats[:, 4, 4, t:t + 1]).then_inc(rstd_made, 1)
                dve.wait_ge(rstd_made, 4 + t + 1)
                for half in range(2):
                    at = slice(half * BANK, (half + 1) * BANK)
                    dve.scalar_tensor_tensor(out=xn[:, t, at], in0=wide[:, 2 * t + half, :],
                                             scalar=stats[:, 4, 5, t:t + 1], in1=gain_row[:, at], op0=ALU.mult,
                                             op1=ALU.mult).then_inc(out_made, 1)


_INS = ['x', 'mem', 'norm_mix', 'w_in', 'ssd_conv_w', 'ssd_conv_b', 'ssd_dt_bias', 'ssd_a_log', 'ssd_d', 'ssd_norm',
        'lru_conv_w', 'lru_conv_b', 'lru_wa', 'lru_ba', 'lru_wx', 'lru_bx', 'lru_lambda', 'w_out',
        'norm_xattn', 'norm_mem', 'w_q', 'w_kv', 'w_o', 'norm_moe', 'w_router', 'b_router',
        'w_gate_up', 'b_gate_up', 'w_down', 'b_down', 'norm_final']
_OUTS = [((1, 256, 1024), 'float32')]


def kernel(**inputs):
    import numpy as _np
    import concourse.bacc as _bacc
    from concourse import mybir as _mybir
    from concourse.bass_utils import run_bass_kernel_spmd as _run

    nc = _bacc.Bacc("TRN2", target_bir_lowering=False, num_devices=1)
    arrays, args = {}, []
    for name in _INS:
        a = _np.ascontiguousarray(inputs[name])
        arrays[f"in_{name}_dram"] = a
        args.append(nc.dram_tensor(f"in_{name}_dram", a.shape, _mybir.dt.from_np(a.dtype), kind="ExternalInput").ap())
    for i, (shape, dtype) in enumerate(_OUTS):
        dt = _mybir.dt.from_np(_np.dtype(dtype))
        args.append(nc.dram_tensor(f"out_{i}_dram", shape, dt, kind="ExternalOutput").ap())
    hybrid_trunk_kernel(nc, *args)
    r = _run(nc, [arrays], core_ids=[0])
    got = tuple(r.results[0][f"out_{i}_dram"] for i in range(len(_OUTS)))
    return got[0]
```
